# Optimizing a Trainium2 kernel written in Bass

```python
import math
import jax, jax.numpy as jnp
from jax import lax
import numpy as np

D_MODEL = 1024
BATCH = 1
SEQ = 256
DEPTH = 2

PLE_DIM = 256
D_FF = 2816
SB_HEADS = 8
SB_HEAD_DIM = 64
DF_HEADS = 4
DF_QK_DIM = 64
DF_V_DIM = 2 * DF_QK_DIM
SB_W = SB_HEADS * SB_HEAD_DIM
DF_QK_W = DF_HEADS * 2 * DF_QK_DIM
DF_W = DF_HEADS * DF_V_DIM
IN_SPLITS = (SB_W, SB_W, SB_W, DF_QK_W, DF_QK_W, DF_W, D_MODEL, D_MODEL)
D_IN = SB_W * 3 + DF_QK_W * 2 + DF_W + 2 * D_MODEL
BLOCK_Q = 128
ROPE_THETA = 10000.0
NORM_EPS = 1e-6
SUBLN_EPS = 1e-5

kernel_name = "hybrid_stickbreak_diffattn_macaron_trunk"

def rms_norm(x, g, eps=NORM_EPS):
    xf = x.astype(jnp.float32)
    y = xf * lax.rsqrt(jnp.mean(xf * xf, axis=-1, keepdims=True) + eps)
    return (y * g.astype(jnp.float32)).astype(x.dtype)

def swiglu(x, w_gu, w_down):
    g, u = jnp.split(x @ w_gu, 2, axis=-1)
    return (jax.nn.silu(g) * u) @ w_down

def rope(x, positions):
    half = x.shape[-1] // 2
    inv_freq = ROPE_THETA ** (-jnp.arange(half, dtype=jnp.float32) / half)
    ang = positions.astype(jnp.float32)[..., None] * inv_freq
    cos = jnp.cos(ang)[:, :, None, None, :]
    sin = jnp.sin(ang)[:, :, None, None, :]
    x1 = x[..., :half].astype(jnp.float32)
    x2 = x[..., half:].astype(jnp.float32)
    return jnp.concatenate([x1 * cos - x2 * sin, x2 * cos + x1 * sin], axis=-1).astype(x.dtype)

def to_query_blocks(q):
    b, h, s = q.shape[:3]
    qb = q.reshape((b, h, s // BLOCK_Q, BLOCK_Q) + q.shape[3:])
    return jnp.moveaxis(qb, 2, 0)

def from_query_blocks(o):
    nb, b, h, bq, d = o.shape
    return jnp.moveaxis(o, 0, 2).reshape(b, h, nb * bq, d)

def stick_breaking_attention(q, k, v):
    s_len, d = q.shape[2], q.shape[3]
    scale = 1.0 / math.sqrt(d)
    key_pos = jnp.arange(s_len)

    def one_block(args):
        qi, bi = args
        q_pos = bi * BLOCK_Q + jnp.arange(BLOCK_Q)
        strict = key_pos[None, :] < q_pos[:, None]
        z = jnp.einsum('bhqd,bhkd->bhqk', qi, k).astype(jnp.float32) * scale
        log_one_minus = jnp.where(strict, jax.nn.log_sigmoid(-z), 0.0)
        later = lax.cumsum(log_one_minus, axis=3, reverse=True) - log_one_minus
        w = jnp.where(strict, jnp.exp(jax.nn.log_sigmoid(z) + later), 0.0)
        return jnp.einsum('bhqk,bhkd->bhqd', w.astype(v.dtype), v)

    nb = s_len // BLOCK_Q
    out = lax.map(one_block, (to_query_blocks(q), jnp.arange(nb)))
    return from_query_blocks(out)

def differential_attention(q, k, v, lam):
    s_len, d = q.shape[2], q.shape[4]
    scale = 1.0 / math.sqrt(d)
    key_pos = jnp.arange(s_len)

    def one_block(args):
        qi, bi = args
        q_pos = bi * BLOCK_Q + jnp.arange(BLOCK_Q)
        causal = key_pos[None, :] <= q_pos[:, None]
        z = jnp.einsum('bhqcd,bhkcd->bhcqk', qi, k).astype(jnp.float32) * scale
        z = jnp.where(causal, z, -jnp.inf)
        probs = jax.nn.softmax(z, axis=-1)
        a = probs[:, :, 0] - lam * probs[:, :, 1]
        return jnp.einsum('bhqk,bhkd->bhqd', a.astype(v.dtype), v)

    nb = s_len // BLOCK_Q
    out = lax.map(one_block, (to_query_blocks(q), jnp.arange(nb)))
    return from_query_blocks(out)

def setup_inputs(seed: int = 0) -> dict:
    key = jax.random.key(seed)
    ks = jax.random.split(key, 24)
    f32 = jnp.float32

    def w(k, shape, fan_in):
        return jax.random.normal(k, shape, f32) * (fan_in ** -0.5)

    def gain(k, n):
        return 1.0 + 0.05 * jax.random.normal(k, (DEPTH, n), f32)

    offsets = jax.random.randint(ks[2], (BATCH, 1), 0, SEQ, dtype=jnp.int32)
    positions = (jnp.arange(SEQ, dtype=jnp.int32)[None, :] + offsets).astype(jnp.int32)
    return {
        "x": jax.random.normal(ks[0], (BATCH, SEQ, D_MODEL), f32),
        "p": jax.random.normal(ks[1], (DEPTH, BATCH, SEQ, PLE_DIM), f32),
        "positions": positions,
        "ffn1_pre_g": gain(ks[3], D_MODEL),
        "ffn1_w_gu": w(ks[4], (DEPTH, D_MODEL, 2 * D_FF), D_MODEL),
        "ffn1_w_down": w(ks[5], (DEPTH, D_FF, D_MODEL), D_FF),
        "ffn1_post_g": gain(ks[6], D_MODEL),
        "mix_pre_g": gain(ks[7], D_MODEL),
        "w_in": w(ks[8], (DEPTH, D_MODEL, D_IN), D_MODEL),
        "diff_lambda": 0.1 * jax.random.normal(ks[9], (DEPTH, 4, DF_QK_DIM), f32),
        "diff_subln_g": gain(ks[10], DF_V_DIM),
        "w_branch_sb": w(ks[11], (DEPTH, SB_W, D_MODEL), SB_W),
        "w_branch_diff": w(ks[12], (DEPTH, DF_W, D_MODEL), DF_W),
        "w_out": w(ks[13], (DEPTH, D_MODEL, D_MODEL), D_MODEL),
        "mix_post_g": gain(ks[14], D_MODEL),
        "ffn2_pre_g": gain(ks[15], D_MODEL),
        "ffn2_w_gu": w(ks[16], (DEPTH, D_MODEL, 2 * D_FF), D_MODEL),
        "ffn2_w_down": w(ks[17], (DEPTH, D_FF, D_MODEL), D_FF),
        "ffn2_post_g": gain(ks[18], D_MODEL),
        "ple_pre_g": gain(ks[19], D_MODEL),
        "w_ple_gate": w(ks[20], (DEPTH, D_MODEL, D_MODEL), D_MODEL),
        "w_ple_proj": w(ks[21], (DEPTH, PLE_DIM, D_MODEL), PLE_DIM),
        "ple_post_g": gain(ks[22], D_MODEL),
    }

def reference(x, p, positions,
              ffn1_pre_g, ffn1_w_gu, ffn1_w_down, ffn1_post_g,
              mix_pre_g, w_in, diff_lambda, diff_subln_g, w_branch_sb, w_branch_diff, w_out, mix_post_g,
              ffn2_pre_g, ffn2_w_gu, ffn2_w_down, ffn2_post_g,
              ple_pre_g, w_ple_gate, w_ple_proj, ple_post_g):
    b, s, _ = x.shape
    split_at = [int(o) for o in np.cumsum(IN_SPLITS)[:-1]]
    h = x
    for i in range(DEPTH):
        f = swiglu(rms_norm(h, ffn1_pre_g[i]), ffn1_w_gu[i], ffn1_w_down[i])
        h = h + 0.5 * rms_norm(f, ffn1_post_g[i])

        u = rms_norm(h, mix_pre_g[i])
        sb_q, sb_k, sb_v, df_q, df_k, df_v, g_sb, g_df = jnp.split(u @ w_in[i], split_at, axis=-1)

        heads_sb = lambda t: t.reshape(b, s, SB_HEADS, SB_HEAD_DIM).transpose(0, 2, 1, 3)
        o_sb = stick_breaking_attention(heads_sb(sb_q), heads_sb(sb_k), heads_sb(sb_v))
        y_sb = o_sb.transpose(0, 2, 1, 3).reshape(b, s, SB_W) @ w_branch_sb[i]

        lam_init = 0.8 - 0.6 * math.exp(-0.3 * i)
        lp = diff_lambda[i].astype(jnp.float32)
        lam = jnp.exp(jnp.sum(lp[0] * lp[1])) - jnp.exp(jnp.sum(lp[2] * lp[3])) + lam_init
        dq = rope(df_q.reshape(b, s, DF_HEADS, 2, DF_QK_DIM), positions).transpose(0, 2, 1, 3, 4)
        dk = rope(df_k.reshape(b, s, DF_HEADS, 2, DF_QK_DIM), positions).transpose(0, 2, 1, 3, 4)
        dv = df_v.reshape(b, s, DF_HEADS, DF_V_DIM).transpose(0, 2, 1, 3)
        o_df = differential_attention(dq, dk, dv, lam)
        o_df = rms_norm(o_df, diff_subln_g[i], SUBLN_EPS) * (1.0 - lam_init)
        y_df = o_df.transpose(0, 2, 1, 3).reshape(b, s, DF_W) @ w_branch_diff[i]

        merged = jax.nn.sigmoid(g_sb) * y_sb + jax.nn.sigmoid(g_df) * y_df
        h = h + rms_norm(merged @ w_out[i], mix_post_g[i])

        f = swiglu(rms_norm(h, ffn2_pre_g[i]), ffn2_w_gu[i], ffn2_w_down[i])
        h = h + 0.5 * rms_norm(f, ffn2_post_g[i])

        gate = jax.nn.sigmoid(rms_norm(h, ple_pre_g[i]) @ w_ple_gate[i])
        e = (p[i] @ w_ple_proj[i]) * gate
        h = h + rms_norm(e, ple_post_g[i])
    return h


_drawn_inputs = setup_inputs


def setup_inputs(seed=0):
    import zlib

    import numpy as np

    out = dict(_drawn_inputs(seed))
    spreads = {}
    factors = {'ffn2_post_g': 3.184, 'ple_pre_g': 4.167}
    for name, (base, spread) in spreads.items():
        noise = np.random.default_rng([zlib.crc32(name.encode()), seed]).standard_normal(out[name].shape)
        drawn = base * np.exp(spread * noise) if base else spread * noise
        out[name] = __import__('jax').numpy.asarray(drawn.astype(out[name].dtype))
    for name, factor in factors.items():
        out[name] = (out[name] * factor).astype(out[name].dtype)
    return out
```

```python
import math
from contextlib import ExitStack

import numpy as np

import concourse.bass as bass
from concourse import mybir

ALU = mybir.AluOpType
ACT = mybir.ActivationFunctionType
AX_X = mybir.AxisListType.X
F32 = mybir.dt.float32
F32R = mybir.dt.float32r
BF16 = mybir.dt.bfloat16
I32 = mybir.dt.int32

P = 128

DEPTH, SEQ, D = 2, 256, 1024
PLE, FF = 256, 2816
SB_HEADS, SB_D = 8, 64
DF_HEADS, DF_D = 4, 64
DF_V = 2 * DF_D
THETA, EPS, SUB_EPS = 10000.0, 1e-6, 1e-5
NEG = -1.0e30

TT = SEQ // P
KD = D // P
FC = 256
NC = FF // FC
W = 512
SLOTS = 3
UNIT = 2048

U_FFN = 3 * NC
U_FFN1 = 0
U_WIN = U_FFN1 + U_FFN
U_BSB = U_WIN + 20
U_BDF = U_BSB + 2
U_WOUT = U_BDF + 2
U_FFN2 = U_WOUT + 4
U_PROJ = U_FFN2 + U_FFN
U_GATE = U_PROJ + 1
UNITS = U_GATE + 4
assert UNITS % SLOTS == 0

SBQ, SBK, SBV, DFQ, DFK, DFV = range(6)
SB_Z0, SB_C0, SB_P0 = 6, 7, 8
DF_Z0, DF_T0, DF_P0 = 12, 13, 14
BY_ACT = (0, 1, 3, 4, 6, 7, 8, 9)
QK_ORDER = {SBQ: 0, SBK: 1, DFQ: 2, DFK: 3}

MEANS = 16
LAM_INIT = [0.8 - 0.6 * math.exp(-0.3 * n) for n in range(DEPTH)]
ROUND = 1.5 * 2.0 ** 23
TWO_PI = [6.28125, round((2 * math.pi - 6.28125) * 2 ** 21) / 2 ** 21]
TWO_PI.append(2 * math.pi - sum(TWO_PI))
PI_IN = 3.1415925


def trunk_kernel(nc, a, out):
    with ExitStack() as ctx:
        def sb(name, shape, dt=F32):
            return ctx.enter_context(nc.sbuf_tensor(name, shape, dt))

        def sem(name):
            return ctx.enter_context(nc.semaphore(name))

        ps = ctx.enter_context(nc.psum_tensor("ps", [P, 8, W], F32))

        def bank(b):
            return ps[:, b, :]

        def pair(b):
            return ps[:, b:b + 2, :].rearrange("p b n -> p (b n)")

        raw = sb("raw", [P, SLOTS, UNIT])
        w_hi = sb("w_hi", [P, SLOTS, UNIT], F32R)
        w_lo = sb("w_lo", [P, SLOTS, UNIT], F32R)
        h = sb("h", [P, TT, D])
        x_hi = sb("x_hi", [P, KD, SEQ], F32R)
        x_lo = sb("x_lo", [P, KD, SEQ], F32R)
        glu = sb("glu", [P, TT, 2, FC])
        ht_hi = sb("ht_hi", [P, 2, SEQ], F32R)
        ht_lo = sb("ht_lo", [P, 2, SEQ], F32R)
        p_hi = sb("p_hi", [P, 2, SEQ], F32R)
        p_lo = sb("p_lo", [P, 2, SEQ], F32R)
        p_nat = sb("p_nat", [P, TT, PLE])
        tmp = sb("tmp", [P, TT, D])
        squares = sb("squares", [P, D])
        post_g = sb("post_g", [P, 2, D])
        g_rows = sb("g_rows", [P, P])
        g_cols = sb("g_cols", [P, 66])
        g_layer = sb("g_layer", [P, 33])
        lam_in = sb("lam_in", [P, DEPTH, 4, DF_D])
        lam_pr = sb("lam_pr", [P, DEPTH, 2, DF_D])
        lam_s = sb("lam_s", [P, DEPTH, 2])
        lam_e = sb("lam_e", [P, DEPTH, 2])
        neg_lams = sb("neg_lams", [P, DEPTH])
        neg_lam = sb("neg_lam", [P, 1])
        mean_pre = sb("mean_pre", [P, TT])
        ms_pre = sb("ms_pre", [P, TT])
        r_pre = sb("r_pre", [P, TT])
        r_query = sb("r_query", [P, TT])
        mean_post = sb("mean_post", [P, TT])
        ms_post = sb("ms_post", [P, TT])
        r_post = sb("r_post", [P, TT])
        neg_half = sb("neg_half", [P, TT])
        eps_norm = sb("eps_norm", [P, TT])
        eps_sub = sb("eps_sub", [P, TT])
        q_factor = sb("q_factor", [P, TT])
        sbq_t = sb("sbq_t", [P, 4, SEQ])
        sbk_t = sb("sbk_t", [P, 4, SEQ])
        dfq_t = sb("dfq_t", [P, 4, SEQ])
        dfk_t = sb("dfk_t", [P, 4, SEQ])
        v_sb = sb("v_sb", [P, TT, W])
        v_df = sb("v_df", [P, TT, W])
        gates = sb("gates", [P, 2, TT, D])
        soft = sb("soft", [P, 2, 384])
        sp = sb("sp", [P, 2, 384])
        w_att = sb("w_att", [P, 2, 384])
        o_sb = sb("o_sb", [P, TT, W])
        os_hi = sb("os_hi", [P, 4, SEQ], F32R)
        os_lo = sb("os_lo", [P, 4, SEQ], F32R)
        prob = sb("prob", [P, 2, 384])
        neg_max = sb("neg_max", [P, 4])
        p_sum = sb("p_sum", [P, 4])
        p_rec = sb("p_rec", [P, 4])
        neg_lr = sb("neg_lr", [P, 2])
        mixed = sb("mixed", [P, 384])
        mixed_t = sb("mixed_t", [P, 384])
        mean_sub = sb("mean_sub", [P, TT])
        ms_sub = sb("ms_sub", [P, TT])
        r_sub = sb("r_sub", [P, TT])
        ident = sb("ident", [P, P])
        ident_b = sb("ident_b", [P, P], BF16)
        neg_tri = sb("neg_tri", [P, P])
        neg_one = sb("neg_one", [P, P])
        mask_sb = sb("mask_sb", [P, 384], BF16)
        mask_df = sb("mask_df", [P, 384], BF16)
        pos_i = sb("pos_i", [P, TT], I32)
        pos_f = sb("pos_f", [P, TT])
        freq = sb("freq", [P, 32])
        ang = sb("ang", [P, TT, 32])
        turns = sb("turns", [P, TT, 32])
        cos_in = sb("cos_in", [P, TT, 32])
        rope_c = sb("rope_c", [P, TT, 64])
        rope_s = sb("rope_s", [P, TT, 64])

        o_df = glu[:, :, :, :].rearrange("p t a n -> p t (a n)")
        rope_b = o_df
        slab = tmp[:, :, 0:W]
        slab_c = tmp[:, :, W:D]

        raw_in = [sem(f"raw_in{s}") for s in range(SLOTS)]
        hi_ready = sem("hi_ready")
        split_done = sem("split_done")
        units_used = sem("units_used")
        gu_done = sem("gu_done")
        silu_done = sem("silu_done")
        prod_done = sem("prod_done")
        ht_turned = sem("ht_turned")
        ht_high = sem("ht_high")
        ht_split = sem("ht_split")
        p_turned = sem("p_turned")
        p_high = sem("p_high")
        p_split = sem("p_split")
        x_turned = sem("x_turned")
        x_high = sem("x_high")
        x_split = sem("x_split")
        h_loaded = sem("h_loaded")
        h_ready = sem("h_ready")
        squared_pre = sem("squared_pre")
        mean_done = sem("mean_done")
        pre_scale = sem("pre_scale")
        query_scale = sem("query_scale")
        squared_post = sem("squared_post")
        post_scale = sem("post_scale")
        f_done = sem("f_done")
        scaled = sem("scaled")
        win_done = sem("win_done")
        kept_act = sem("kept_act")
        kept_dve = sem("kept_dve")
        rope_parts = sem("rope_parts")
        roped = sem("roped")
        qk_turned = sem("qk_turned")
        sb_turned = sem("sb_turned")
        df_turned = sem("df_turned")
        s_score = sem("s_score")
        s_abs = sem("s_abs")
        s_exp = sem("s_exp")
        s_log = sem("s_log")
        s_soft = sem("s_soft")
        s_later = sem("s_later")
        s_weight = sem("s_weight")
        s_value = sem("s_value")
        s_kept = sem("s_kept")
        os_turned = sem("os_turned")
        os_high = sem("os_high")
        os_split = sem("os_split")
        d_score = sem("d_score")
        d_max = sem("d_max")
        d_exp = sem("d_exp")
        d_rec = sem("d_rec")
        d_part = sem("d_part")
        d_mixed = sem("d_mixed")
        d_turned = sem("d_turned")
        d_kept = sem("d_kept")
        d_value = sem("d_value")
        d_square = sem("d_square")
        d_scale = sem("d_scale")
        d_normed = sem("d_normed")
        od_turned = sem("od_turned")
        od_high = sem("od_high")
        od_split = sem("od_split")
        y_sb_done = sem("y_sb_done")
        y_df_done = sem("y_df_done")
        gate_sig = sem("gate_sig")
        gated_sb = sem("gated_sb")
        gated_df = sem("gated_df")
        merged = sem("merged")
        e_done = sem("e_done")
        ple_sig = sem("ple_sig")
        ple_e = sem("ple_e")
        layer_g = sem("layer_g")
        post_in = [sem(f"post_in{s}") for s in range(2)]
        p_in = sem("p_in")
        g_in = sem("g_in")
        lam_loaded = sem("lam_loaded")
        pos_in = sem("pos_in")
        const_id = sem("const_id")
        const_all = sem("const_all")
        cols_turned = sem("cols_turned")
        cols_kept = sem("cols_kept")
        d_lam = sem("d_lam")
        setup_step = sem("setup_step")
        angles = sem("angles")
        sines = sem("sines")
        lam_sum = sem("lam_sum")
        lam_exp = sem("lam_exp")
        blank = sem("blank")
        out_done = sem("out_done")

        X_BANK = ((0, 1, 2, 3), (6, 7, 0, 1), (4, 5, 2, 3), (2, 3, 0, 1), (0, 1, 2, 3))
        HT_BANK, P_BANK = 6, 7
        GU_BANK = (4, 5)
        WIN_BANK = ((4, 5), (2, 3))
        DOWN_PAIR = (0, 2)
        OUT_PAIR = (0, 6)
        Y_SB_PAIR = (4, 2)
        Y_DF_PAIR = (0, 6)
        E_PAIR = (4, 6)
        GATE_PAIR = (0, 2)
        QK_PAIR, OS_PAIR, OD_PAIR = 6, 0, 6
        SB_BANK = (0, 1)
        DF_BANK = (6, 7)
        SB_OUT = 384

        def slot(u):
            return u % SLOTS


        def wait_product(eng, done, count, i, u, t, c=0):
            if t == 0:
                eng.wait_ge(done, count)
            else:
                eng.wait_ge(units_used, UNITS * i + 3 * c + u + 1 + SLOTS)

        F_UNIT = (U_WIN - 1, U_FFN2 - 1, U_PROJ - 1, UNITS - 1)

        block = ctx.enter_context(nc.Block())

        @block.sync
        def _(sp_):
            for t in range(TT):
                sp_.dma_start(h[:, t, :], a["x"][0, t * P:(t + 1) * P, :]).then_inc(h_loaded, 16)

            def load(i, u, parts, c=0):
                sp_.wait_ge(split_done, UNITS * i + 3 * c + u + 1)
                for dst, src in parts:
                    sp_.dma_start(dst, src).then_inc(raw_in[slot(u)], 16)

            def load_gu(i, u, w, step, s, c=0):
                dst = raw[:, slot(u), :].rearrange("p (k g n) -> p k g n", k=4, g=2)
                rows = w[bass.ds(i, 1), s * 4 * P:(s + 1) * 4 * P, :].rearrange("o (k p) n -> p (o k) n", p=P)
                load(i, u, [(dst[:, :, g, :], rows[:, :, bass.ds(step * FC + g * FF, FC)]) for g in range(2)], c)

            def load_deep(i, u, w, row, c=0):
                dst = raw[:, slot(u), :].rearrange("p (k n) -> p k n", k=2)
                load(i, u, [(dst[:, k, :], w[bass.ds(i, 1), bass.ds(row + k * P, P), :].rearrange("o p n -> p (o n)"))
                            for k in range(2)], c)

            def load_ffn(i, u0, w_gu, w_down):
                for s in range(2):
                    load_gu(i, u0 + s, w_gu, 0, s)
                with sp_.Fori(1, NC) as c:
                    load_gu(i, u0 - 1, w_gu, c, 0, c)
                    load_gu(i, u0, w_gu, c, 1, c)
                    load_deep(i, u0 + 1, w_down, c * FC - FC, c)
                load_deep(i, u0 + U_FFN - 1, w_down, (NC - 1) * FC)

            with sp_.Fori(0, DEPTH) as i:
                load_ffn(i, U_FFN1, a["ffn1_w_gu"], a["ffn1_w_down"])
                for m in range(20):
                    dst = raw[:, slot(U_WIN + m), :].rearrange("p (k n) -> p k n", k=4)
                    r0, c0 = (m % 2) * 4 * P, (m // 2) * W
                    src = a["w_in"][bass.ds(i, 1), r0:r0 + 4 * P, c0:c0 + W].rearrange("o (k p) n -> p (o k) n", p=P)
                    load(i, U_WIN + m, [(dst[:, k:k + 2, :], src[:, k:k + 2, :]) for k in (0, 2)])
                for s in range(2):
                    load_deep(i, U_BSB + s, a["w_branch_sb"], 2 * P * s)
                for s in range(2):
                    load_deep(i, U_BDF + s, a["w_branch_diff"], 2 * P * s)
                for s in range(4):
                    load_deep(i, U_WOUT + s, a["w_out"], 2 * P * s)
                load_ffn(i, U_FFN2, a["ffn2_w_gu"], a["ffn2_w_down"])
                load_deep(i, U_PROJ, a["w_ple_proj"], 0)
                for s in range(4):
                    load_deep(i, U_GATE + s, a["w_ple_gate"], 2 * P * s)
            for t in range(TT):
                for n in range(2):
                    sp_.wait_ge(h_ready, 16 * DEPTH + 2 * t + n + 1)
                    sp_.dma_start(out[0, t * P:(t + 1) * P, n * W:(n + 1) * W],
                                  h[:, t, n * W:(n + 1) * W]).then_inc(out_done, 16)
            sp_.wait_ge(out_done, 16 * 2 * TT)

        @block.gpsimd
        def _(pool):
            for n, name in enumerate(("ffn1_pre_g", "mix_pre_g", "ffn2_pre_g", "ple_pre_g")):
                pool.dma_start(g_rows[2 * KD * n:2 * KD * (n + 1), :],
                               a[name].rearrange("l (k p) -> (l k) p", p=P)).then_inc(g_in, 16)
            pool.dma_start(g_rows[64:66, :], a["diff_subln_g"]).then_inc(g_in, 16)
            for t in range(TT):
                pool.dma_start(pos_i[:, t:t + 1], a["positions"][0, t * P:(t + 1) * P].rearrange(
                    "(p o) -> p o", o=1)).then_inc(pos_in, 16)
            pool.dma_start(lam_in[:, :, :, :].rearrange("p l f d -> p (l f d)"),
                           a["diff_lambda"].rearrange("l f d -> (l f d)").partition_broadcast(P)
                           ).then_inc(lam_loaded, 16)
            pool.memset(ident[:, :], 0.0).then_inc(blank, 1)
            pool.wait_ge(blank, 1)
            pool.affine_select(out=ident[:, :], in_=ident[:, :], compare_op=ALU.not_equal, fill=1.0,
                               base=0, pattern=[[-1, P]], channel_multiplier=1).then_inc(const_id, 1)
            pool.memset(neg_half[:, :], -0.5)
            pool.memset(eps_norm[:, :], EPS)
            pool.memset(eps_sub[:, :], SUB_EPS)
            pool.memset(q_factor[:, :], SB_D ** -0.5)
            pool.memset(ident_b[:, :], 0.0)
            pool.memset(neg_tri[:, :], -1.0)
            pool.memset(neg_one[:, :], -1.0)
            pool.memset(mask_sb[:, :], 0.0)
            pool.memset(mask_df[:, :], 0.0).then_inc(blank, 1)
            pool.wait_ge(blank, 2)
            pool.affine_select(out=ident_b[:, :], in_=ident_b[:, :], compare_op=ALU.not_equal, fill=1.0,
                               base=0, pattern=[[-1, P]], channel_multiplier=1)
            pool.affine_select(out=neg_tri[:, :], in_=neg_tri[:, :], compare_op=ALU.is_ge, fill=0.0,
                               base=0, pattern=[[-1, P]], channel_multiplier=1)
            for c in (0, 256):
                pool.affine_select(out=mask_sb[:, c:c + P], in_=mask_sb[:, c:c + P], compare_op=ALU.is_gt,
                                   fill=NEG, base=0, pattern=[[1, P]], channel_multiplier=-1)
                last = pool.affine_select(out=mask_df[:, c:c + P], in_=mask_df[:, c:c + P],
                                          compare_op=ALU.is_ge, fill=NEG, base=0, pattern=[[-1, P]],
                                          channel_multiplier=1)
            last.then_inc(const_all, 1)

            def rsqrt_mean(i, order, mean, ms, r, eps):
                pool.tensor_tensor(ms, mean, eps[:, 0:ms.shape[1]], ALU.add).then_inc(mean_done, 1)
                pool.wait_ge(mean_done, MEANS * i + order + 1)
                return pool.tensor_tensor(r, ms, neg_half[:, 0:ms.shape[1]], ALU.pow)

            def pre_norm(i, n, order):
                pool.wait_ge(squared_pre, 8 * i + 2 * n + 2)
                rsqrt_mean(i, order, mean_pre[:, :], ms_pre[:, :], r_pre[:, :], eps_norm).then_inc(pre_scale, 1)

            def post_norm(i, n, order):
                for t in range(TT):
                    pool.wait_ge(squared_post, 8 * i + 2 * n + t + 1)
                    rsqrt_mean(i, order + t, mean_post[:, t:t + 1], ms_post[:, t:t + 1], r_post[:, t:t + 1],
                               eps_norm).then_inc(post_scale, 1)

            with pool.Fori(0, DEPTH) as i:
                pre_norm(i, 0, 0)
                post_norm(i, 0, 1)
                pre_norm(i, 1, 3)
                pool.wait_ge(pre_scale, 4 * i + 2)
                pool.tensor_tensor(r_query[:, :], r_pre[:, :], q_factor[:, :], ALU.mult).then_inc(query_scale, 1)
                for hd in range(DF_HEADS):
                    pool.wait_ge(d_square, 4 * i + hd + 1)
                    rsqrt_mean(i, 4 + hd, mean_sub[:, :], ms_sub[:, :], r_sub[:, :], eps_sub
                               ).then_inc(d_scale, 1)
                post_norm(i, 1, 8)
                pre_norm(i, 2, 10)
                post_norm(i, 2, 11)
                pre_norm(i, 3, 13)
                post_norm(i, 3, 14)

        @block.scalar
        def _(act):
            act.wait_ge(angles, 1)
            act.activation(rope_s[:, :, 32:64], ang[:, :, :], ACT.Sin)
            act.activation(rope_c[:, :, 0:32], cos_in[:, :, :], ACT.Sin).then_inc(sines, 1)
            act.wait_ge(lam_sum, 1)
            act.activation(lam_e[:, :, :], lam_s[:, :, :], ACT.Exp).then_inc(lam_exp, 1)

            def high(i, u, gain=None, ks=4, c=0):
                s = slot(u)
                act.wait_ge(raw_in[s], 32 * (UNITS // 3) * i + 32 * c + 32 * (u // 3) + 32)
                act.wait_ge(units_used, UNITS * i + 3 * c + u + 1)
                if gain is None:
                    last = act.activation(w_hi[:, s, :], raw[:, s, :], ACT.Copy)
                else:
                    n = UNIT // ks
                    for k in range(ks):
                        last = act.activation(w_hi[:, s, k * n:(k + 1) * n], raw[:, s, k * n:(k + 1) * n],
                                              ACT.Copy, scale=g_layer[:, gain + k:gain + k + 1])
                last.then_inc(hi_ready, 1)

            def high_inputs(i, q):
                for idx in range(4):
                    t, n = idx // 2, idx % 2
                    act.wait_ge(x_turned, 20 * i + 4 * q + idx + 1)
                    act.activation(x_hi[:, 4 * n:4 * n + 4, t * P:(t + 1) * P],
                                   bank(X_BANK[q][idx]).rearrange("p (k n) -> p k n", k=4),
                                   ACT.Copy).then_inc(x_high, 1)

            def square_pre(i, n):
                for t in range(TT):
                    act.wait_ge(h_ready, 16 * i + 4 * n + 2 * t + 2)
                    act.activation(squares[:, :], h[:, t, :], ACT.Square, scale=D ** -0.5,
                                   accum_out=mean_pre[:, t:t + 1]).then_inc(squared_pre, 1)
                    act.wait_ge(squared_pre, 8 * i + 2 * n + t + 1)

            def square_post(i, n, src):
                for t in range(TT):
                    if n < 3:
                        wait_product(act, f_done, 4 * i + n + 1, i, F_UNIT[n], t)
                    else:
                        act.wait_ge(ple_e, 2 * i + t + 1)
                    act.activation(squares[:, :], src(t), ACT.Square, scale=D ** -0.5,
                                   accum_out=mean_post[:, t:t + 1]).then_inc(squared_post, 1)
                    act.wait_ge(squared_post, 8 * i + 2 * n + t + 1)

            def high_ht(i, f, c):
                act.wait_ge(ht_turned, 2 * NC * i + NC * f + c + 1)
                act.activation(ht_hi[:, :, :], bank(HT_BANK).rearrange("p (k n) -> p k n", k=2),
                               ACT.Copy).then_inc(ht_high, 1)

            def silu(i, f, step, u, c=0):
                for t in range(TT):
                    wait_product(act, gu_done, 2 * NC * i + NC * f + step + 1, i, u, t, c)
                    act.activation(glu[:, t, 0, :], bank(GU_BANK[t])[:, 0:FC], ACT.Silu,
                                   scale=r_pre[:, t:t + 1]).then_inc(silu_done, 1)

            def ffn(i, f, u0, g0, next_units):
                high(i, u0 + 2, g0)
                high(i, u0 + 3, g0 + 4)
                act.wait_ge(pre_scale, 4 * i + 2 * f + 1)
                silu(i, f, 0, u0 + 1)
                with act.Fori(1, NC - 1) as c:
                    high(i, u0 + 1, c=c)
                    high_ht(i, f, c - 1)
                    high(i, u0 + 2, g0, c=c)
                    silu(i, f, c, u0, c)
                    high(i, u0 + 3, g0 + 4, c=c)
                high(i, u0 + 3 * NC - 2)
                high_ht(i, f, NC - 2)
                high(i, u0 + 3 * NC - 1)
                silu(i, f, NC - 1, u0 + 3 * NC - 3)
                next_units(0)
                high_ht(i, f, NC - 1)
                next_units(1)

            def stick_weights(i, m):
                hd = m - SB_C0
                if 0 <= hd < SB_HEADS:
                    act.wait_ge(s_later, SB_HEADS * i + hd + 1)
                    act.activation(w_att[:, hd % 2, :], bank(SB_BANK[hd % 2])[:, 0:384], ACT.Exp
                                   ).then_inc(s_weight, 1)

            def stick_softplus(i, m):
                hd = m - SB_Z0
                if 0 <= hd < SB_HEADS:
                    act.wait_ge(s_score, SB_HEADS * i + hd + 1)
                    act.activation(soft[:, hd % 2, :], bank(SB_BANK[hd % 2])[:, 0:384], ACT.Abs).then_inc(s_abs, 1)
                    act.wait_ge(s_abs, SB_HEADS * i + hd + 1)
                    act.activation(soft[:, hd % 2, :], soft[:, hd % 2, :], ACT.Exp, scale=-1.0).then_inc(s_exp, 1)
                    act.wait_ge(s_exp, SB_HEADS * i + hd + 1)
                    act.activation(soft[:, hd % 2, :], soft[:, hd % 2, :], ACT.Ln, bias=1.0).then_inc(s_log, 1)

            def diff_after(i, m):
                if m >= DF_Z0 and (m - DF_Z0) % 2 == 0 and (m - DF_Z0) // 2 < DF_HEADS:
                    hd = (m - DF_Z0) // 2
                    act.wait_ge(d_max, DF_HEADS * i + hd + 1)
                    for c in range(2):
                        for t, (lo, hi) in enumerate(((0, P), (P, 384))):
                            last = act.activation(prob[:, c, lo:hi], bank(DF_BANK[c])[:, lo:hi], ACT.Exp,
                                                  bias=neg_max[:, 2 * c + t:2 * c + t + 1],
                                                  accum_out=p_sum[:, 2 * c + t:2 * c + t + 1])
                    last.then_inc(d_exp, 1)
                if m >= DF_T0 and (m - DF_T0) % 2 == 0 and (m - DF_T0) // 2 < DF_HEADS:
                    hd = (m - DF_T0) // 2
                    act.wait_ge(d_turned, DF_HEADS * i + hd + 1)
                    act.activation(mixed_t[:, :], bank(DF_BANK[0])[:, 0:384], ACT.Copy).then_inc(d_kept, 1)

            def diff_mid(i, m):
                if m >= DF_P0 and (m - DF_P0) % 2 == 0 and (m - DF_P0) // 2 < DF_HEADS:
                    hd = (m - DF_P0) // 2
                    act.wait_ge(d_value, DF_HEADS * i + hd + 1)
                    if hd:
                        act.wait_ge(d_square, DF_HEADS * i + hd)
                    for t in range(TT):
                        last = act.activation(squares[:, t * P:(t + 1) * P], bank(DF_BANK[1])[:, t * P:(t + 1) * P],
                                              ACT.Square, scale=DF_V ** -0.5, accum_out=mean_sub[:, t:t + 1])
                    last.then_inc(d_square, 1)

            def keep(i, m):
                j = m // 2
                if m % 2 == 0 or m >= 20 or j in (SBV, DFV):
                    return
                if j == SBQ:
                    act.wait_ge(query_scale, i + 1)
                for t in range(TT):
                    wait_product(act, win_done, 10 * i + j + 1, i, U_WIN + m, t)
                    src = bank(WIN_BANK[j % 2][t])
                    if j < 6:
                        if t == 0 and QK_ORDER[j]:
                            act.wait_ge(qk_turned, 4 * i + QK_ORDER[j])
                        r = r_query if j in (SBQ, DFQ) else r_pre
                        act.activation(slab[:, t, :], src, ACT.Copy, scale=r[:, t:t + 1]).then_inc(kept_act, 1)
                    else:
                        g, n = (j - 6) // 2, (j - 6) % 2
                        act.activation(gates[:, g, t, n * W:(n + 1) * W], src, ACT.Copy,
                                       scale=r_pre[:, t:t + 1]).then_inc(kept_act, 1)

            def mixer(i):
                for m in range(28):
                    if m < 18:
                        high(i, U_WIN + m + 2, 8 + 4 * (m % 2))
                    elif m in (20, 21):
                        high(i, U_WIN + m + 2, 32, ks=1)
                    elif m < 26:
                        high(i, U_WIN + m + 2)
                    else:
                        high(i, U_WIN + m + 2, 16 + 4 * (m - 26))
                    diff_mid(i, m)
                    if m == 20:
                        act.wait_ge(kept_act, 16 * i + 16)
                        for g in range(2):
                            for t in range(TT):
                                act.activation(gates[:, g, t, :], gates[:, g, t, :], ACT.Sigmoid).then_inc(gate_sig, 1)
                    keep(i, m)
                    stick_weights(i, m)
                    diff_after(i, m)
                    if m in (2, 4):
                        k = (m - 2) // 2
                        act.wait_ge(qk_turned, 4 * i + k + 1)
                        act.activation((sbq_t, sbk_t)[k][:, :, :].rearrange("p k n -> p (k n)"), pair(QK_PAIR),
                                       ACT.Copy).then_inc(sb_turned, 1)
                    if m == 16:
                        act.wait_ge(os_turned, i + 1)
                        act.activation(os_hi[:, :, :].rearrange("p k n -> p (k n)"), pair(OS_PAIR),
                                       ACT.Copy).then_inc(os_high, 1)
                    if m == 20:
                        act.wait_ge(od_turned, i + 1)
                        act.activation(x_hi[:, 0:4, :].rearrange("p k n -> p (k n)"), pair(OD_PAIR),
                                       ACT.Copy).then_inc(od_high, 1)
                    stick_softplus(i, m)
                    if m == 23:
                        high_inputs(i, 2)

            def load_post(i, name, n, s):
                act.wait_ge(h_ready, 16 * i + 4 * n + 4)
                act.dma_start(post_g[:, s, :],
                              a[name][bass.ds(i, 1), :].rearrange("o n -> (o n)").partition_broadcast(P)
                              ).then_inc(post_in[s], 16)

            with act.Fori(0, DEPTH) as i:
                act.wait_ge(layer_g, i + 1)
                high(i, 0, 0)
                high(i, 1, 4)
                high_inputs(i, 0)
                square_pre(i, 0)
                load_post(i, "ffn1_post_g", 0, 0)
                load_post(i, "mix_post_g", 0, 1)
                act.dma_start(p_nat[:, :, :], a["p"][bass.ds(i, 1), 0, :, :].rearrange(
                    "o (t p) n -> p (o t) n", p=P)).then_inc(p_in, 16)
                ffn(i, 0, U_FFN1, 0, lambda s: high(i, U_WIN + s, 8 + 4 * s))
                square_post(i, 0, lambda t: pair(DOWN_PAIR[t]))

                high_inputs(i, 1)
                square_pre(i, 1)
                load_post(i, "ffn2_post_g", 1, 0)
                act.wait_ge(pre_scale, 4 * i + 2)
                mixer(i)
                square_post(i, 1, lambda t: pair(OUT_PAIR[t]))

                high_inputs(i, 3)
                square_pre(i, 2)
                load_post(i, "ple_post_g", 2, 1)
                ffn(i, 1, U_FFN2, 16, lambda s: high(i, U_PROJ + s, (None, 24)[s], ks=2))
                act.wait_ge(p_turned, i + 1)
                act.activation(p_hi[:, :, :], bank(P_BANK).rearrange("p (k n) -> p k n", k=2),
                               ACT.Copy).then_inc(p_high, 1)
                square_post(i, 2, lambda t: pair(DOWN_PAIR[t]))

                high(i, U_GATE + 1, 26, ks=2)
                high_inputs(i, 4)
                high(i, U_GATE + 2, 28, ks=2)
                square_pre(i, 3)
                high(i, U_GATE + 3, 30, ks=2)
                act.wait_ge(pre_scale, 4 * i + 4)
                for t in range(TT):
                    wait_product(act, f_done, 4 * i + 4, i, F_UNIT[3], t)
                    act.activation(gates[:, 0, t, :], pair(GATE_PAIR[t]), ACT.Sigmoid,
                                   scale=r_pre[:, t:t + 1]).then_inc(ple_sig, 1)
                square_post(i, 3, lambda t: gates[:, 1, t, :])

        @block.vector
        def _(dve):
            dve.memset(freq[:, 0:1], 1.0).then_inc(split_done, SLOTS)
            dve.memset(freq[:, 1:2], float(np.float32(THETA ** (-1 / 32)))).then_inc(h_ready, 4)
            for j in range(2, 32):
                last = dve.memset(freq[:, j:j + 1], float(np.float32(THETA ** (-j / 32))))

            linked = [0]

            def link(ins):
                linked[0] += 1
                ins.then_inc(setup_step, 1)
                dve.wait_ge(setup_step, linked[0])

            link(last)
            dve.wait_ge(pos_in, 16 * TT)
            link(dve.tensor_copy(pos_f[:, :], pos_i[:, :]))
            for t in range(TT):
                last = dve.tensor_scalar(ang[:, t, :], freq[:, :], pos_f[:, t:t + 1], None, ALU.mult)
            link(last)
            link(dve.tensor_scalar(turns[:, :, :], ang[:, :, :], 1 / (2 * math.pi), ROUND, ALU.mult, ALU.add))
            link(dve.tensor_scalar(turns[:, :, :], turns[:, :, :], -ROUND, None, ALU.add))
            for part in TWO_PI:
                link(dve.scalar_tensor_tensor(out=ang[:, :, :], in0=turns[:, :, :], scalar=-part, in1=ang[:, :, :],
                                              op0=ALU.mult, op1=ALU.add))
            link(dve.tensor_scalar(ang[:, :, :], ang[:, :, :], PI_IN, -PI_IN, ALU.min, ALU.max))
            link(dve.scalar_tensor_tensor(out=cos_in[:, :, :], in0=ang[:, :, :], scalar=-1.0, in1=ang[:, :, :],
                                          op0=ALU.mult, op1=ALU.min))
            dve.tensor_scalar(cos_in[:, :, :], cos_in[:, :, :], math.pi / 2, None, ALU.add).then_inc(angles, 1)
            dve.wait_ge(lam_loaded, 16)
            link(dve.tensor_tensor(lam_pr[:, :, :, :], lam_in[:, :, 0::2, :], lam_in[:, :, 1::2, :], ALU.mult))
            dve.tensor_reduce(lam_s[:, :, :], lam_pr[:, :, :, :], AX_X, ALU.add).then_inc(lam_sum, 1)
            dve.wait_ge(sines, 1)
            dve.tensor_scalar(rope_s[:, :, 0:32], rope_s[:, :, 32:64], -1.0, None, ALU.mult)
            dve.tensor_copy(rope_c[:, :, 32:64], rope_c[:, :, 0:32])
            dve.wait_ge(lam_exp, 1)
            link(dve.tensor_tensor(neg_lams[:, :], lam_e[:, :, 1], lam_e[:, :, 0], ALU.subtract))
            for n in range(DEPTH):
                last = dve.tensor_scalar(neg_lams[:, n:n + 1], neg_lams[:, n:n + 1], -LAM_INIT[n], None, ALU.add)
            dve.wait_ge(cols_turned, 1)
            dve.tensor_copy(g_cols[:, 0:64], bank(0)[:, 0:64])
            for n in range(DEPTH):
                last = dve.tensor_scalar(g_cols[:, 64 + n:65 + n], bank(0)[:, 64 + n:65 + n], 1.0 - LAM_INIT[n],
                                         None, ALU.mult)
            last.then_inc(cols_kept, 1)
            dve.wait_ge(cols_kept, 1)

            def low(i, u, gain=None, ks=4, c=0):
                s = slot(u)
                dve.wait_ge(hi_ready, UNITS * i + 3 * c + u + 1)
                whi = w_hi[:, s, :].bitcast(F32)
                if gain is None:
                    last = dve.tensor_tensor(w_lo[:, s, :], raw[:, s, :], whi, ALU.subtract)
                else:
                    n = UNIT // ks
                    for k in range(ks):
                        part = slice(k * n, (k + 1) * n)
                        last = dve.scalar_tensor_tensor(out=w_lo[:, s, part], in0=raw[:, s, part],
                                                        scalar=g_layer[:, gain + k:gain + k + 1],
                                                        in1=whi[:, part], op0=ALU.mult, op1=ALU.subtract)
                last.then_inc(split_done, 1)

            def low_inputs(i, q, idxs):
                for idx in idxs:
                    t, n = idx // 2, idx % 2
                    dve.wait_ge(x_high, 20 * i + 4 * q + idx + 1)
                    part = (slice(None), slice(4 * n, 4 * n + 4), slice(t * P, (t + 1) * P))
                    dve.tensor_tensor(x_lo[part], bank(X_BANK[q][idx]).rearrange("p (k n) -> p k n", k=4),
                                      x_hi[part].bitcast(F32), ALU.subtract).then_inc(x_split, 1)

            def low_ht(i, f, c):
                dve.wait_ge(ht_high, 2 * NC * i + NC * f + c + 1)
                dve.tensor_tensor(ht_lo[:, :, :], bank(HT_BANK).rearrange("p (k n) -> p k n", k=2),
                                  ht_hi[:, :, :].bitcast(F32), ALU.subtract).then_inc(ht_split, 1)

            def products(i, f, c):
                for t in range(TT):
                    dve.wait_ge(silu_done, 4 * NC * i + 2 * NC * f + 2 * c + t + 1)
                    dve.scalar_tensor_tensor(out=glu[:, t, 1, :], in0=bank(GU_BANK[t])[:, FC:2 * FC],
                                             scalar=r_pre[:, t:t + 1], in1=glu[:, t, 0, :],
                                             op0=ALU.mult, op1=ALU.mult).then_inc(prod_done, 1)

            def ffn(i, f, u0, g0, next_units):
                low(i, u0 + 2, g0)
                low(i, u0 + 3, g0 + 4)
                products(i, f, 0)
                with dve.Fori(1, NC - 1) as c:
                    low(i, u0 + 1, c=c)
                    low_ht(i, f, c - 1)
                    low(i, u0 + 2, g0, c=c)
                    products(i, f, c)
                    low(i, u0 + 3, g0 + 4, c=c)
                low(i, u0 + 3 * NC - 2)
                low_ht(i, f, NC - 2)
                low(i, u0 + 3 * NC - 1)
                products(i, f, NC - 1)
                next_units(0)
                low_ht(i, f, NC - 1)
                next_units(1)

            def post_norm(i, n, src, factor, t):
                dve.wait_ge(post_in[n % 2], 32 * i + 16 * (n // 2) + 16)
                dve.wait_ge(post_scale, 8 * i + 2 * n + t + 1)
                halves = [slice(0, W), slice(W, D)]
                for s in halves:
                    dve.scalar_tensor_tensor(out=tmp[:, t, s], in0=src[:, s], scalar=r_post[:, t:t + 1],
                                             in1=post_g[:, n % 2, s], op0=ALU.mult, op1=ALU.mult
                                             ).then_inc(scaled, 1)
                for k, s in enumerate(halves):
                    dve.wait_ge(scaled, 16 * i + 4 * n + 2 * t + k + 1)
                    dve.scalar_tensor_tensor(out=h[:, t, s], in0=tmp[:, t, s], scalar=factor, in1=h[:, t, s],
                                             op0=ALU.mult, op1=ALU.add).then_inc(h_ready, 1)

            def norm_and_inputs(i, n, q, pairs, factor):
                for t in range(TT):
                    post_norm(i, n, pair(pairs[t]), factor, t)
                    low_inputs(i, q, (2 * t, 2 * t + 1))

            def rope(i, k):
                dve.wait_ge(kept_act, 16 * i + 2 * (2 + k) + 2)
                for t in range(TT):
                    x = slab[:, t, :].rearrange("p (g c) -> p g c", c=64)
                    y = rope_b[:, t, :].rearrange("p (g c) -> p g c", c=64)
                    dve.tensor_tensor(slab_c[:, t, :].rearrange("p (g c) -> p g c", c=64), x,
                                      rope_c[:, t:t + 1, :].to_broadcast([P, 8, 64]), ALU.mult)
                    dve.tensor_tensor(y[:, :, 0:32], x[:, :, 32:64],
                                      rope_s[:, t:t + 1, 0:32].to_broadcast([P, 8, 32]), ALU.mult)
                    dve.tensor_tensor(y[:, :, 32:64], x[:, :, 0:32],
                                      rope_s[:, t:t + 1, 32:64].to_broadcast([P, 8, 32]), ALU.mult
                                      ).then_inc(rope_parts, 1)
                for t in range(TT):
                    dve.wait_ge(rope_parts, 4 * i + 2 * k + t + 1)
                    dve.tensor_tensor(slab[:, t, :], slab_c[:, t, :], rope_b[:, t, :], ALU.add).then_inc(roped, 1)

            def mixer(i):
                for m in range(28):
                    if m < 18:
                        low(i, U_WIN + m + 2, 8 + 4 * (m % 2))
                    elif m in (20, 21):
                        low(i, U_WIN + m + 2, 32, ks=1)
                    elif m < 26:
                        low(i, U_WIN + m + 2)
                    else:
                        low(i, U_WIN + m + 2, 16 + 4 * (m - 26))
                    hd = m - SB_P0
                    if 0 <= hd < SB_HEADS:
                        dve.wait_ge(s_value, SB_HEADS * i + hd + 1)
                        dve.tensor_copy(o_sb[:, :, hd * SB_D:(hd + 1) * SB_D],
                                        bank(SB_BANK[hd % 2])[:, SB_OUT:W].rearrange("p (t n) -> p t n", t=TT)
                                        ).then_inc(s_kept, 1)
                    if m >= DF_P0 and (m - DF_P0) % 2 == 0 and (m - DF_P0) // 2 < DF_HEADS:
                        hd = (m - DF_P0) // 2
                        dve.wait_ge(d_scale, DF_HEADS * i + hd + 1)
                        for t in range(TT):
                            last = dve.tensor_scalar(o_df[:, t, hd * DF_V:(hd + 1) * DF_V],
                                                     bank(DF_BANK[1])[:, t * P:(t + 1) * P], r_sub[:, t:t + 1],
                                                     None, ALU.mult)
                        last.then_inc(d_normed, 1)
                    if m in (5, 11):
                        j = m // 2
                        for t in range(TT):
                            wait_product(dve, win_done, 10 * i + j + 1, i, U_WIN + m, t)
                            dve.tensor_scalar((v_sb, v_df)[j == DFV][:, t, :], bank(WIN_BANK[j % 2][t]),
                                              r_pre[:, t:t + 1], None, ALU.mult).then_inc(kept_dve, 1)
                    diff = m >= DF_Z0 and (m - DF_Z0) % 2 == 0 and (m - DF_Z0) // 2 < DF_HEADS
                    if diff:
                        hd = (m - DF_Z0) // 2
                        dve.wait_ge(d_score, DF_HEADS * i + hd + 1)
                        for c in range(2):
                            for t, (lo, hi) in enumerate(((0, P), (P, 384))):
                                last = dve.tensor_reduce(neg_max[:, 2 * c + t:2 * c + t + 1],
                                                         bank(DF_BANK[c])[:, lo:hi], AX_X, ALU.max, negate=True)
                        last.then_inc(d_max, 1)
                    if m in (9, 11):
                        k = (m - 9) // 2
                        dve.wait_ge(qk_turned, 4 * i + 2 + k + 1)
                        dve.tensor_copy((dfq_t, dfk_t)[k][:, :, :].rearrange("p k n -> p (k n)"),
                                        pair(QK_PAIR)).then_inc(df_turned, 1)
                    hd = m - SB_Z0
                    if 0 <= hd < SB_HEADS:
                        dve.wait_ge(s_log, SB_HEADS * i + hd + 1)
                        dve.scalar_tensor_tensor(out=sp[:, hd % 2, :], in0=bank(SB_BANK[hd % 2])[:, 0:384], scalar=0.0,
                                                 in1=soft[:, hd % 2, :], op0=ALU.max, op1=ALU.add
                                                 ).then_inc(s_soft, 1)
                    if diff:
                        hd = (m - DF_Z0) // 2
                        n = DF_HEADS * i + hd + 1
                        dve.wait_ge(d_exp, n)
                        dve.reciprocal(p_rec[:, :], p_sum[:, :]).then_inc(d_rec, 1)
                        dve.wait_ge(d_rec, n)
                        dve.tensor_scalar(neg_lr[:, :], p_rec[:, 2:4], neg_lam[:, 0:1], None, ALU.mult
                                          ).then_inc(d_lam, 1)
                        dve.wait_ge(d_lam, n)
                        for t, (lo, hi) in enumerate(((0, P), (P, 384))):
                            last = dve.tensor_scalar(prob[:, 1, lo:hi], prob[:, 1, lo:hi], neg_lr[:, t:t + 1],
                                                     None, ALU.mult)
                        last.then_inc(d_part, 1)
                        dve.wait_ge(d_part, n)
                        for t, (lo, hi) in enumerate(((0, P), (P, 384))):
                            last = dve.scalar_tensor_tensor(out=mixed[:, lo:hi], in0=prob[:, 0, lo:hi],
                                                            scalar=p_rec[:, t:t + 1], in1=prob[:, 1, lo:hi],
                                                            op0=ALU.mult, op1=ALU.add)
                        last.then_inc(d_mixed, 1)
                    if m in (7, 9):
                        rope(i, (m - 7) // 2)
                    if m == 16:
                        dve.wait_ge(os_high, i + 1)
                        dve.tensor_tensor(os_lo[:, :, :].rearrange("p k n -> p (k n)"), pair(OS_PAIR),
                                          os_hi[:, :, :].rearrange("p k n -> p (k n)").bitcast(F32),
                                          ALU.subtract).then_inc(os_split, 1)
                    if m == 20:
                        dve.wait_ge(od_high, i + 1)
                        dve.tensor_tensor(x_lo[:, 0:4, :].rearrange("p k n -> p (k n)"), pair(OD_PAIR),
                                          x_hi[:, 0:4, :].rearrange("p k n -> p (k n)").bitcast(F32),
                                          ALU.subtract).then_inc(od_split, 1)
                    if m == 21:
                        for t in range(TT):
                            dve.wait_ge(gate_sig, 4 * i + 4)
                            wait_product(dve, y_sb_done, i + 1, i, U_BSB + 1, t)
                            dve.tensor_tensor(gates[:, 0, t, :], pair(Y_SB_PAIR[t]), gates[:, 0, t, :],
                                              ALU.mult).then_inc(gated_sb, 1)
                    if m == 23:
                        for t in range(TT):
                            wait_product(dve, y_df_done, i + 1, i, U_BDF + 1, t)
                            for n in range(2):
                                s = slice(n * W, (n + 1) * W)
                                dve.tensor_tensor(gates[:, 1, t, s], bank(Y_DF_PAIR[t] + n), gates[:, 1, t, s],
                                                  ALU.mult).then_inc(gated_df, 1)
                            for n in range(2):
                                s = slice(n * W, (n + 1) * W)
                                dve.wait_ge(gated_sb, 2 * i + t + 1)
                                dve.wait_ge(gated_df, 4 * i + 2 * t + n + 1)
                                dve.tensor_tensor(gates[:, 0, t, s], gates[:, 0, t, s], gates[:, 1, t, s],
                                                  ALU.add).then_inc(merged, 1)
                            low_inputs(i, 2, (2 * t, 2 * t + 1))

            with dve.Fori(0, DEPTH) as i:
                dve.tensor_copy(neg_lam[:, :], neg_lams[:, bass.ds(i, 1)])
                dve.tensor_copy(g_layer[:, 32:33], g_cols[:, bass.ds(i + 64, 1)])
                dve.tensor_copy(g_layer[:, 0:32].rearrange("p (n k) -> p n k", n=4),
                                g_cols[:, 0:64].rearrange("p (n l k) -> p n (l k)", n=4, l=DEPTH)[
                                    :, :, bass.ds(i * KD, KD)]).then_inc(layer_g, 1)
                dve.wait_ge(layer_g, i + 1)
                low(i, 0, 0)
                low_inputs(i, 0, (0, 1))
                low(i, 1, 4)
                low_inputs(i, 0, (2, 3))
                ffn(i, 0, U_FFN1, 0, lambda s: low(i, U_WIN + s, 8 + 4 * s))
                norm_and_inputs(i, 0, 1, DOWN_PAIR, 0.5)
                mixer(i)
                norm_and_inputs(i, 1, 3, OUT_PAIR, 1.0)
                ffn(i, 1, U_FFN2, 16, lambda s: low(i, U_PROJ + s, (None, 24)[s], ks=2))
                dve.wait_ge(p_high, i + 1)
                dve.tensor_tensor(p_lo[:, :, :], bank(P_BANK).rearrange("p (k n) -> p k n", k=2),
                                  p_hi[:, :, :].bitcast(F32), ALU.subtract).then_inc(p_split, 1)
                post_norm(i, 2, pair(DOWN_PAIR[0]), 0.5, 0)
                post_norm(i, 2, pair(DOWN_PAIR[1]), 0.5, 1)
                low(i, U_GATE + 1, 26, ks=2)
                low_inputs(i, 4, range(4))
                low(i, U_GATE + 2, 28, ks=2)
                low(i, U_GATE + 3, 30, ks=2)
                for t in range(TT):
                    dve.wait_ge(ple_sig, 2 * i + t + 1)
                    wait_product(dve, e_done, i + 1, i, U_PROJ, t)
                    dve.tensor_tensor(gates[:, 1, t, :], pair(E_PAIR[t]), gates[:, 0, t, :], ALU.mult
                                      ).then_inc(ple_e, 1)
                for t in range(TT):
                    post_norm(i, 3, gates[:, 1, t, :], 1.0, t)

        @block.tensor
        def _(pe):
            pe.wait_ge(const_id, 1)
            pe.wait_ge(g_in, 16 * 5)
            pe.transpose(bank(0)[:, 0:66], g_rows[0:66, :], ident[0:66, 0:66]).then_inc(cols_turned, 1)
            pe.transpose(bank(1)[:, 0:66], g_rows[0:66, :], ident[0:66, 0:66]).then_inc(units_used, SLOTS)

            def exact(dst, x_h, x_l, w_h, w_l, first, last):
                pe.matmul(dst, x_h, w_h, start=first, stop=False)
                pe.matmul(dst, x_h, w_l, start=False, stop=False)
                return pe.matmul(dst, x_l, w_h, start=False, stop=last)

            def wide(s, dst, xh, xl, k0, t, first, last):
                for k in range(4):
                    cols, toks = slice(k * W, (k + 1) * W), slice(t * P, (t + 1) * P)
                    mm = exact(dst, xh[:, k0 + k, toks], xl[:, k0 + k, toks], w_hi[:, s, cols], w_lo[:, s, cols],
                               first and k == 0, last and k == 3)
                return mm

            def deep(s, b, xh, xl, k0, t, first, last):
                toks = slice(t * P, (t + 1) * P)
                for n in range(2):
                    for k in range(2):
                        cols = slice(k * D + n * W, k * D + (n + 1) * W)
                        mm = exact(bank(b + n), xh[:, k0 + k, toks], xl[:, k0 + k, toks],
                                   w_hi[:, s, cols], w_lo[:, s, cols], first and k == 0, last and k == 1)
                return mm

            def begin(i, u, c=0):
                pe.wait_ge(split_done, UNITS * i + 3 * c + u + 1 + SLOTS)

            def turn_inputs(i, q, src, ready, count):
                for idx in range(4):
                    t, n = idx // 2, idx % 2
                    pe.wait_ge(ready, count + idx + 1)
                    for k in range(4):
                        mm = pe.transpose(bank(X_BANK[q][idx])[:, k * P:(k + 1) * P],
                                          src(t)[:, (4 * n + k) * P:(4 * n + k + 1) * P], ident[:, :])
                    mm.then_inc(x_turned, 1)

            def inputs(i, q, t):
                pe.wait_ge(x_split, 20 * i + 4 * q + 2 * t + 2)

            def turn_ht(i, f, c):
                pe.wait_ge(prod_done, 4 * NC * i + 2 * NC * f + 2 * c + 2)
                for k in range(2):
                    for t in range(TT):
                        mm = pe.transpose(bank(HT_BANK)[:, k * SEQ + t * P:k * SEQ + (t + 1) * P],
                                          glu[:, t, 1, k * P:(k + 1) * P], ident[:, :])
                mm.then_inc(ht_turned, 1)


            def ffn(i, f, q, u0, before_last):
                def gate_up(u, half, step, c=0):
                    begin(i, u, c)
                    for t in range(TT):
                        if half == 0 and step is None:
                            inputs(i, q, t)
                        elif half == 0:
                            pe.wait_ge(prod_done, 4 * NC * i + 2 * NC * f + 2 * step + t - 1)
                        mm = wide(slot(u), bank(GU_BANK[t]), x_hi, x_lo, 4 * half, t, half == 0, half == 1)
                        if half == 1 and t == 0:
                            mm.then_inc(gu_done, 1)
                    mm.then_inc(units_used, 1)

                def down(u, step, first=False, last=False, c=0):
                    begin(i, u, c)
                    pe.wait_ge(ht_split, 2 * NC * i + NC * f + step + 1)
                    for t in range(TT):
                        mm = deep(slot(u), DOWN_PAIR[t], ht_hi, ht_lo, 0, t, first, last)
                        if last and t == 0:
                            mm.then_inc(f_done, 1)
                    mm.then_inc(units_used, 1)

                def step(c, at, first=False):
                    gate_up(u0 - 1, 0, c, at)
                    turn_ht(i, f, c - 1)
                    gate_up(u0, 1, c, at)
                    down(u0 + 1, c - 1, first=first, c=at)

                gate_up(u0, 0, None)
                gate_up(u0 + 1, 1, 0)
                step(1, 1, first=True)
                with pe.Fori(2, NC) as c:
                    step(c, c)
                turn_ht(i, f, NC - 1)
                before_last()
                down(u0 + 3 * NC - 1, NC - 1, last=True)

            def turn_four(dst, src):
                for k in range(4):
                    for t in range(TT):
                        mm = pe.transpose(dst[:, k * SEQ + t * P:k * SEQ + (t + 1) * P],
                                          src[:, t, k * P:(k + 1) * P], ident[:, :])
                return mm

            def stick_scores(i, hd):
                pe.wait_ge(sb_turned, 2 * i + 2)
                if hd >= 2:
                    pe.wait_ge(s_kept, SB_HEADS * i + hd - 1)
                dst, rows, k = bank(SB_BANK[hd % 2]), slice(64 * (hd % 2), 64 * (hd % 2) + 64), hd // 2
                pe.matmul(dst[:, 0:384], ident_b[:, :], mask_sb[:, :], start=True, stop=False, skip_group_check=True)
                pe.matmul(dst[:, 0:SEQ], sbk_t[rows, k, 0:P], sbq_t[rows, k, :], start=False, stop=False,
                          skip_group_check=True)
                pe.matmul(dst[:, SEQ:384], sbk_t[rows, k, P:SEQ], sbq_t[rows, k, P:SEQ], start=False, stop=True,
                          skip_group_check=True).then_inc(s_score, 1)

            def stick_later(i, hd):
                pe.wait_ge(s_soft, SB_HEADS * i + hd + 1)
                dst, s = bank(SB_BANK[hd % 2]), sp[:, hd % 2, :]
                pe.matmul(dst[:, 0:SEQ], neg_tri[:, :], s[:, 0:SEQ], start=False, stop=False, skip_group_check=True)
                pe.matmul(dst[:, P:SEQ], neg_one[:, :], s[:, SEQ:384], start=False, stop=False, skip_group_check=True)
                pe.matmul(dst[:, SEQ:384], neg_tri[:, :], s[:, SEQ:384], start=False, stop=True,
                          skip_group_check=True).then_inc(s_later, 1)

            def stick_values(i, hd):
                pe.wait_ge(s_weight, SB_HEADS * i + hd + 1)
                pe.wait_ge(kept_dve, 4 * i + 2)
                dst, w, c = bank(SB_BANK[hd % 2]), w_att[:, hd % 2, :], slice(hd * SB_D, (hd + 1) * SB_D)
                pe.matmul(dst[:, SB_OUT:SB_OUT + 64], w[:, 0:P], v_sb[:, 0, c], start=True, stop=True,
                          skip_group_check=True)
                pe.matmul(dst[:, SB_OUT + 64:W], w[:, P:SEQ], v_sb[:, 0, c], start=True, stop=False,
                          skip_group_check=True)
                pe.matmul(dst[:, SB_OUT + 64:W], w[:, SEQ:384], v_sb[:, 1, c], start=False, stop=True,
                          skip_group_check=True).then_inc(s_value, 1)

            def diff_scores(i, hd):
                pe.wait_ge(df_turned, 2 * i + 2)
                if hd:
                    pe.wait_ge(d_kept, DF_HEADS * i + hd)
                    pe.wait_ge(d_normed, DF_HEADS * i + hd)
                for c in range(2):
                    dst, rows = bank(DF_BANK[c]), slice(64 * c, 64 * c + 64)
                    pe.matmul(dst[:, 0:384], ident_b[:, :], mask_df[:, :], start=True, stop=False,
                              skip_group_check=True)
                    pe.matmul(dst[:, 0:P], dfq_t[rows, hd, 0:P], dfk_t[rows, hd, 0:P], start=False, stop=False,
                              skip_group_check=True)
                    mm = pe.matmul(dst[:, P:384], dfq_t[rows, hd, P:SEQ], dfk_t[rows, hd, :], start=False, stop=True,
                                   skip_group_check=True)
                mm.then_inc(d_score, 1)

            def diff_turn(i, hd):
                pe.wait_ge(d_mixed, DF_HEADS * i + hd + 1)
                for k in range(3):
                    mm = pe.transpose(bank(DF_BANK[0])[:, k * P:(k + 1) * P], mixed[:, k * P:(k + 1) * P], ident[:, :])
                mm.then_inc(d_turned, 1)

            def diff_values(i, hd):
                pe.wait_ge(d_kept, DF_HEADS * i + hd + 1)
                pe.wait_ge(kept_dve, 4 * i + 4)
                dst, c = bank(DF_BANK[1]), slice(hd * DF_V, (hd + 1) * DF_V)
                pe.matmul(dst[:, 0:P], mixed_t[:, 0:P], v_df[:, 0, c], start=True, stop=True, skip_group_check=True)
                pe.matmul(dst[:, P:SEQ], mixed_t[:, P:SEQ], v_df[:, 0, c], start=True, stop=False,
                          skip_group_check=True)
                pe.matmul(dst[:, P:SEQ], mixed_t[:, SEQ:384], v_df[:, 1, c], start=False, stop=True,
                          skip_group_check=True).then_inc(d_value, 1)

            def middle(i, m):
                if 0 <= m - SB_P0 < SB_HEADS:
                    stick_values(i, m - SB_P0)
                if 0 <= m - DF_P0 < 2 * DF_HEADS and (m - DF_P0) % 2 == 0:
                    diff_values(i, (m - DF_P0) // 2)

            def behind(i, m):
                if m == 2:
                    pe.wait_ge(kept_act, 16 * i + 2)
                    turn_four(pair(QK_PAIR), slab).then_inc(qk_turned, 1)
                if m == 4:
                    pe.wait_ge(kept_act, 16 * i + 4)
                    pe.wait_ge(sb_turned, 2 * i + 1)
                    turn_four(pair(QK_PAIR), slab).then_inc(qk_turned, 1)
                if m == 9:
                    pe.wait_ge(roped, 4 * i + 2)
                    pe.wait_ge(sb_turned, 2 * i + 2)
                    turn_four(pair(QK_PAIR), slab).then_inc(qk_turned, 1)
                if m == 11:
                    pe.wait_ge(roped, 4 * i + 4)
                    pe.wait_ge(df_turned, 2 * i + 1)
                    turn_four(pair(QK_PAIR), slab).then_inc(qk_turned, 1)
                if 0 <= m - SB_C0 < SB_HEADS:
                    stick_later(i, m - SB_C0)
                if 0 <= m - SB_Z0 < SB_HEADS:
                    stick_scores(i, m - SB_Z0)
                if 0 <= m - DF_Z0 < 2 * DF_HEADS and (m - DF_Z0) % 2 == 0:
                    diff_scores(i, (m - DF_Z0) // 2)
                if 0 <= m - DF_T0 < 2 * DF_HEADS and (m - DF_T0) % 2 == 0:
                    diff_turn(i, (m - DF_T0) // 2)
                if m == 16:
                    pe.wait_ge(s_kept, SB_HEADS * (i + 1))
                    turn_four(pair(OS_PAIR), o_sb).then_inc(os_turned, 1)
                if m == 20:
                    pe.wait_ge(d_normed, DF_HEADS * (i + 1))
                    turn_four(pair(OD_PAIR), o_df).then_inc(od_turned, 1)

            def kept(i, j, t):
                if j in (SBV, DFV):
                    pe.wait_ge(kept_dve, 4 * i + 2 * (SBV, DFV).index(j) + t + 1)
                else:
                    pe.wait_ge(kept_act, 16 * i + 2 * BY_ACT.index(j) + t + 1)

            def mixer(i):
                for m in range(20):
                    j, half = m // 2, m % 2
                    begin(i, U_WIN + m)
                    for t in range(TT):
                        if m == 0:
                            inputs(i, 1, t)
                        elif half == 0 and j >= 2:
                            kept(i, j - 2, t)
                        mm = wide(slot(U_WIN + m), bank(WIN_BANK[j % 2][t]), x_hi, x_lo, 4 * half, t,
                                  half == 0, half == 1)
                        if half == 1 and t == 0:
                            mm.then_inc(win_done, 1)
                        if t == 0:
                            middle(i, m)
                    mm.then_inc(units_used, 1)
                    behind(i, m)
                for m in range(20, 24):
                    df, half = (m - 20) // 2, m % 2
                    begin(i, U_WIN + m)
                    if half == 0:
                        pe.wait_ge(od_split if df else os_split, i + 1)
                    for t in range(TT):
                        if m == 20:
                            kept(i, 8 + t, 1)
                        if df:
                            mm = deep(slot(U_WIN + m), Y_DF_PAIR[t], x_hi, x_lo, 2 * half, t, half == 0, half == 1)
                        else:
                            mm = deep(slot(U_WIN + m), Y_SB_PAIR[t], os_hi, os_lo, 2 * half, t, half == 0, half == 1)
                        if half == 1 and t == 0:
                            mm.then_inc(y_df_done if df else y_sb_done, 1)
                        if t == 0:
                            middle(i, m)
                    mm.then_inc(units_used, 1)
                    behind(i, m)
                turn_inputs(i, 2, lambda t: gates[:, 0, t, :], merged, 4 * i)
                for m in range(24, 28):
                    begin(i, U_WIN + m)
                    for t in range(TT):
                        if m == 24:
                            inputs(i, 2, t)
                        mm = deep(slot(U_WIN + m), OUT_PAIR[t], x_hi, x_lo, 2 * (m - 24), t, m == 24, m == 27)
                        if m == 27 and t == 0:
                            mm.then_inc(f_done, 1)
                    mm.then_inc(units_used, 1)

            def turn_p(i):
                pe.wait_ge(p_in, 16 * i + 16)
                for k in range(2):
                    for t in range(TT):
                        mm = pe.transpose(bank(P_BANK)[:, k * SEQ + t * P:k * SEQ + (t + 1) * P],
                                          p_nat[:, t, k * P:(k + 1) * P], ident[:, :])
                mm.then_inc(p_turned, 1)

            pe.wait_ge(h_loaded, 16 * TT)
            pe.wait_ge(cols_kept, 1)
            with pe.Fori(0, DEPTH) as i:
                turn_inputs(i, 0, lambda t: h[:, t, :], h_ready, 16 * i)
                ffn(i, 0, 0, U_FFN1, lambda: None)
                turn_inputs(i, 1, lambda t: h[:, t, :], h_ready, 16 * i + 4)
                pe.wait_ge(const_all, 1)
                mixer(i)
                turn_inputs(i, 3, lambda t: h[:, t, :], h_ready, 16 * i + 8)
                ffn(i, 1, 3, U_FFN2, lambda: turn_p(i))
                begin(i, U_PROJ)
                pe.wait_ge(p_split, i + 1)
                for t in range(TT):
                    mm = deep(slot(U_PROJ), E_PAIR[t], p_hi, p_lo, 0, t, True, True)
                    if t == 0:
                        mm.then_inc(e_done, 1)
                mm.then_inc(units_used, 1)
                turn_inputs(i, 4, lambda t: h[:, t, :], h_ready, 16 * i + 12)
                for s in range(4):
                    begin(i, U_GATE + s)
                    for t in range(TT):
                        if s == 0:
                            inputs(i, 4, t)
                        mm = deep(slot(U_GATE + s), GATE_PAIR[t], x_hi, x_lo, 2 * s, t, s == 0, s == 3)
                        if s == 3 and t == 0:
                            mm.then_inc(f_done, 1)
                    mm.then_inc(units_used, 1)


_NAMES = ["x", "p", "positions",
          "ffn1_pre_g", "ffn1_w_gu", "ffn1_w_down", "ffn1_post_g",
          "mix_pre_g", "w_in", "diff_lambda", "diff_subln_g", "w_branch_sb", "w_branch_diff", "w_out", "mix_post_g",
          "ffn2_pre_g", "ffn2_w_gu", "ffn2_w_down", "ffn2_post_g",
          "ple_pre_g", "w_ple_gate", "w_ple_proj", "ple_post_g"]


def kernel(**inputs):
    import concourse.bacc as bacc
    from concourse.bass_utils import run_bass_kernel_spmd

    nc = bacc.Bacc("TRN2", target_bir_lowering=False, num_devices=1)
    arrays, args = {}, {}
    for name in _NAMES:
        x = np.ascontiguousarray(inputs[name])
        arrays[f"in_{name}"] = x
        args[name] = nc.dram_tensor(f"in_{name}", x.shape, mybir.dt.from_np(x.dtype), kind="ExternalInput").ap()
    out = nc.dram_tensor("out_h", (1, SEQ, D), F32, kind="ExternalOutput").ap()
    trunk_kernel(nc, args, out)
    r = run_bass_kernel_spmd(nc, [arrays], core_ids=[0])
    return r.results[0]["out_h"]
```

```python
import math
from contextlib import ExitStack

import numpy as np

import concourse.bass as bass
from concourse import mybir

ALU = mybir.AluOpType
ACT = mybir.ActivationFunctionType
AX_X = mybir.AxisListType.X
F32 = mybir.dt.float32
F32R = mybir.dt.float32r
BF16 = mybir.dt.bfloat16
I32 = mybir.dt.int32

P = 128

DEPTH, SEQ, D = 2, 256, 1024
PLE, FF = 256, 2816
SB_HEADS, SB_D = 8, 64
DF_HEADS, DF_D = 4, 64
DF_V = 2 * DF_D
THETA, EPS, SUB_EPS = 10000.0, 1e-6, 1e-5
NEG = -1.0e30

TT = SEQ // P
KD = D // P
FC = 256
NC = FF // FC
W = 512
SLOTS = 3
UNIT = 2048

U_FFN = 3 * NC
U_FFN1 = 0
U_WIN = U_FFN1 + U_FFN
U_BSB = U_WIN + 20
U_BDF = U_BSB + 2
U_WOUT = U_BDF + 2
U_FFN2 = U_WOUT + 4
U_PROJ = U_FFN2 + U_FFN
U_GATE = U_PROJ + 1
UNITS = U_GATE + 4
assert UNITS % SLOTS == 0

SBQ, SBK, SBV, DFQ, DFK, DFV = range(6)
SB_Z0, SB_C0, SB_P0 = 6, 7, 8
DF_Z0, DF_T0, DF_P0 = 12, 13, 14
BY_ACT = (0, 1, 3, 4, 6, 7, 8, 9)
QK_ORDER = {SBQ: 0, SBK: 1, DFQ: 2, DFK: 3}

MEANS = 20
HTS = NC + 1
FACTOR = (0.5, 1.0, 0.5, 1.0)
LAM_INIT = [0.8 - 0.6 * math.exp(-0.3 * n) for n in range(DEPTH)]
ROUND = 1.5 * 2.0 ** 23
TWO_PI = [6.28125, round((2 * math.pi - 6.28125) * 2 ** 21) / 2 ** 21]
TWO_PI.append(2 * math.pi - sum(TWO_PI))
PI_IN = 3.1415925


def trunk_kernel(nc, a, out):
    with ExitStack() as ctx:
        def sb(name, shape, dt=F32):
            return ctx.enter_context(nc.sbuf_tensor(name, shape, dt))

        def sem(name):
            return ctx.enter_context(nc.semaphore(name))

        ps = ctx.enter_context(nc.psum_tensor("ps", [P, 8, W], F32))

        def bank(b):
            return ps[:, b, :]

        def pair(b):
            return ps[:, b:b + 2, :].rearrange("p b n -> p (b n)")

        raw = sb("raw", [P, SLOTS, UNIT])
        w_hi = sb("w_hi", [P, SLOTS, UNIT], F32R)
        w_lo = sb("w_lo", [P, SLOTS, UNIT], F32R)
        h = sb("h", [P, TT, D])
        x_hi = sb("x_hi", [P, KD, SEQ], F32R)
        x_lo = sb("x_lo", [P, KD, SEQ], F32R)
        glu = sb("glu", [P, TT, 2, FC])
        ht_hi = sb("ht_hi", [P, 2, SEQ], F32R)
        ht_lo = sb("ht_lo", [P, 2, SEQ], F32R)
        p_hi = sb("p_hi", [P, 2, SEQ], F32R)
        p_lo = sb("p_lo", [P, 2, SEQ], F32R)
        p_nat = sb("p_nat", [P, TT, PLE])
        tmp = sb("tmp", [P, TT, D])
        squares = sb("squares", [P, D])
        post_g = sb("post_g", [P, 2, D])
        g_rows = sb("g_rows", [P, P])
        g_cols = sb("g_cols", [P, 66])
        g_layer = sb("g_layer", [P, 33])
        lam_in = sb("lam_in", [P, DEPTH, 4, DF_D])
        lam_pr = sb("lam_pr", [P, DEPTH, 2, DF_D])
        lam_s = sb("lam_s", [P, DEPTH, 2])
        lam_e = sb("lam_e", [P, DEPTH, 2])
        neg_lams = sb("neg_lams", [P, DEPTH])
        neg_lam = sb("neg_lam", [P, 1])
        mean_pre = sb("mean_pre", [P, TT])
        ms_pre = sb("ms_pre", [P, TT])
        r_pre = sb("r_pre", [P, TT])
        r_query = sb("r_query", [P, TT])
        mean_post = sb("mean_post", [P, TT])
        ms_post = sb("ms_post", [P, TT])
        r_post = sb("r_post", [P, TT])
        neg_half = sb("neg_half", [P, TT])
        eps_norm = sb("eps_norm", [P, TT])
        eps_half = sb("eps_half", [P, TT])
        eps_sub = sb("eps_sub", [P, TT])
        q_factor = sb("q_factor", [P, TT])
        sbq_t = sb("sbq_t", [P, 4, SEQ])
        sbk_t = sb("sbk_t", [P, 4, SEQ])
        dfq_t = sb("dfq_t", [P, 4, SEQ])
        dfk_t = sb("dfk_t", [P, 4, SEQ])
        v_sb = sb("v_sb", [P, TT, W])
        v_df = sb("v_df", [P, TT, W])
        gates = sb("gates", [P, 2, TT, D])
        soft = sb("soft", [P, 2, 384])
        sp = sb("sp", [P, 2, 384])
        w_att = sb("w_att", [P, 2, 384])
        o_sb = sb("o_sb", [P, TT, W])
        os_hi = sb("os_hi", [P, 4, SEQ], F32R)
        os_lo = sb("os_lo", [P, 4, SEQ], F32R)
        prob = sb("prob", [P, 2, 384])
        neg_max = sb("neg_max", [P, 4])
        p_sum = sb("p_sum", [P, 4])
        p_rec = sb("p_rec", [P, 4])
        neg_lr = sb("neg_lr", [P, 2])
        mixed = sb("mixed", [P, 384])
        mixed_t = sb("mixed_t", [P, 384])
        mean_sub = sb("mean_sub", [P, TT])
        ms_sub = sb("ms_sub", [P, TT])
        r_sub = sb("r_sub", [P, TT])
        ident = sb("ident", [P, P])
        ident_b = sb("ident_b", [P, P], BF16)
        neg_tri = sb("neg_tri", [P, P])
        neg_one = sb("neg_one", [P, P])
        mask_sb = sb("mask_sb", [P, 384], BF16)
        mask_df = sb("mask_df", [P, 384], BF16)
        pos_i = sb("pos_i", [P, TT], I32)
        pos_f = sb("pos_f", [P, TT])
        freq = sb("freq", [P, 32])
        ang = sb("ang", [P, TT, 32])
        turns = sb("turns", [P, TT, 32])
        cos_in = sb("cos_in", [P, TT, 32])
        rope_c = sb("rope_c", [P, TT, 64])
        rope_s = sb("rope_s", [P, TT, 64])

        o_df = glu[:, :, :, :].rearrange("p t a n -> p t (a n)")
        rope_b = o_df
        slab = tmp[:, :, 0:W]
        slab_c = tmp[:, :, W:D]

        raw_in = [sem(f"raw_in{s}") for s in range(SLOTS)]
        hi_ready = sem("hi_ready")
        split_done = sem("split_done")
        units_used = sem("units_used")
        gu_done = sem("gu_done")
        silu_done = sem("silu_done")
        prod_done = sem("prod_done")
        ht_turned = sem("ht_turned")
        ht_high = sem("ht_high")
        ht_split = sem("ht_split")
        p_turned = sem("p_turned")
        p_high = sem("p_high")
        p_split = sem("p_split")
        x_turned = sem("x_turned")
        x_high = sem("x_high")
        x_split = sem("x_split")
        h_loaded = sem("h_loaded")
        h_ready = sem("h_ready")
        squared_pre = sem("squared_pre")
        mean_done = sem("mean_done")
        pre_scale = sem("pre_scale")
        query_scale = sem("query_scale")
        squared_post = sem("squared_post")
        post_scale = sem("post_scale")
        f_done = sem("f_done")
        scaled = sem("scaled")
        win_done = sem("win_done")
        kept_act = sem("kept_act")
        kept_dve = sem("kept_dve")
        rope_parts = sem("rope_parts")
        roped = sem("roped")
        qk_turned = sem("qk_turned")
        sb_turned = sem("sb_turned")
        df_turned = sem("df_turned")
        s_score = sem("s_score")
        s_abs = sem("s_abs")
        s_exp = sem("s_exp")
        s_log = sem("s_log")
        s_soft = sem("s_soft")
        s_later = sem("s_later")
        s_weight = sem("s_weight")
        s_value = sem("s_value")
        s_kept = sem("s_kept")
        os_turned = sem("os_turned")
        os_high = sem("os_high")
        os_split = sem("os_split")
        d_score = sem("d_score")
        d_max = sem("d_max")
        d_exp = sem("d_exp")
        d_rec = sem("d_rec")
        d_part = sem("d_part")
        d_mixed = sem("d_mixed")
        d_turned = sem("d_turned")
        d_kept = sem("d_kept")
        d_value = sem("d_value")
        d_square = sem("d_square")
        d_scale = sem("d_scale")
        d_normed = sem("d_normed")
        od_turned = sem("od_turned")
        od_high = sem("od_high")
        od_split = sem("od_split")
        y_sb_done = sem("y_sb_done")
        y_df_done = sem("y_df_done")
        gate_sig = sem("gate_sig")
        gated_sb = sem("gated_sb")
        gated_df = sem("gated_df")
        merged = sem("merged")
        e_done = sem("e_done")
        ple_sig = sem("ple_sig")
        ple_e = sem("ple_e")
        layer_g = sem("layer_g")
        post_in = [sem(f"post_in{s}") for s in range(2)]
        p_in = sem("p_in")
        g_in = sem("g_in")
        lam_loaded = sem("lam_loaded")
        pos_in = sem("pos_in")
        const_id = sem("const_id")
        const_all = sem("const_all")
        cols_turned = sem("cols_turned")
        cols_kept = sem("cols_kept")
        d_lam = sem("d_lam")
        setup_step = sem("setup_step")
        angles = sem("angles")
        sines = sem("sines")
        rope_ready = sem("rope_ready")
        lam_sum = sem("lam_sum")
        lam_exp = sem("lam_exp")
        blank = sem("blank")
        out_done = sem("out_done")

        X_BANK = ((0, 1, 2, 3), (6, 7, 0, 1), (4, 5, 2, 3), (2, 3, 0, 1), (0, 1, 2, 3))
        HT_BANK, P_BANK = 6, 7
        GU_BANK = (4, 5)
        WIN_BANK = ((4, 5), (2, 3))
        DOWN_PAIR = (0, 2)
        OUT_PAIR = (0, 6)
        Y_SB_PAIR = (4, 2)
        Y_DF_PAIR = (0, 6)
        E_PAIR = (4, 6)
        GATE_PAIR = (0, 2)
        QK_PAIR, OS_PAIR, OD_PAIR = 6, 0, 6
        SB_BANK = (0, 1)
        DF_BANK = (6, 7)
        SB_OUT = 384

        def slot(u):
            return u % SLOTS


        def wait_product(eng, done, count, i, u, t, c=0):
            if t == 0:
                eng.wait_ge(done, count)
            else:
                eng.wait_ge(units_used, UNITS * i + 3 * c + u + 1 + SLOTS)

        F_UNIT = (U_WIN - 1, U_FFN2 - 1, U_PROJ - 1, UNITS - 1)

        block = ctx.enter_context(nc.Block())

        @block.sync
        def _(sp_):
            for n, name in ((2, "ffn2_pre_g"), (3, "ple_pre_g")):
                sp_.dma_start(g_rows[2 * KD * n:2 * KD * (n + 1), :],
                              a[name].rearrange("l (k p) -> (l k) p", p=P)).then_inc(g_in, 16)
            sp_.dma_start(g_rows[64:66, :], a["diff_subln_g"]).then_inc(g_in, 16)

            def load(i, u, parts, c=0):
                sp_.wait_ge(split_done, UNITS * i + 3 * c + u + 1)
                for dst, src in parts:
                    sp_.dma_start(dst, src).then_inc(raw_in[slot(u)], 16)

            def load_gu(i, u, w, step, s, c=0):
                dst = raw[:, slot(u), :].rearrange("p (k g n) -> p k g n", k=4, g=2)
                rows = w[bass.ds(i, 1), s * 4 * P:(s + 1) * 4 * P, :].rearrange("o (k p) n -> p (o k) n", p=P)
                load(i, u, [(dst[:, :, g, :], rows[:, :, bass.ds(step * FC + g * FF, FC)]) for g in range(2)], c)

            def load_deep(i, u, w, row, c=0):
                dst = raw[:, slot(u), :].rearrange("p (k n) -> p k n", k=2)
                load(i, u, [(dst[:, k, :], w[bass.ds(i, 1), bass.ds(row + k * P, P), :].rearrange("o p n -> p (o n)"))
                            for k in range(2)], c)

            def load_ffn(i, u0, w_gu, w_down):
                for s in range(2):
                    load_gu(i, u0 + s, w_gu, 0, s)
                with sp_.Fori(1, NC) as c:
                    load_gu(i, u0 - 1, w_gu, c, 0, c)
                    load_gu(i, u0, w_gu, c, 1, c)
                    load_deep(i, u0 + 1, w_down, c * FC - FC, c)
                load_deep(i, u0 + U_FFN - 1, w_down, (NC - 1) * FC)

            with sp_.Fori(0, DEPTH) as i:
                load_ffn(i, U_FFN1, a["ffn1_w_gu"], a["ffn1_w_down"])
                for m in range(20):
                    dst = raw[:, slot(U_WIN + m), :].rearrange("p (k n) -> p k n", k=4)
                    r0, c0 = (m % 2) * 4 * P, (m // 2) * W
                    src = a["w_in"][bass.ds(i, 1), r0:r0 + 4 * P, c0:c0 + W].rearrange("o (k p) n -> p (o k) n", p=P)
                    load(i, U_WIN + m, [(dst[:, k:k + 2, :], src[:, k:k + 2, :]) for k in (0, 2)])
                for s in range(2):
                    load_deep(i, U_BSB + s, a["w_branch_sb"], 2 * P * s)
                for s in range(2):
                    load_deep(i, U_BDF + s, a["w_branch_diff"], 2 * P * s)
                for s in range(4):
                    load_deep(i, U_WOUT + s, a["w_out"], 2 * P * s)
                load_ffn(i, U_FFN2, a["ffn2_w_gu"], a["ffn2_w_down"])
                load_deep(i, U_PROJ, a["w_ple_proj"], 0)
                for s in range(4):
                    load_deep(i, U_GATE + s, a["w_ple_gate"], 2 * P * s)
            for t in range(TT):
                for n in range(2):
                    sp_.wait_ge(h_ready, 16 * DEPTH + 2 * t + n + 1)
                    sp_.dma_start(out[0, t * P:(t + 1) * P, n * W:(n + 1) * W],
                                  h[:, t, n * W:(n + 1) * W]).then_inc(out_done, 16)
            sp_.wait_ge(out_done, 16 * 2 * TT)

        @block.gpsimd
        def _(pool):
            pool.memset(ident[:, :], 0.0).then_inc(blank, 1)
            pool.wait_ge(blank, 1)
            pool.affine_select(out=ident[:, :], in_=ident[:, :], compare_op=ALU.not_equal, fill=1.0,
                               base=0, pattern=[[-1, P]], channel_multiplier=1).then_inc(const_id, 1)
            for t in range(TT):
                pool.dma_start(pos_i[:, t:t + 1], a["positions"][0, t * P:(t + 1) * P].rearrange(
                    "(p o) -> p o", o=1)).then_inc(pos_in, 16)
            pool.dma_start(lam_in[:, :, :, :].rearrange("p l f d -> p (l f d)"),
                           a["diff_lambda"].rearrange("l f d -> (l f d)").partition_broadcast(P)
                           ).then_inc(lam_loaded, 16)
            pool.memset(neg_half[:, :], -0.5)
            pool.memset(eps_norm[:, :], EPS)
            pool.memset(eps_half[:, :], EPS / 0.25)
            pool.memset(eps_sub[:, :], SUB_EPS)
            pool.memset(q_factor[:, :], SB_D ** -0.5)
            pool.memset(ident_b[:, :], 0.0)
            pool.memset(neg_tri[:, :], -1.0)
            pool.memset(neg_one[:, :], -1.0)
            pool.memset(mask_sb[:, :], 0.0)
            pool.memset(mask_df[:, :], 0.0).then_inc(blank, 1)
            pool.wait_ge(blank, 2)
            pool.affine_select(out=ident_b[:, :], in_=ident_b[:, :], compare_op=ALU.not_equal, fill=1.0,
                               base=0, pattern=[[-1, P]], channel_multiplier=1)
            pool.affine_select(out=neg_tri[:, :], in_=neg_tri[:, :], compare_op=ALU.is_ge, fill=0.0,
                               base=0, pattern=[[-1, P]], channel_multiplier=1)
            for c in (0, 256):
                pool.affine_select(out=mask_sb[:, c:c + P], in_=mask_sb[:, c:c + P], compare_op=ALU.is_gt,
                                   fill=NEG, base=0, pattern=[[1, P]], channel_multiplier=-1)
                last = pool.affine_select(out=mask_df[:, c:c + P], in_=mask_df[:, c:c + P],
                                          compare_op=ALU.is_ge, fill=NEG, base=0, pattern=[[-1, P]],
                                          channel_multiplier=1)
            last.then_inc(const_all, 1)

            def rsqrt_mean(i, order, mean, ms, r, eps):
                pool.tensor_tensor(ms, mean, eps[:, 0:ms.shape[1]], ALU.add).then_inc(mean_done, 1)
                pool.wait_ge(mean_done, MEANS * i + order + 1)
                return pool.tensor_tensor(r, ms, neg_half[:, 0:ms.shape[1]], ALU.pow)

            def pre_norm(i, n, order):
                for t in range(TT):
                    pool.wait_ge(squared_pre, 8 * i + 2 * n + t + 1)
                    rsqrt_mean(i, order + t, mean_pre[:, t:t + 1], ms_pre[:, t:t + 1], r_pre[:, t:t + 1],
                               eps_norm).then_inc(pre_scale, 1)

            def post_norm(i, n, order):
                for t in range(TT):
                    pool.wait_ge(squared_post, 8 * i + 2 * n + t + 1)
                    rsqrt_mean(i, order + t, mean_post[:, t:t + 1], ms_post[:, t:t + 1], r_post[:, t:t + 1],
                               eps_half if FACTOR[n] == 0.5 else eps_norm).then_inc(post_scale, 1)

            def rope(i, k):
                for t in range(TT):
                    pool.wait_ge(kept_act, 16 * i + 2 * (2 + k) + t + 1)
                    if k or t:
                        pool.wait_ge(roped, 4 * i + 2 * k + t)
                    x = slab[:, t, :].rearrange("p (g c) -> p g c", c=64)
                    y = rope_b[:, t, :].rearrange("p (g c) -> p g c", c=64)
                    pool.tensor_tensor(slab_c[:, t, :].rearrange("p (g c) -> p g c", c=64), x,
                                       rope_c[:, t:t + 1, :].to_broadcast([P, 8, 64]), ALU.mult)
                    pool.tensor_tensor(y[:, :, 0:32], x[:, :, 32:64],
                                       rope_s[:, t:t + 1, 0:32].to_broadcast([P, 8, 32]), ALU.mult)
                    pool.tensor_tensor(y[:, :, 32:64], x[:, :, 0:32],
                                       rope_s[:, t:t + 1, 32:64].to_broadcast([P, 8, 32]), ALU.mult
                                       ).then_inc(rope_parts, 1)
                    pool.wait_ge(rope_parts, 4 * i + 2 * k + t + 1)
                    pool.tensor_tensor(slab[:, t, :], slab_c[:, t, :], rope_b[:, t, :], ALU.add).then_inc(roped, 1)

            pool.wait_ge(rope_ready, 1)
            with pool.Fori(0, DEPTH) as i:
                pre_norm(i, 0, 0)
                post_norm(i, 0, 2)
                pre_norm(i, 1, 4)
                pool.wait_ge(pre_scale, 8 * i + 4)
                pool.tensor_tensor(r_query[:, :], r_pre[:, :], q_factor[:, :], ALU.mult).then_inc(query_scale, 1)
                rope(i, 0)
                rope(i, 1)
                for hd in range(DF_HEADS):
                    pool.wait_ge(d_square, 4 * i + hd + 1)
                    rsqrt_mean(i, 6 + hd, mean_sub[:, :], ms_sub[:, :], r_sub[:, :], eps_sub
                               ).then_inc(d_scale, 1)
                post_norm(i, 1, 10)
                pre_norm(i, 2, 12)
                post_norm(i, 2, 14)
                pre_norm(i, 3, 16)
                post_norm(i, 3, 18)

        @block.scalar
        def _(act):
            for n, name in ((0, "ffn1_pre_g"), (1, "mix_pre_g")):
                act.dma_start(g_rows[2 * KD * n:2 * KD * (n + 1), :],
                              a[name].rearrange("l (k p) -> (l k) p", p=P)).then_inc(g_in, 16)
            for t in range(TT):
                act.dma_start(h[:, t, :], a["x"][0, t * P:(t + 1) * P, :]).then_inc(h_loaded, 16)
            act.wait_ge(angles, 1)
            act.activation(rope_s[:, :, 32:64], ang[:, :, :], ACT.Sin)
            act.activation(rope_c[:, :, 0:32], cos_in[:, :, :], ACT.Sin).then_inc(sines, 1)
            act.wait_ge(lam_sum, 1)
            act.activation(lam_e[:, :, :], lam_s[:, :, :], ACT.Exp).then_inc(lam_exp, 1)

            def high(i, u, gain=None, ks=4, c=0, halves=(0, 1)):
                s = slot(u)
                for half in halves:
                    if half == 0:
                        act.wait_ge(raw_in[s], 32 * (UNITS // 3) * i + 32 * c + 32 * (u // 3) + 32)
                        act.wait_ge(units_used, UNITS * i + 3 * c + u + 1)
                    pieces = 2 if ks == 4 and gain is not None else 1
                    n = UNIT // 2 // pieces
                    for k in range(pieces * half, pieces * half + pieces):
                        part = slice(k * n, (k + 1) * n)
                        if gain is None:
                            last = act.activation(w_hi[:, s, part], raw[:, s, part], ACT.Copy)
                        else:
                            g = gain + (k if ks > 1 else 0)
                            last = act.activation(w_hi[:, s, part], raw[:, s, part], ACT.Copy,
                                                  scale=g_layer[:, g:g + 1])
                    last.then_inc(hi_ready, 1)

            def high_inputs(i, q, t):
                for n in range(2):
                    idx = 2 * t + n
                    act.wait_ge(x_turned, 20 * i + 4 * q + idx + 1)
                    act.activation(x_hi[:, 4 * n:4 * n + 4, t * P:(t + 1) * P],
                                   bank(X_BANK[q][idx]).rearrange("p (k n) -> p k n", k=4),
                                   ACT.Copy).then_inc(x_high, 1)

            def square_pre(i, n, t):
                act.wait_ge(h_ready, 16 * i + 4 * n + 2 * t + 2)
                act.activation(squares[:, :], h[:, t, :], ACT.Square, scale=D ** -0.5,
                               accum_out=mean_pre[:, t:t + 1]).then_inc(squared_pre, 1)
                act.wait_ge(squared_pre, 8 * i + 2 * n + t + 1)

            def square_post(i, n, src, t):
                if n < 3:
                    wait_product(act, f_done, 4 * i + n + 1, i, F_UNIT[n], t)
                else:
                    act.wait_ge(ple_e, 2 * i + t + 1)
                act.activation(squares[:, :], src(t), ACT.Square, scale=D ** -0.5 / FACTOR[n],
                               accum_out=mean_post[:, t:t + 1]).then_inc(squared_post, 1)
                act.wait_ge(squared_post, 8 * i + 2 * n + t + 1)

            def boundary(i, n, q, src, next_unit):
                square_post(i, n, src, 0)
                next_unit(0)
                high_inputs(i, q, 0)
                next_unit(1)
                square_post(i, n, src, 1)
                square_pre(i, n + 1, 0)
                high_inputs(i, q, 1)
                square_pre(i, n + 1, 1)

            def high_ht(i, f, c):
                act.wait_ge(ht_turned, 2 * HTS * i + HTS * f + c + 1)
                act.activation(ht_hi[:, :, :], bank(HT_BANK).rearrange("p (k n) -> p k n", k=2),
                               ACT.Copy).then_inc(ht_high, 1)

            def high_last_ht(i, f, t):
                toks = slice(t * P, (t + 1) * P)
                act.wait_ge(ht_turned, 2 * HTS * i + HTS * f + NC + t)
                act.activation(x_hi[:, 0:2, toks], bank(HT_BANK).rearrange("p (k n) -> p k n", k=2)[:, :, toks],
                               ACT.Copy).then_inc(ht_high, 1)

            def silu(i, f, step, u, t, c=0):
                wait_product(act, gu_done, 2 * NC * i + NC * f + step + 1, i, u, t, c)
                act.activation(glu[:, t, 0, :], bank(GU_BANK[t])[:, 0:FC], ACT.Silu,
                               scale=r_pre[:, t:t + 1]).then_inc(silu_done, 1)

            def ffn(i, f, u0, g0, next_unit):
                high(i, u0 + 2, g0)
                act.wait_ge(pre_scale, 8 * i + 4 * f + 1)
                silu(i, f, 0, u0 + 1, 0)
                high(i, u0 + 3, g0 + 4)
                act.wait_ge(pre_scale, 8 * i + 4 * f + 2)
                silu(i, f, 0, u0 + 1, 1)
                with act.Fori(1, NC - 1) as c:
                    high(i, u0 + 1, c=c)
                    high_ht(i, f, c - 1)
                    high(i, u0 + 2, g0, c=c)
                    for t in range(TT):
                        silu(i, f, c, u0, t, c)
                    high(i, u0 + 3, g0 + 4, c=c)
                high(i, u0 + 3 * NC - 2)
                high_ht(i, f, NC - 2)
                high(i, u0 + 3 * NC - 1)
                for t in range(TT):
                    silu(i, f, NC - 1, u0 + 3 * NC - 3, t)
                high_last_ht(i, f, 0)
                next_unit()
                high_last_ht(i, f, 1)

            def stick_weights(i, m):
                hd = m - SB_C0
                if 0 <= hd < SB_HEADS:
                    act.wait_ge(s_later, SB_HEADS * i + hd + 1)
                    act.activation(w_att[:, hd % 2, :], bank(SB_BANK[hd % 2])[:, 0:384], ACT.Exp
                                   ).then_inc(s_weight, 1)

            def stick_softplus(i, m):
                hd = m - SB_Z0
                if 0 <= hd < SB_HEADS:
                    act.wait_ge(s_score, SB_HEADS * i + hd + 1)
                    act.activation(soft[:, hd % 2, :], bank(SB_BANK[hd % 2])[:, 0:384], ACT.Abs).then_inc(s_abs, 1)
                    act.wait_ge(s_abs, SB_HEADS * i + hd + 1)
                    act.activation(soft[:, hd % 2, :], soft[:, hd % 2, :], ACT.Exp, scale=-1.0).then_inc(s_exp, 1)
                    act.wait_ge(s_exp, SB_HEADS * i + hd + 1)
                    act.activation(soft[:, hd % 2, :], soft[:, hd % 2, :], ACT.Ln, bias=1.0).then_inc(s_log, 1)

            def diff_after(i, m):
                if m >= DF_Z0 and (m - DF_Z0) % 2 == 0 and (m - DF_Z0) // 2 < DF_HEADS:
                    hd = (m - DF_Z0) // 2
                    act.wait_ge(d_max, DF_HEADS * i + hd + 1)
                    for c in range(2):
                        for t, (lo, hi) in enumerate(((0, P), (P, 384))):
                            last = act.activation(prob[:, c, lo:hi], bank(DF_BANK[c])[:, lo:hi], ACT.Exp,
                                                  bias=neg_max[:, 2 * c + t:2 * c + t + 1],
                                                  accum_out=p_sum[:, 2 * c + t:2 * c + t + 1])
                    last.then_inc(d_exp, 1)
                if m >= DF_T0 and (m - DF_T0) % 2 == 0 and (m - DF_T0) // 2 < DF_HEADS:
                    hd = (m - DF_T0) // 2
                    act.wait_ge(d_turned, DF_HEADS * i + hd + 1)
                    act.activation(mixed_t[:, :], bank(DF_BANK[0])[:, 0:384], ACT.Copy).then_inc(d_kept, 1)

            def diff_mid(i, m):
                if m >= DF_P0 and (m - DF_P0) % 2 == 0 and (m - DF_P0) // 2 < DF_HEADS:
                    hd = (m - DF_P0) // 2
                    act.wait_ge(d_value, DF_HEADS * i + hd + 1)
                    if hd:
                        act.wait_ge(d_square, DF_HEADS * i + hd)
                    for t in range(TT):
                        last = act.activation(squares[:, t * P:(t + 1) * P], bank(DF_BANK[1])[:, t * P:(t + 1) * P],
                                              ACT.Square, scale=DF_V ** -0.5, accum_out=mean_sub[:, t:t + 1])
                    last.then_inc(d_square, 1)

            def keep(i, m):
                j = m // 2
                if m % 2 == 0 or m >= 20 or j in (SBV, DFV):
                    return
                if j == SBQ:
                    act.wait_ge(query_scale, i + 1)
                for t in range(TT):
                    wait_product(act, win_done, 10 * i + j + 1, i, U_WIN + m, t)
                    src = bank(WIN_BANK[j % 2][t])
                    if j < 6:
                        if t == 0 and QK_ORDER[j]:
                            act.wait_ge(qk_turned, 4 * i + QK_ORDER[j])
                        r = r_query if j in (SBQ, DFQ) else r_pre
                        act.activation(slab[:, t, :], src, ACT.Copy, scale=r[:, t:t + 1]).then_inc(kept_act, 1)
                    else:
                        g, n = (j - 6) // 2, (j - 6) % 2
                        act.activation(gates[:, g, t, n * W:(n + 1) * W], src, ACT.Copy,
                                       scale=r_pre[:, t:t + 1]).then_inc(kept_act, 1)

            def mixer(i):
                for m in range(23):
                    if m < 18:
                        high(i, U_WIN + m + 2, 8 + 4 * (m % 2))
                    elif m in (20, 21):
                        high(i, U_WIN + m + 2, 32, ks=1)
                    else:
                        high(i, U_WIN + m + 2)
                    diff_mid(i, m)
                    if m == 20:
                        act.wait_ge(kept_act, 16 * i + 16)
                        for g in range(2):
                            for t in range(TT):
                                act.activation(gates[:, g, t, :], gates[:, g, t, :], ACT.Sigmoid).then_inc(gate_sig, 1)
                    keep(i, m)
                    stick_weights(i, m)
                    diff_after(i, m)
                    if m in (2, 4):
                        k = (m - 2) // 2
                        act.wait_ge(qk_turned, 4 * i + k + 1)
                        act.activation((sbq_t, sbk_t)[k][:, :, :].rearrange("p k n -> p (k n)"), pair(QK_PAIR),
                                       ACT.Copy).then_inc(sb_turned, 1)
                    if m == 16:
                        act.wait_ge(os_turned, i + 1)
                        act.activation(os_hi[:, :, :].rearrange("p k n -> p (k n)"), pair(OS_PAIR),
                                       ACT.Copy).then_inc(os_high, 1)
                    if m == 20:
                        act.wait_ge(od_turned, i + 1)
                        act.activation(x_hi[:, 0:4, :].rearrange("p k n -> p (k n)"), pair(OD_PAIR),
                                       ACT.Copy).then_inc(od_high, 1)
                    stick_softplus(i, m)
                high(i, U_WIN + 25, halves=(0,))
                high_inputs(i, 2, 0)
                high(i, U_WIN + 25, halves=(1,))
                high_inputs(i, 2, 1)
                high(i, U_WIN + 26)
                high(i, U_WIN + 27)
                high(i, U_FFN2, 16)

            def load_post(i, name, n, s):
                act.wait_ge(h_ready, 16 * i + 4 * n + 4)
                act.dma_start(post_g[:, s, :],
                              a[name][bass.ds(i, 1), :].rearrange("o n -> (o n)").partition_broadcast(P)
                              ).then_inc(post_in[s], 16)

            with act.Fori(0, DEPTH) as i:
                act.wait_ge(layer_g, i + 1)
                high(i, 0, 0)
                high_inputs(i, 0, 0)
                high(i, 1, 4)
                high_inputs(i, 0, 1)
                square_pre(i, 0, 0)
                square_pre(i, 0, 1)
                load_post(i, "ffn1_post_g", 0, 0)
                load_post(i, "mix_post_g", 0, 1)
                act.dma_start(p_nat[:, :, :], a["p"][bass.ds(i, 1), 0, :, :].rearrange(
                    "o (t p) n -> p (o t) n", p=P)).then_inc(p_in, 16)
                ffn(i, 0, U_FFN1, 0, lambda: high(i, U_WIN, 8))
                boundary(i, 0, 1, lambda t: pair(DOWN_PAIR[t]), lambda n: high(i, U_WIN + 1, 12, halves=(n,)))

                load_post(i, "ffn2_post_g", 1, 0)
                act.preload_act_table_set("natural_log_exp_and_others")
                act.wait_ge(pre_scale, 8 * i + 4)
                mixer(i)
                boundary(i, 1, 3, lambda t: pair(OUT_PAIR[t]), lambda n: high(i, U_FFN2 + 1, 20, halves=(n,)))

                load_post(i, "ple_post_g", 2, 1)
                ffn(i, 1, U_FFN2, 16, lambda: high(i, U_PROJ))
                act.wait_ge(p_turned, i + 1)
                act.activation(p_hi[:, :, :], bank(P_BANK).rearrange("p (k n) -> p k n", k=2),
                               ACT.Copy).then_inc(p_high, 1)
                boundary(i, 2, 4, lambda t: pair(DOWN_PAIR[t]),
                         lambda n: high(i, U_GATE, 24, ks=2, halves=(n,)))

                for s in range(1, 4):
                    high(i, U_GATE + s, 24 + 2 * s, ks=2)
                for t in range(TT):
                    act.wait_ge(pre_scale, 8 * i + 7 + t)
                    wait_product(act, f_done, 4 * i + 4, i, F_UNIT[3], t)
                    act.activation(gates[:, 0, t, :], pair(GATE_PAIR[t]), ACT.Sigmoid,
                                   scale=r_pre[:, t:t + 1]).then_inc(ple_sig, 1)
                    square_post(i, 3, lambda t: gates[:, 1, t, :], t)

        @block.vector
        def _(dve):
            dve.memset(freq[:, 0:1], 1.0).then_inc(split_done, SLOTS)
            dve.memset(freq[:, 1:2], float(np.float32(THETA ** (-1 / 32)))).then_inc(h_ready, 4)
            for j in range(2, 32):
                last = dve.memset(freq[:, j:j + 1], float(np.float32(THETA ** (-j / 32))))

            linked = [0]

            def link(ins):
                linked[0] += 1
                ins.then_inc(setup_step, 1)
                dve.wait_ge(setup_step, linked[0])

            link(last)
            dve.wait_ge(cols_turned, 1)
            dve.tensor_copy(g_cols[:, 0:64], bank(0)[:, 0:64])
            for n in range(DEPTH):
                last = dve.tensor_scalar(g_cols[:, 64 + n:65 + n], bank(0)[:, 64 + n:65 + n], 1.0 - LAM_INIT[n],
                                         None, ALU.mult)
            last.then_inc(cols_kept, 1)
            dve.wait_ge(cols_kept, 1)
            dve.wait_ge(pos_in, 16 * TT)
            link(dve.tensor_copy(pos_f[:, :], pos_i[:, :]))
            for t in range(TT):
                last = dve.tensor_scalar(ang[:, t, :], freq[:, :], pos_f[:, t:t + 1], None, ALU.mult)
            link(last)
            link(dve.tensor_scalar(turns[:, :, :], ang[:, :, :], 1 / (2 * math.pi), ROUND, ALU.mult, ALU.add))
            link(dve.tensor_scalar(turns[:, :, :], turns[:, :, :], -ROUND, None, ALU.add))
            for part in TWO_PI:
                link(dve.scalar_tensor_tensor(out=ang[:, :, :], in0=turns[:, :, :], scalar=-part, in1=ang[:, :, :],
                                              op0=ALU.mult, op1=ALU.add))
            link(dve.tensor_scalar(ang[:, :, :], ang[:, :, :], PI_IN, -PI_IN, ALU.min, ALU.max))
            link(dve.scalar_tensor_tensor(out=cos_in[:, :, :], in0=ang[:, :, :], scalar=-1.0, in1=ang[:, :, :],
                                          op0=ALU.mult, op1=ALU.min))
            dve.tensor_scalar(cos_in[:, :, :], cos_in[:, :, :], math.pi / 2, None, ALU.add).then_inc(angles, 1)
            dve.wait_ge(lam_loaded, 16)
            link(dve.tensor_tensor(lam_pr[:, :, :, :], lam_in[:, :, 0::2, :], lam_in[:, :, 1::2, :], ALU.mult))
            dve.tensor_reduce(lam_s[:, :, :], lam_pr[:, :, :, :], AX_X, ALU.add).then_inc(lam_sum, 1)
            dve.wait_ge(sines, 1)
            dve.tensor_scalar(rope_s[:, :, 0:32], rope_s[:, :, 32:64], -1.0, None, ALU.mult)
            dve.tensor_copy(rope_c[:, :, 32:64], rope_c[:, :, 0:32]).then_inc(rope_ready, 1)
            dve.wait_ge(lam_exp, 1)
            link(dve.tensor_tensor(neg_lams[:, :], lam_e[:, :, 1], lam_e[:, :, 0], ALU.subtract))
            for n in range(DEPTH):
                last = dve.tensor_scalar(neg_lams[:, n:n + 1], neg_lams[:, n:n + 1], -LAM_INIT[n], None, ALU.add)
            link(last)

            def low(i, u, gain=None, ks=4, c=0, halves=(0, 1)):
                s = slot(u)
                whi = w_hi[:, s, :].bitcast(F32)
                for half in halves:
                    dve.wait_ge(hi_ready, 2 * UNITS * i + 6 * c + 2 * u + half + 1)
                    pieces = 2 if ks == 4 and gain is not None else 1
                    n = UNIT // 2 // pieces
                    for k in range(pieces * half, pieces * half + pieces):
                        part = slice(k * n, (k + 1) * n)
                        if gain is None:
                            last = dve.tensor_tensor(w_lo[:, s, part], raw[:, s, part], whi[:, part], ALU.subtract)
                        else:
                            g = gain + (k if ks > 1 else 0)
                            last = dve.scalar_tensor_tensor(out=w_lo[:, s, part], in0=raw[:, s, part],
                                                            scalar=g_layer[:, g:g + 1], in1=whi[:, part],
                                                            op0=ALU.mult, op1=ALU.subtract)
                    if half:
                        last.then_inc(split_done, 1)

            def low_inputs(i, q, t):
                for n in range(2):
                    idx = 2 * t + n
                    dve.wait_ge(x_high, 20 * i + 4 * q + idx + 1)
                    part = (slice(None), slice(4 * n, 4 * n + 4), slice(t * P, (t + 1) * P))
                    dve.tensor_tensor(x_lo[part], bank(X_BANK[q][idx]).rearrange("p (k n) -> p k n", k=4),
                                      x_hi[part].bitcast(F32), ALU.subtract).then_inc(x_split, 1)

            def low_ht(i, f, c):
                dve.wait_ge(ht_high, 2 * HTS * i + HTS * f + c + 1)
                dve.tensor_tensor(ht_lo[:, :, :], bank(HT_BANK).rearrange("p (k n) -> p k n", k=2),
                                  ht_hi[:, :, :].bitcast(F32), ALU.subtract).then_inc(ht_split, 1)

            def low_last_ht(i, f, t):
                toks = slice(t * P, (t + 1) * P)
                dve.wait_ge(ht_high, 2 * HTS * i + HTS * f + NC + t)
                dve.tensor_tensor(x_lo[:, 0:2, toks], bank(HT_BANK).rearrange("p (k n) -> p k n", k=2)[:, :, toks],
                                  x_hi[:, 0:2, toks].bitcast(F32), ALU.subtract).then_inc(ht_split, 1)

            def product(i, f, c, t):
                dve.wait_ge(silu_done, 4 * NC * i + 2 * NC * f + 2 * c + t + 1)
                dve.scalar_tensor_tensor(out=glu[:, t, 1, :], in0=bank(GU_BANK[t])[:, FC:2 * FC],
                                         scalar=r_pre[:, t:t + 1], in1=glu[:, t, 0, :],
                                         op0=ALU.mult, op1=ALU.mult).then_inc(prod_done, 1)

            def ffn(i, f, u0, g0, next_unit):
                low(i, u0 + 2, g0)
                product(i, f, 0, 0)
                low(i, u0 + 3, g0 + 4)
                product(i, f, 0, 1)
                with dve.Fori(1, NC - 1) as c:
                    low(i, u0 + 1, c=c)
                    low_ht(i, f, c - 1)
                    low(i, u0 + 2, g0, c=c)
                    for t in range(TT):
                        product(i, f, c, t)
                    low(i, u0 + 3, g0 + 4, c=c)
                low(i, u0 + 3 * NC - 2)
                low_ht(i, f, NC - 2)
                low(i, u0 + 3 * NC - 1)
                for t in range(TT):
                    product(i, f, NC - 1, t)
                low_last_ht(i, f, 0)
                next_unit()
                low_last_ht(i, f, 1)

            HALVES = [slice(0, W), slice(W, D)]

            def gained(i, n, src, t, k):
                dve.tensor_tensor(tmp[:, t, HALVES[k]], src[:, HALVES[k]], post_g[:, n % 2, HALVES[k]],
                                  ALU.mult).then_inc(scaled, 1)

            def wait_gained(i, n, t):
                dve.wait_ge(post_in[n % 2], 32 * i + 16 * (n // 2) + 16)
                if n < 3:
                    dve.wait_ge(squared_post, 8 * i + 2 * n + t + 1)
                else:
                    dve.wait_ge(ple_e, 2 * i + t + 1)

            def update_h(i, n, t, k):
                if k == 0:
                    dve.wait_ge(post_scale, 8 * i + 2 * n + t + 1)
                dve.wait_ge(scaled, 16 * i + 4 * n + 2 * t + k + 1)
                dve.scalar_tensor_tensor(out=h[:, t, HALVES[k]], in0=tmp[:, t, HALVES[k]],
                                         scalar=r_post[:, t:t + 1], in1=h[:, t, HALVES[k]],
                                         op0=ALU.mult, op1=ALU.add).then_inc(h_ready, 1)

            def boundary(i, n, q, pairs, next_unit):
                wait_gained(i, n, 0)
                for k in range(2):
                    gained(i, n, pair(pairs[0]), 0, k)
                    update_h(i, n, 0, k)
                next_unit(0)
                low_inputs(i, q, 0)
                wait_gained(i, n, 1)
                gained(i, n, pair(pairs[1]), 1, 0)
                next_unit(1)
                update_h(i, n, 1, 0)
                gained(i, n, pair(pairs[1]), 1, 1)
                update_h(i, n, 1, 1)
                low_inputs(i, q, 1)

            def merge(i, t):
                wait_product(dve, y_df_done, i + 1, i, U_BDF + 1, t)
                for n in range(2):
                    s = slice(n * W, (n + 1) * W)
                    dve.tensor_tensor(gates[:, 1, t, s], bank(Y_DF_PAIR[t] + n), gates[:, 1, t, s],
                                      ALU.mult).then_inc(gated_df, 1)
                for n in range(2):
                    s = slice(n * W, (n + 1) * W)
                    dve.wait_ge(gated_sb, 2 * i + t + 1)
                    dve.wait_ge(gated_df, 4 * i + 2 * t + n + 1)
                    dve.tensor_tensor(gates[:, 0, t, s], gates[:, 0, t, s], gates[:, 1, t, s],
                                      ALU.add).then_inc(merged, 1)

            def mixer(i):
                for m in range(23):
                    hd = m - SB_P0
                    if 0 <= hd < SB_HEADS:
                        dve.wait_ge(s_value, SB_HEADS * i + hd + 1)
                        dve.tensor_copy(o_sb[:, :, hd * SB_D:(hd + 1) * SB_D],
                                        bank(SB_BANK[hd % 2])[:, SB_OUT:W].rearrange("p (t n) -> p t n", t=TT)
                                        ).then_inc(s_kept, 1)
                    if m >= DF_P0 and (m - DF_P0) % 2 == 0 and (m - DF_P0) // 2 < DF_HEADS:
                        hd = (m - DF_P0) // 2
                        dve.wait_ge(d_scale, DF_HEADS * i + hd + 1)
                        for t in range(TT):
                            last = dve.tensor_scalar(o_df[:, t, hd * DF_V:(hd + 1) * DF_V],
                                                     bank(DF_BANK[1])[:, t * P:(t + 1) * P], r_sub[:, t:t + 1],
                                                     None, ALU.mult)
                        last.then_inc(d_normed, 1)
                    if m < 18:
                        low(i, U_WIN + m + 2, 8 + 4 * (m % 2))
                    elif m in (20, 21):
                        low(i, U_WIN + m + 2, 32, ks=1)
                    else:
                        low(i, U_WIN + m + 2)
                    if m in (5, 11):
                        j = m // 2
                        for t in range(TT):
                            wait_product(dve, win_done, 10 * i + j + 1, i, U_WIN + m, t)
                            dve.tensor_scalar((v_sb, v_df)[j == DFV][:, t, :], bank(WIN_BANK[j % 2][t]),
                                              r_pre[:, t:t + 1], None, ALU.mult).then_inc(kept_dve, 1)
                    diff = m >= DF_Z0 and (m - DF_Z0) % 2 == 0 and (m - DF_Z0) // 2 < DF_HEADS
                    if diff:
                        hd = (m - DF_Z0) // 2
                        dve.wait_ge(d_score, DF_HEADS * i + hd + 1)
                        for c in range(2):
                            for t, (lo, hi) in enumerate(((0, P), (P, 384))):
                                last = dve.tensor_reduce(neg_max[:, 2 * c + t:2 * c + t + 1],
                                                         bank(DF_BANK[c])[:, lo:hi], AX_X, ALU.max, negate=True)
                        last.then_inc(d_max, 1)
                    if m in (9, 11):
                        k = (m - 9) // 2
                        dve.wait_ge(qk_turned, 4 * i + 2 + k + 1)
                        dve.tensor_copy((dfq_t, dfk_t)[k][:, :, :].rearrange("p k n -> p (k n)"),
                                        pair(QK_PAIR)).then_inc(df_turned, 1)
                    hd = m - SB_Z0
                    if 0 <= hd < SB_HEADS:
                        dve.wait_ge(s_log, SB_HEADS * i + hd + 1)
                        dve.scalar_tensor_tensor(out=sp[:, hd % 2, :], in0=bank(SB_BANK[hd % 2])[:, 0:384], scalar=0.0,
                                                 in1=soft[:, hd % 2, :], op0=ALU.max, op1=ALU.add
                                                 ).then_inc(s_soft, 1)
                    if diff:
                        hd = (m - DF_Z0) // 2
                        n = DF_HEADS * i + hd + 1
                        dve.wait_ge(d_exp, n)
                        dve.reciprocal(p_rec[:, :], p_sum[:, :]).then_inc(d_rec, 1)
                        dve.wait_ge(d_rec, n)
                        dve.tensor_scalar(neg_lr[:, :], p_rec[:, 2:4], neg_lam[:, 0:1], None, ALU.mult
                                          ).then_inc(d_lam, 1)
                        dve.wait_ge(d_lam, n)
                        for t, (lo, hi) in enumerate(((0, P), (P, 384))):
                            last = dve.tensor_scalar(prob[:, 1, lo:hi], prob[:, 1, lo:hi], neg_lr[:, t:t + 1],
                                                     None, ALU.mult)
                        last.then_inc(d_part, 1)
                        dve.wait_ge(d_part, n)
                        for t, (lo, hi) in enumerate(((0, P), (P, 384))):
                            last = dve.scalar_tensor_tensor(out=mixed[:, lo:hi], in0=prob[:, 0, lo:hi],
                                                            scalar=p_rec[:, t:t + 1], in1=prob[:, 1, lo:hi],
                                                            op0=ALU.mult, op1=ALU.add)
                        last.then_inc(d_mixed, 1)
                    if m == 16:
                        dve.wait_ge(os_high, i + 1)
                        dve.tensor_tensor(os_lo[:, :, :].rearrange("p k n -> p (k n)"), pair(OS_PAIR),
                                          os_hi[:, :, :].rearrange("p k n -> p (k n)").bitcast(F32),
                                          ALU.subtract).then_inc(os_split, 1)
                    if m == 20:
                        dve.wait_ge(od_high, i + 1)
                        dve.tensor_tensor(x_lo[:, 0:4, :].rearrange("p k n -> p (k n)"), pair(OD_PAIR),
                                          x_hi[:, 0:4, :].rearrange("p k n -> p (k n)").bitcast(F32),
                                          ALU.subtract).then_inc(od_split, 1)
                    if m == 21:
                        for t in range(TT):
                            dve.wait_ge(gate_sig, 4 * i + 4)
                            wait_product(dve, y_sb_done, i + 1, i, U_BSB + 1, t)
                            dve.tensor_tensor(gates[:, 0, t, :], pair(Y_SB_PAIR[t]), gates[:, 0, t, :],
                                              ALU.mult).then_inc(gated_sb, 1)
                merge(i, 0)
                low(i, U_WIN + 25, halves=(0,))
                low_inputs(i, 2, 0)
                low(i, U_WIN + 25, halves=(1,))
                merge(i, 1)
                low_inputs(i, 2, 1)
                low(i, U_WIN + 26)
                low(i, U_WIN + 27)
                low(i, U_FFN2, 16)

            with dve.Fori(0, DEPTH) as i:
                dve.tensor_copy(neg_lam[:, :], neg_lams[:, bass.ds(i, 1)])
                dve.tensor_copy(g_layer[:, 32:33], g_cols[:, bass.ds(i + 64, 1)])
                dve.tensor_copy(g_layer[:, 0:32].rearrange("p (n k) -> p n k", n=4),
                                g_cols[:, 0:64].rearrange("p (n l k) -> p n (l k)", n=4, l=DEPTH)[
                                    :, :, bass.ds(i * KD, KD)]).then_inc(layer_g, 1)
                dve.wait_ge(layer_g, i + 1)
                low(i, 0, 0)
                low_inputs(i, 0, 0)
                low(i, 1, 4)
                low_inputs(i, 0, 1)
                ffn(i, 0, U_FFN1, 0, lambda: low(i, U_WIN, 8))
                boundary(i, 0, 1, DOWN_PAIR, lambda n: low(i, U_WIN + 1, 12, halves=(n,)))
                mixer(i)
                boundary(i, 1, 3, OUT_PAIR, lambda n: low(i, U_FFN2 + 1, 20, halves=(n,)))
                ffn(i, 1, U_FFN2, 16, lambda: low(i, U_PROJ))
                dve.wait_ge(p_high, i + 1)
                dve.tensor_tensor(p_lo[:, :, :], bank(P_BANK).rearrange("p (k n) -> p k n", k=2),
                                  p_hi[:, :, :].bitcast(F32), ALU.subtract).then_inc(p_split, 1)
                boundary(i, 2, 4, DOWN_PAIR, lambda n: low(i, U_GATE, 24, ks=2, halves=(n,)))
                for s in range(1, 4):
                    low(i, U_GATE + s, 24 + 2 * s, ks=2)
                for t in range(TT):
                    dve.wait_ge(ple_sig, 2 * i + t + 1)
                    wait_product(dve, e_done, i + 1, i, U_PROJ, t)
                    dve.tensor_tensor(gates[:, 1, t, :], pair(E_PAIR[t]), gates[:, 0, t, :], ALU.mult
                                      ).then_inc(ple_e, 1)
                    wait_gained(i, 3, t)
                    for k in range(2):
                        gained(i, 3, gates[:, 1, t, :], t, k)
                    for k in range(2):
                        update_h(i, 3, t, k)

        @block.tensor
        def _(pe):
            pe.wait_ge(const_id, 1)
            pe.wait_ge(g_in, 16 * 5)
            pe.transpose(bank(0)[:, 0:66], g_rows[0:66, :], ident[0:66, 0:66]).then_inc(cols_turned, 1)
            pe.transpose(bank(1)[:, 0:66], g_rows[0:66, :], ident[0:66, 0:66]).then_inc(units_used, SLOTS)

            def exact(dst, x_h, x_l, w_h, w_l, first, last):
                pe.matmul(dst, x_h, w_h, start=first, stop=False)
                pe.matmul(dst, x_h, w_l, start=False, stop=False)
                return pe.matmul(dst, x_l, w_h, start=False, stop=last)

            def wide(s, dst, xh, xl, k0, t, first, last, before=None):
                for k in range(4):
                    if before and k in before:
                        before[k]()
                    cols, toks = slice(k * W, (k + 1) * W), slice(t * P, (t + 1) * P)
                    mm = exact(dst, xh[:, k0 + k, toks], xl[:, k0 + k, toks], w_hi[:, s, cols], w_lo[:, s, cols],
                               first and k == 0, last and k == 3)
                return mm

            def deep(s, b, xh, xl, k0, t, first, last, before=None):
                toks = slice(t * P, (t + 1) * P)
                for n in range(2):
                    for k in range(2):
                        if before and 2 * n + k in before:
                            before[2 * n + k]()
                        cols = slice(k * D + n * W, k * D + (n + 1) * W)
                        mm = exact(bank(b + n), xh[:, k0 + k, toks], xl[:, k0 + k, toks],
                                   w_hi[:, s, cols], w_lo[:, s, cols], first and k == 0, last and k == 1)
                return mm

            def begin(i, u, c=0):
                pe.wait_ge(split_done, UNITS * i + 3 * c + u + 1 + SLOTS)

            def turn(i, q, idx):
                t, n = idx // 2, idx % 2
                if q == 2:
                    pe.wait_ge(merged, 4 * i + idx + 1)
                    src = gates[:, 0, t, :]
                else:
                    pe.wait_ge(h_ready, 16 * i + 4 * (q - (q > 2)) + idx + 1)
                    src = h[:, t, :]
                for k in range(4):
                    mm = pe.transpose(bank(X_BANK[q][idx])[:, k * P:(k + 1) * P],
                                      src[:, (4 * n + k) * P:(4 * n + k + 1) * P], ident[:, :])
                mm.then_inc(x_turned, 1)

            def turns(i, q, idxs, at):
                return {k: (lambda idx=idx: turn(i, q, idx)) for idx, k in zip(idxs, at)}

            def inputs(i, q, t, n):
                pe.wait_ge(x_split, 20 * i + 4 * q + 2 * t + n + 1)

            def by_tiles(i, u, product, done=None, before=None):
                for t in range(TT):
                    for s in range(2):
                        if t == 0:
                            begin(i, u + s)
                        mm = product(s, t, (before or {}).get((s, t)))
                        if t == 1:
                            mm.then_inc(units_used, 1)
                        elif s == 1 and done is not None:
                            mm.then_inc(done, 1)

            def turn_ht(i, f, c):
                pe.wait_ge(prod_done, 4 * NC * i + 2 * NC * f + 2 * c + 2)
                for k in range(2):
                    for t in range(TT):
                        mm = pe.transpose(bank(HT_BANK)[:, k * SEQ + t * P:k * SEQ + (t + 1) * P],
                                          glu[:, t, 1, k * P:(k + 1) * P], ident[:, :])
                mm.then_inc(ht_turned, 1)

            def turn_last_ht(i, f, t):
                pe.wait_ge(prod_done, 4 * NC * i + 2 * NC * f + 2 * (NC - 1) + t + 1)
                if t == 0:
                    pe.wait_ge(ht_split, 2 * HTS * i + HTS * f + NC - 1)
                for k in range(2):
                    mm = pe.transpose(bank(HT_BANK)[:, k * SEQ + t * P:k * SEQ + (t + 1) * P],
                                      glu[:, t, 1, k * P:(k + 1) * P], ident[:, :])
                mm.then_inc(ht_turned, 1)

            def ffn(i, f, q, u0, before_last):
                def gate_up(u, half, step, c=0):
                    begin(i, u, c)
                    for t in range(TT):
                        if half == 0:
                            pe.wait_ge(prod_done, 4 * NC * i + 2 * NC * f + 2 * step + t - 1)
                        mm = wide(slot(u), bank(GU_BANK[t]), x_hi, x_lo, 4 * half, t, half == 0, half == 1)
                        if half == 1 and t == 0:
                            mm.then_inc(gu_done, 1)
                    mm.then_inc(units_used, 1)

                def down(u, step, first=False, c=0):
                    begin(i, u, c)
                    pe.wait_ge(ht_split, 2 * HTS * i + HTS * f + step + 1)
                    for t in range(TT):
                        mm = deep(slot(u), DOWN_PAIR[t], ht_hi, ht_lo, 0, t, first, False)
                    mm.then_inc(units_used, 1)

                def step(c, at, first=False):
                    gate_up(u0 - 1, 0, c, at)
                    turn_ht(i, f, c - 1)
                    gate_up(u0, 1, c, at)
                    down(u0 + 1, c - 1, first=first, c=at)

                def first_gate_up(s, t, before):
                    inputs(i, q, t, s)
                    return wide(slot(u0 + s), bank(GU_BANK[t]), x_hi, x_lo, 4 * s, t, s == 0, s == 1, before)

                def last_down(s, t, before):
                    if s == 0:
                        pe.wait_ge(ht_split, 2 * HTS * i + HTS * f + NC - 1)
                    else:
                        pe.wait_ge(ht_split, 2 * HTS * i + HTS * f + NC + t)
                    xh, xl = (x_hi, x_lo) if s else (ht_hi, ht_lo)
                    return deep(slot(u0 + 3 * NC - 2 + s), DOWN_PAIR[t], xh, xl, 0, t, False, s == 1, before)

                by_tiles(i, u0, first_gate_up, gu_done, {(1, 0): turns(i, q, (2,), (3,)),
                                                         (0, 1): turns(i, q, (3,), (1,))})
                step(1, 1, first=True)
                with pe.Fori(2, NC - 1) as c:
                    step(c, c)
                gate_up(u0 + 3 * NC - 4, 0, NC - 1)
                turn_ht(i, f, NC - 2)
                gate_up(u0 + 3 * NC - 3, 1, NC - 1)
                before_last()
                by_tiles(i, u0 + 3 * NC - 2, last_down, f_done, {
                    (0, 0): {2: lambda: turn_last_ht(i, f, 0)}, (1, 0): {2: lambda: turn_last_ht(i, f, 1)},
                    (1, 1): turns(i, NEXT_INPUT[q], (0, 1), (1, 2))})

            def turn_four(dst, src):
                for k in range(4):
                    for t in range(TT):
                        mm = pe.transpose(dst[:, k * SEQ + t * P:k * SEQ + (t + 1) * P],
                                          src[:, t, k * P:(k + 1) * P], ident[:, :])
                return mm

            def stick_scores(i, hd):
                pe.wait_ge(sb_turned, 2 * i + 2)
                if hd >= 2:
                    pe.wait_ge(s_kept, SB_HEADS * i + hd - 1)
                dst, rows, k = bank(SB_BANK[hd % 2]), slice(64 * (hd % 2), 64 * (hd % 2) + 64), hd // 2
                pe.matmul(dst[:, 0:384], ident_b[:, :], mask_sb[:, :], start=True, stop=False, skip_group_check=True)
                pe.matmul(dst[:, 0:SEQ], sbk_t[rows, k, 0:P], sbq_t[rows, k, :], start=False, stop=False,
                          skip_group_check=True)
                pe.matmul(dst[:, SEQ:384], sbk_t[rows, k, P:SEQ], sbq_t[rows, k, P:SEQ], start=False, stop=True,
                          skip_group_check=True).then_inc(s_score, 1)

            def stick_later(i, hd):
                pe.wait_ge(s_soft, SB_HEADS * i + hd + 1)
                dst, s = bank(SB_BANK[hd % 2]), sp[:, hd % 2, :]
                pe.matmul(dst[:, 0:SEQ], neg_tri[:, :], s[:, 0:SEQ], start=False, stop=False, skip_group_check=True)
                pe.matmul(dst[:, P:SEQ], neg_one[:, :], s[:, SEQ:384], start=False, stop=False, skip_group_check=True)
                pe.matmul(dst[:, SEQ:384], neg_tri[:, :], s[:, SEQ:384], start=False, stop=True,
                          skip_group_check=True).then_inc(s_later, 1)

            def stick_values(i, hd):
                pe.wait_ge(s_weight, SB_HEADS * i + hd + 1)
                pe.wait_ge(kept_dve, 4 * i + 2)
                dst, w, c = bank(SB_BANK[hd % 2]), w_att[:, hd % 2, :], slice(hd * SB_D, (hd + 1) * SB_D)
                pe.matmul(dst[:, SB_OUT:SB_OUT + 64], w[:, 0:P], v_sb[:, 0, c], start=True, stop=True,
                          skip_group_check=True)
                pe.matmul(dst[:, SB_OUT + 64:W], w[:, P:SEQ], v_sb[:, 0, c], start=True, stop=False,
                          skip_group_check=True)
                pe.matmul(dst[:, SB_OUT + 64:W], w[:, SEQ:384], v_sb[:, 1, c], start=False, stop=True,
                          skip_group_check=True).then_inc(s_value, 1)

            def diff_scores(i, hd):
                pe.wait_ge(df_turned, 2 * i + 2)
                if hd:
                    pe.wait_ge(d_kept, DF_HEADS * i + hd)
                    pe.wait_ge(d_normed, DF_HEADS * i + hd)
                for c in range(2):
                    dst, rows = bank(DF_BANK[c]), slice(64 * c, 64 * c + 64)
                    pe.matmul(dst[:, 0:384], ident_b[:, :], mask_df[:, :], start=True, stop=False,
                              skip_group_check=True)
                    pe.matmul(dst[:, 0:P], dfq_t[rows, hd, 0:P], dfk_t[rows, hd, 0:P], start=False, stop=False,
                              skip_group_check=True)
                    mm = pe.matmul(dst[:, P:384], dfq_t[rows, hd, P:SEQ], dfk_t[rows, hd, :], start=False, stop=True,
                                   skip_group_check=True)
                mm.then_inc(d_score, 1)

            def diff_turn(i, hd):
                pe.wait_ge(d_mixed, DF_HEADS * i + hd + 1)
                for k in range(3):
                    mm = pe.transpose(bank(DF_BANK[0])[:, k * P:(k + 1) * P], mixed[:, k * P:(k + 1) * P], ident[:, :])
                mm.then_inc(d_turned, 1)

            def diff_values(i, hd):
                pe.wait_ge(d_kept, DF_HEADS * i + hd + 1)
                pe.wait_ge(kept_dve, 4 * i + 4)
                dst, c = bank(DF_BANK[1]), slice(hd * DF_V, (hd + 1) * DF_V)
                pe.matmul(dst[:, 0:P], mixed_t[:, 0:P], v_df[:, 0, c], start=True, stop=True, skip_group_check=True)
                pe.matmul(dst[:, P:SEQ], mixed_t[:, P:SEQ], v_df[:, 0, c], start=True, stop=False,
                          skip_group_check=True)
                pe.matmul(dst[:, P:SEQ], mixed_t[:, SEQ:384], v_df[:, 1, c], start=False, stop=True,
                          skip_group_check=True).then_inc(d_value, 1)

            def middle(i, m):
                if 0 <= m - SB_P0 < SB_HEADS:
                    stick_values(i, m - SB_P0)
                if 0 <= m - DF_P0 < 2 * DF_HEADS and (m - DF_P0) % 2 == 0:
                    diff_values(i, (m - DF_P0) // 2)

            def behind(i, m):
                if m == 2:
                    pe.wait_ge(kept_act, 16 * i + 2)
                    turn_four(pair(QK_PAIR), slab).then_inc(qk_turned, 1)
                if m == 4:
                    pe.wait_ge(kept_act, 16 * i + 4)
                    pe.wait_ge(sb_turned, 2 * i + 1)
                    turn_four(pair(QK_PAIR), slab).then_inc(qk_turned, 1)
                if m == 9:
                    pe.wait_ge(roped, 4 * i + 2)
                    pe.wait_ge(sb_turned, 2 * i + 2)
                    turn_four(pair(QK_PAIR), slab).then_inc(qk_turned, 1)
                if m == 11:
                    pe.wait_ge(roped, 4 * i + 4)
                    pe.wait_ge(df_turned, 2 * i + 1)
                    turn_four(pair(QK_PAIR), slab).then_inc(qk_turned, 1)
                if 0 <= m - SB_C0 < SB_HEADS:
                    stick_later(i, m - SB_C0)
                if 0 <= m - SB_Z0 < SB_HEADS:
                    stick_scores(i, m - SB_Z0)
                if 0 <= m - DF_Z0 < 2 * DF_HEADS and (m - DF_Z0) % 2 == 0:
                    diff_scores(i, (m - DF_Z0) // 2)
                if 0 <= m - DF_T0 < 2 * DF_HEADS and (m - DF_T0) % 2 == 0:
                    diff_turn(i, (m - DF_T0) // 2)
                if m == 16:
                    pe.wait_ge(s_kept, SB_HEADS * (i + 1))
                    turn_four(pair(OS_PAIR), o_sb).then_inc(os_turned, 1)
                if m == 20:
                    pe.wait_ge(d_normed, DF_HEADS * (i + 1))
                    turn_four(pair(OD_PAIR), o_df).then_inc(od_turned, 1)

            def kept(i, j, t):
                if j in (SBV, DFV):
                    pe.wait_ge(kept_dve, 4 * i + 2 * (SBV, DFV).index(j) + t + 1)
                else:
                    pe.wait_ge(kept_act, 16 * i + 2 * BY_ACT.index(j) + t + 1)

            def mixer(i):
                def first_win(s, t, before):
                    inputs(i, 1, t, s)
                    return wide(slot(U_WIN + s), bank(WIN_BANK[0][t]), x_hi, x_lo, 4 * s, t, s == 0, s == 1, before)

                def last_df(s, t, before):
                    return deep(slot(U_BDF + s), Y_DF_PAIR[t], x_hi, x_lo, 2 * s, t, s == 0, s == 1, before)

                def w_out(u, s, t, before):
                    inputs(i, 2, t, u // 2)
                    return deep(slot(U_WOUT + u + s), OUT_PAIR[t], x_hi, x_lo, 2 * (u + s), t,
                                u + s == 0, u + s == 3, before)

                by_tiles(i, U_WIN, first_win, win_done, {(1, 0): turns(i, 1, (2,), (3,)),
                                                         (0, 1): turns(i, 1, (3,), (1,))})
                for m in range(2, 20):
                    j, half = m // 2, m % 2
                    begin(i, U_WIN + m)
                    for t in range(TT):
                        if half == 0 and j >= 2:
                            kept(i, j - 2, t)
                        mm = wide(slot(U_WIN + m), bank(WIN_BANK[j % 2][t]), x_hi, x_lo, 4 * half, t,
                                  half == 0, half == 1)
                        if half == 1 and t == 0:
                            mm.then_inc(win_done, 1)
                        if t == 0:
                            middle(i, m)
                    mm.then_inc(units_used, 1)
                    behind(i, m)
                for m in (20, 21):
                    half = m % 2
                    begin(i, U_WIN + m)
                    if half == 0:
                        pe.wait_ge(os_split, i + 1)
                    for t in range(TT):
                        if m == 20:
                            kept(i, 8 + t, 1)
                        mm = deep(slot(U_WIN + m), Y_SB_PAIR[t], os_hi, os_lo, 2 * half, t, half == 0, half == 1)
                        if half == 1 and t == 0:
                            mm.then_inc(y_sb_done, 1)
                        if t == 0:
                            middle(i, m)
                    mm.then_inc(units_used, 1)
                    behind(i, m)
                pe.wait_ge(od_split, i + 1)
                by_tiles(i, U_BDF, last_df, y_df_done, {(1, 1): turns(i, 2, (0, 1), (0, 1))})
                by_tiles(i, U_WOUT, lambda s, t, before: w_out(0, s, t, before), None,
                         {(1, 0): turns(i, 2, (2, 3), (2, 3))})
                by_tiles(i, U_WOUT + 2, lambda s, t, before: w_out(2, s, t, before), f_done,
                         {(1, 1): turns(i, 3, (0, 1), (1, 2))})

            NEXT_INPUT = {0: 1, 3: 4}

            def turn_p(i):
                pe.wait_ge(p_in, 16 * i + 16)
                for k in range(2):
                    for t in range(TT):
                        mm = pe.transpose(bank(P_BANK)[:, k * SEQ + t * P:k * SEQ + (t + 1) * P],
                                          p_nat[:, t, k * P:(k + 1) * P], ident[:, :])
                mm.then_inc(p_turned, 1)

            pe.wait_ge(h_loaded, 16 * TT)
            pe.wait_ge(cols_kept, 1)
            with pe.Fori(0, DEPTH) as i:
                for idx in range(2):
                    turn(i, 0, idx)
                ffn(i, 0, 0, U_FFN1, lambda: None)
                pe.wait_ge(const_all, 1)
                mixer(i)
                ffn(i, 1, 3, U_FFN2, lambda: turn_p(i))
                begin(i, U_PROJ)
                pe.wait_ge(p_split, i + 1)
                for t in range(TT):
                    mm = deep(slot(U_PROJ), E_PAIR[t], p_hi, p_lo, 0, t, True, True)
                    if t == 0:
                        mm.then_inc(e_done, 1)
                mm.then_inc(units_used, 1)
                for idx in range(2, 4):
                    turn(i, 4, idx)

                def gate(u, s, t, before):
                    inputs(i, 4, t, 1)
                    return deep(slot(U_GATE + u + s), GATE_PAIR[t], x_hi, x_lo, 2 * (u + s), t,
                                u + s == 0, u + s == 3, before)

                by_tiles(i, U_GATE, lambda s, t, before: gate(0, s, t, before))
                by_tiles(i, U_GATE + 2, lambda s, t, before: gate(2, s, t, before), f_done)


_NAMES = ["x", "p", "positions",
          "ffn1_pre_g", "ffn1_w_gu", "ffn1_w_down", "ffn1_post_g",
          "mix_pre_g", "w_in", "diff_lambda", "diff_subln_g", "w_branch_sb", "w_branch_diff", "w_out", "mix_post_g",
          "ffn2_pre_g", "ffn2_w_gu", "ffn2_w_down", "ffn2_post_g",
          "ple_pre_g", "w_ple_gate", "w_ple_proj", "ple_post_g"]


def kernel(**inputs):
    import concourse.bacc as bacc
    from concourse.bass_utils import run_bass_kernel_spmd

    nc = bacc.Bacc("TRN2", target_bir_lowering=False, num_devices=1)
    arrays, args = {}, {}
    for name in _NAMES:
        x = np.ascontiguousarray(inputs[name])
        arrays[f"in_{name}"] = x
        args[name] = nc.dram_tensor(f"in_{name}", x.shape, mybir.dt.from_np(x.dtype), kind="ExternalInput").ap()
    out = nc.dram_tensor("out_h", (1, SEQ, D), F32, kind="ExternalOutput").ap()
    trunk_kernel(nc, args, out)
    r = run_bass_kernel_spmd(nc, [arrays], core_ids=[0])
    return r.results[0]["out_h"]
```

```python
import math
from contextlib import ExitStack

import numpy as np

import concourse.bass as bass
from concourse import mybir

ALU = mybir.AluOpType
ACT = mybir.ActivationFunctionType
AX_X = mybir.AxisListType.X
F32 = mybir.dt.float32
F32R = mybir.dt.float32r
BF16 = mybir.dt.bfloat16
I32 = mybir.dt.int32

P = 128

DEPTH, SEQ, D = 2, 256, 1024
PLE, FF = 256, 2816
SB_HEADS, SB_D = 8, 64
DF_HEADS, DF_D = 4, 64
DF_V = 2 * DF_D
THETA, EPS, SUB_EPS = 10000.0, 1e-6, 1e-5
NEG = -1.0e30

TT = SEQ // P
KD = D // P
FC = 256
NC = FF // FC
W = 512
SLOTS = 3
UNIT = 2048

U_FFN = 3 * NC
U_FFN1 = 0
U_WIN = U_FFN1 + U_FFN
U_BSB = U_WIN + 20
U_BDF = U_BSB + 2
U_WOUT = U_BDF + 2
U_FFN2 = U_WOUT + 4
U_PROJ = U_FFN2 + U_FFN
U_GATE = U_PROJ + 1
UNITS = U_GATE + 4
assert UNITS % SLOTS == 0

SBQ, SBK, SBV, DFQ, DFK, DFV = range(6)
SB_Z0, SB_C0, SB_P0 = 6, 7, 8
DF_Z0, DF_T0, DF_P0 = 12, 13, 14
BY_ACT = (0, 1, 3, 4, 6, 7, 8, 9)
QK_ORDER = {SBQ: 0, SBK: 1, DFQ: 2, DFK: 3}

WARM_UP = 30
MEANS = 20
HTS = NC + 1
FACTOR = (0.5, 1.0, 0.5, 1.0)
LAM_INIT = [0.8 - 0.6 * math.exp(-0.3 * n) for n in range(DEPTH)]
ROUND = 1.5 * 2.0 ** 23
TWO_PI = [6.28125, round((2 * math.pi - 6.28125) * 2 ** 21) / 2 ** 21]
TWO_PI.append(2 * math.pi - sum(TWO_PI))
PI_IN = 3.1415925


def trunk_kernel(nc, a, out):
    with ExitStack() as ctx:
        def sb(name, shape, dt=F32):
            return ctx.enter_context(nc.sbuf_tensor(name, shape, dt))

        def sem(name):
            return ctx.enter_context(nc.semaphore(name))

        ps = ctx.enter_context(nc.psum_tensor("ps", [P, 8, W], F32))

        def bank(b):
            return ps[:, b, :]

        def pair(b):
            return ps[:, b:b + 2, :].rearrange("p b n -> p (b n)")

        raw = sb("raw", [P, SLOTS, UNIT])
        w_hi = sb("w_hi", [P, SLOTS, UNIT], F32R)
        w_lo = sb("w_lo", [P, SLOTS, UNIT], F32R)
        h = sb("h", [P, TT, D])
        x_hi = sb("x_hi", [P, KD, SEQ], F32R)
        x_lo = sb("x_lo", [P, KD, SEQ], F32R)
        glu = sb("glu", [P, TT, 2, FC])
        ht_hi = sb("ht_hi", [P, 2, SEQ], F32R)
        ht_lo = sb("ht_lo", [P, 2, SEQ], F32R)
        p_hi = sb("p_hi", [P, 2, SEQ], F32R)
        p_lo = sb("p_lo", [P, 2, SEQ], F32R)
        p_nat = sb("p_nat", [P, TT, PLE])
        tmp = sb("tmp", [P, TT, D])
        squares = sb("squares", [P, D])
        post_g = sb("post_g", [P, 2, D])
        g_cols = sb("g_cols", [P, 4, (DEPTH + 1) * KD])
        g_sub = sb("g_sub", [P, DEPTH + 1])
        g_layer = sb("g_layer", [P, 33])
        lam_layer = sb("lam_layer", [P, 4, DF_D])
        lam_pr = sb("lam_pr", [P, 2, DF_D])
        lam_s = sb("lam_s", [P, 2])
        lam_e = sb("lam_e", [P, 2])
        neg_inits = sb("neg_inits", [P, DEPTH + 1])
        neg_init = sb("neg_init", [P, 1])
        neg_lam = sb("neg_lam", [P, 1])
        mean_pre = sb("mean_pre", [P, TT])
        ms_pre = sb("ms_pre", [P, TT])
        r_pre = sb("r_pre", [P, TT])
        r_query = sb("r_query", [P, TT])
        mean_post = sb("mean_post", [P, TT])
        ms_post = sb("ms_post", [P, TT])
        r_post = sb("r_post", [P, TT])
        neg_half = sb("neg_half", [P, TT])
        eps_norm = sb("eps_norm", [P, TT])
        eps_half = sb("eps_half", [P, TT])
        eps_sub = sb("eps_sub", [P, TT])
        q_factor = sb("q_factor", [P, TT])
        sbq_t = sb("sbq_t", [P, 4, SEQ])
        sbk_t = sb("sbk_t", [P, 4, SEQ])
        dfq_t = sb("dfq_t", [P, 4, SEQ])
        dfk_t = sb("dfk_t", [P, 4, SEQ])
        v_sb = sb("v_sb", [P, TT, W])
        v_df = sb("v_df", [P, TT, W])
        gates = sb("gates", [P, 2, TT, D])
        soft = sb("soft", [P, 2, 384])
        sp_hi = sb("sp_hi", [P, 2, 384], F32R)
        sp_lo = sb("sp_lo", [P, 2, 384], F32R)
        w_att = sb("w_att", [P, 2, 384])
        o_sb = sb("o_sb", [P, TT, W])
        os_hi = sb("os_hi", [P, 4, SEQ], F32R)
        os_lo = sb("os_lo", [P, 4, SEQ], F32R)
        prob = sb("prob", [P, 2, 384])
        neg_max = sb("neg_max", [P, 4])
        p_sum = sb("p_sum", [P, 4])
        p_rec = sb("p_rec", [P, 4])
        neg_lr = sb("neg_lr", [P, 2])
        mixed = sb("mixed", [P, 384])
        mixed_t = sb("mixed_t", [P, 384])
        mean_sub = sb("mean_sub", [P, TT])
        ms_sub = sb("ms_sub", [P, TT])
        r_sub = sb("r_sub", [P, TT])
        ident = sb("ident", [P, P])
        ident_b = sb("ident_b", [P, P], BF16)
        neg_tri = sb("neg_tri", [P, P], F32R)
        neg_one = sb("neg_one", [P, P], F32R)
        mask_sb = sb("mask_sb", [P, 384], BF16)
        mask_df = sb("mask_df", [P, 384], BF16)
        pos_i = sb("pos_i", [P, TT], I32)
        pos_f = sb("pos_f", [P, TT])
        freq = sb("freq", [P, 32])
        rope_c = sb("rope_c", [P, TT, 64])
        rope_s = sb("rope_s", [P, TT, 64])

        o_df = glu[:, :, :, :].rearrange("p t a n -> p t (a n)")
        rope_b = o_df
        slab = tmp[:, :, 0:W]
        slab_c = tmp[:, :, W:D]

        minus = mixed_t[:, 0:P]
        g_rows = mixed_t[:, P:2 * P]
        ang, turns, cos_in = (mixed[:, 64 * n:64 * n + 64].rearrange("p (t f) -> p t f", t=TT) for n in range(3))

        raw_in = [sem(f"raw_in{s}") for s in range(SLOTS)]
        hi_ready = sem("hi_ready")
        split_done = sem("split_done")
        units_used = sem("units_used")
        gu_done = sem("gu_done")
        silu_done = sem("silu_done")
        prod_done = sem("prod_done")
        ht_turned = sem("ht_turned")
        ht_high = sem("ht_high")
        ht_split = sem("ht_split")
        p_turned = sem("p_turned")
        p_high = sem("p_high")
        p_split = sem("p_split")
        x_turned = sem("x_turned")
        x_high = sem("x_high")
        x_split = sem("x_split")
        h_loaded = [sem(f"h_loaded{n}") for n in range(2 * TT)]
        h_ready = sem("h_ready")
        squared_pre = sem("squared_pre")
        mean_done = sem("mean_done")
        pre_scale = sem("pre_scale")
        query_scale = sem("query_scale")
        squared_post = sem("squared_post")
        post_scale = sem("post_scale")
        f_done = sem("f_done")
        scaled = sem("scaled")
        win_done = sem("win_done")
        kept_act = sem("kept_act")
        kept_dve = sem("kept_dve")
        rope_parts = sem("rope_parts")
        roped = sem("roped")
        qk_turned = sem("qk_turned")
        sb_turned = sem("sb_turned")
        df_turned = sem("df_turned")
        s_score = sem("s_score")
        s_abs = sem("s_abs")
        s_exp = sem("s_exp")
        s_log = sem("s_log")
        s_soft = sem("s_soft")
        s_later = sem("s_later")
        s_weight = sem("s_weight")
        s_value = sem("s_value")
        s_kept = sem("s_kept")
        os_turned = sem("os_turned")
        os_high = sem("os_high")
        os_split = sem("os_split")
        d_score = sem("d_score")
        d_max = sem("d_max")
        d_exp = sem("d_exp")
        d_rec = sem("d_rec")
        d_part = sem("d_part")
        d_mixed = sem("d_mixed")
        d_turned = sem("d_turned")
        d_kept = sem("d_kept")
        d_value = sem("d_value")
        d_square = sem("d_square")
        d_scale = sem("d_scale")
        d_normed = sem("d_normed")
        od_turned = sem("od_turned")
        od_high = sem("od_high")
        od_split = sem("od_split")
        y_sb_done = sem("y_sb_done")
        y_df_done = sem("y_df_done")
        gate_sig = sem("gate_sig")
        gated_sb = sem("gated_sb")
        gated_df = sem("gated_df")
        merged = sem("merged")
        e_done = sem("e_done")
        ple_sig = sem("ple_sig")
        ple_e = sem("ple_e")
        layer_g = sem("layer_g")
        post_in = [sem(f"post_in{s}") for s in range(2)]
        p_in = sem("p_in")
        g_in = sem("g_in")
        last_g_in = sem("last_g_in")
        lam_loaded = sem("lam_loaded")
        pos_in = sem("pos_in")
        const_id = sem("const_id")
        const_all = sem("const_all")
        cols_turned = sem("cols_turned")
        cols_kept = sem("cols_kept")
        d_lam = sem("d_lam")
        setup_step = sem("setup_step")
        angles = sem("angles")
        sines = sem("sines")
        rope_ready = sem("rope_ready")
        lam_step = sem("lam_step")
        lam_exp = sem("lam_exp")
        lam_known = sem("lam_known")
        blank = sem("blank")
        out_done = sem("out_done")

        X_BANK = ((0, 1, 2, 3), (6, 7, 0, 1), (4, 5, 2, 3), (2, 3, 0, 1), (0, 1, 2, 3))
        HT_BANK, P_BANK = 6, 7
        GU_BANK = (4, 5)
        WIN_BANK = ((4, 5), (2, 3))
        DOWN_PAIR = (0, 2)
        OUT_PAIR = (0, 6)
        Y_SB_PAIR = (4, 2)
        Y_DF_PAIR = (0, 6)
        E_PAIR = (4, 6)
        GATE_PAIR = (0, 2)
        QK_PAIR, OS_PAIR, OD_PAIR = 6, 0, 6
        SB_BANK = (0, 1)
        DF_BANK = (6, 7)
        SB_OUT = 384

        def slot(u):
            return u % SLOTS

        def wait_product(eng, done, count, i, u, t, c=0):
            if t == 0:
                eng.wait_ge(done, count)
            else:
                eng.wait_ge(units_used, UNITS * i + 3 * c + u + 1 + SLOTS)

        F_UNIT = (U_WIN - 1, U_FFN2 - 1, U_PROJ - 1, UNITS - 1)

        block = ctx.enter_context(nc.Block())

        @block.sync
        def _(sp_):
            for n, name in ((0, "ffn1_pre_g"), (1, "mix_pre_g")):
                sp_.dma_start(g_rows[2 * KD * n:2 * KD * (n + 1), :],
                              a[name].rearrange("l (k p) -> (l k) p", p=P)).then_inc(g_in, 16)

            def load(i, u, parts, c=0):
                sp_.wait_ge(split_done, UNITS * i + 3 * c + u + 1)
                for dst, src in parts:
                    sp_.dma_start(dst, src).then_inc(raw_in[slot(u)], 16)

            def load_gu(i, u, w, step, s, c=0):
                dst = raw[:, slot(u), :].rearrange("p (k g n) -> p k g n", k=4, g=2)
                rows = w[bass.ds(i, 1), s * 4 * P:(s + 1) * 4 * P, :].rearrange("o (k p) n -> p (o k) n", p=P)
                load(i, u, [(dst[:, :, g, :], rows[:, :, bass.ds(step * FC + g * FF, FC)]) for g in range(2)], c)

            def load_deep(i, u, w, row, c=0):
                dst = raw[:, slot(u), :].rearrange("p (k n) -> p k n", k=2)
                load(i, u, [(dst[:, k, :], w[bass.ds(i, 1), bass.ds(row + k * P, P), :].rearrange("o p n -> p (o n)"))
                            for k in range(2)], c)

            def load_ffn(i, u0, w_gu, w_down):
                for s in range(2):
                    load_gu(i, u0 + s, w_gu, 0, s)
                with sp_.Fori(1, NC) as c:
                    load_gu(i, u0 - 1, w_gu, c, 0, c)
                    load_gu(i, u0, w_gu, c, 1, c)
                    load_deep(i, u0 + 1, w_down, c * FC - FC, c)
                load_deep(i, u0 + U_FFN - 1, w_down, (NC - 1) * FC)

            with sp_.Fori(0, DEPTH) as i:
                load_ffn(i, U_FFN1, a["ffn1_w_gu"], a["ffn1_w_down"])
                for m in range(20):
                    dst = raw[:, slot(U_WIN + m), :].rearrange("p (k n) -> p k n", k=4)
                    r0, c0 = (m % 2) * 4 * P, (m // 2) * W
                    src = a["w_in"][bass.ds(i, 1), r0:r0 + 4 * P, c0:c0 + W].rearrange("o (k p) n -> p (o k) n", p=P)
                    load(i, U_WIN + m, [(dst[:, k:k + 2, :], src[:, k:k + 2, :]) for k in (0, 2)])
                for s in range(2):
                    load_deep(i, U_BSB + s, a["w_branch_sb"], 2 * P * s)
                for s in range(2):
                    load_deep(i, U_BDF + s, a["w_branch_diff"], 2 * P * s)
                for s in range(4):
                    load_deep(i, U_WOUT + s, a["w_out"], 2 * P * s)
                load_ffn(i, U_FFN2, a["ffn2_w_gu"], a["ffn2_w_down"])
                load_deep(i, U_PROJ, a["w_ple_proj"], 0)
                for s in range(4):
                    load_deep(i, U_GATE + s, a["w_ple_gate"], 2 * P * s)
            for t in range(TT):
                for n in range(2):
                    sp_.wait_ge(h_ready, 16 * DEPTH + 2 * t + n + 1)
                    sp_.dma_start(out[0, t * P:(t + 1) * P, n * W:(n + 1) * W],
                                  h[:, t, n * W:(n + 1) * W]).then_inc(out_done, 16)
            sp_.wait_ge(out_done, 16 * 2 * TT)

        @block.gpsimd
        def _(pool):
            pool.memset(ident[:, :], 0.0).then_inc(blank, 1)
            pool.dma_start(g_rows[48:64, :], a["ple_pre_g"].rearrange("l (k p) -> (l k) p", p=P)
                           ).then_inc(last_g_in, 16)
            pool.dma_start(g_rows[64:66, :], a["diff_subln_g"]).then_inc(last_g_in, 16)
            pool.wait_ge(blank, 1)
            pool.affine_select(out=ident[:, :], in_=ident[:, :], compare_op=ALU.not_equal, fill=1.0,
                               base=0, pattern=[[-1, P]], channel_multiplier=1).then_inc(const_id, 1)
            for t in range(TT):
                pool.dma_start(pos_i[:, t:t + 1], a["positions"][0, t * P:(t + 1) * P].rearrange(
                    "(p o) -> p o", o=1)).then_inc(pos_in, 16)
            pool.memset(neg_half[:, :], -0.5)
            pool.memset(eps_norm[:, :], EPS)
            pool.memset(eps_half[:, :], EPS / 0.25)
            pool.memset(eps_sub[:, :], SUB_EPS)
            pool.memset(q_factor[:, :], SB_D ** -0.5)
            pool.memset(ident_b[:, :], 0.0)
            pool.memset(minus[:, :], -1.0)
            pool.memset(mask_sb[:, :], 0.0)
            pool.memset(mask_df[:, :], 0.0).then_inc(blank, 1)
            pool.wait_ge(blank, 2)
            pool.affine_select(out=ident_b[:, :], in_=ident_b[:, :], compare_op=ALU.not_equal, fill=1.0,
                               base=0, pattern=[[-1, P]], channel_multiplier=1)
            pool.tensor_copy(neg_one[:, :], minus[:, :])
            pool.affine_select(out=neg_tri[:, :], in_=minus[:, :], compare_op=ALU.is_ge, fill=0.0,
                               base=0, pattern=[[-1, P]], channel_multiplier=1)
            for c in (0, 256):
                pool.affine_select(out=mask_sb[:, c:c + P], in_=mask_sb[:, c:c + P], compare_op=ALU.is_gt,
                                   fill=NEG, base=0, pattern=[[1, P]], channel_multiplier=-1)
                last = pool.affine_select(out=mask_df[:, c:c + P], in_=mask_df[:, c:c + P],
                                          compare_op=ALU.is_ge, fill=NEG, base=0, pattern=[[-1, P]],
                                          channel_multiplier=1)
            last.then_inc(const_all, 1)

            def rsqrt_mean(i, order, mean, ms, r, eps):
                pool.tensor_tensor(ms, mean, eps[:, 0:ms.shape[1]], ALU.add).then_inc(mean_done, 1)
                pool.wait_ge(mean_done, MEANS * i + order + 1)
                return pool.tensor_tensor(r, ms, neg_half[:, 0:ms.shape[1]], ALU.pow)

            def pre_norm(i, n, order):
                for t in range(TT):
                    pool.wait_ge(squared_pre, 8 * i + 2 * n + t + 1)
                    rsqrt_mean(i, order + t, mean_pre[:, t:t + 1], ms_pre[:, t:t + 1], r_pre[:, t:t + 1],
                               eps_norm).then_inc(pre_scale, 1)

            def post_norm(i, n, order):
                for t in range(TT):
                    pool.wait_ge(squared_post, 8 * i + 2 * n + t + 1)
                    rsqrt_mean(i, order + t, mean_post[:, t:t + 1], ms_post[:, t:t + 1], r_post[:, t:t + 1],
                               eps_half if FACTOR[n] == 0.5 else eps_norm).then_inc(post_scale, 1)

            def rope(i, k):
                for t in range(TT):
                    pool.wait_ge(kept_act, 16 * i + 2 * (2 + k) + t + 1)
                    if k or t:
                        pool.wait_ge(roped, 4 * i + 2 * k + t)
                    x = slab[:, t, :].rearrange("p (g c) -> p g c", c=64)
                    y = rope_b[:, t, :].rearrange("p (g c) -> p g c", c=64)
                    pool.tensor_tensor(slab_c[:, t, :].rearrange("p (g c) -> p g c", c=64), x,
                                       rope_c[:, t:t + 1, :].to_broadcast([P, 8, 64]), ALU.mult)
                    pool.tensor_tensor(y[:, :, 0:32], x[:, :, 32:64],
                                       rope_s[:, t:t + 1, 0:32].to_broadcast([P, 8, 32]), ALU.mult)
                    pool.tensor_tensor(y[:, :, 32:64], x[:, :, 0:32],
                                       rope_s[:, t:t + 1, 32:64].to_broadcast([P, 8, 32]), ALU.mult
                                       ).then_inc(rope_parts, 1)
                    pool.wait_ge(rope_parts, 4 * i + 2 * k + t + 1)
                    pool.tensor_tensor(slab[:, t, :], slab_c[:, t, :], rope_b[:, t, :], ALU.add).then_inc(roped, 1)

            with pool.Fori(0, DEPTH) as i:
                pre_norm(i, 0, 0)
                post_norm(i, 0, 2)
                pre_norm(i, 1, 4)
                pool.wait_ge(pre_scale, 8 * i + 4)
                pool.tensor_tensor(r_query[:, :], r_pre[:, :], q_factor[:, :], ALU.mult).then_inc(query_scale, 1)
                pool.wait_ge(rope_ready, 1)
                rope(i, 0)
                rope(i, 1)
                for hd in range(DF_HEADS):
                    pool.wait_ge(d_square, 4 * i + hd + 1)
                    rsqrt_mean(i, 6 + hd, mean_sub[:, :], ms_sub[:, :], r_sub[:, :], eps_sub
                               ).then_inc(d_scale, 1)
                post_norm(i, 1, 10)
                pre_norm(i, 2, 12)
                post_norm(i, 2, 14)
                pre_norm(i, 3, 16)
                post_norm(i, 3, 18)

        @block.scalar
        def _(act):
            act.dma_start(g_rows[32:48, :], a["ffn2_pre_g"].rearrange("l (k p) -> (l k) p", p=P)).then_inc(g_in, 16)

            def load_x(idx):
                rows, cols = slice(idx // 2 * P, (idx // 2 + 1) * P), slice(idx % 2 * W, (idx % 2 + 1) * W)
                act.dma_start(h[:, idx // 2, cols], a["x"][0, rows, cols]).then_inc(h_loaded[idx], 16)

            load_x(0)
            act.preload_act_table_set("silu_and_others")
            load_x(1)

            def high(i, u, gain=None, ks=4, c=0, halves=(0, 1)):
                s = slot(u)
                for half in halves:
                    if half == 0:
                        act.wait_ge(raw_in[s], 32 * (UNITS // 3) * i + 32 * c + 32 * (u // 3) + 32)
                        act.wait_ge(units_used, UNITS * i + 3 * c + u + 1)
                    pieces = 2 if ks == 4 and gain is not None else 1
                    n = UNIT // 2 // pieces
                    for k in range(pieces * half, pieces * half + pieces):
                        part = slice(k * n, (k + 1) * n)
                        if gain is None:
                            last = act.activation(w_hi[:, s, part], raw[:, s, part], ACT.Copy)
                        else:
                            g = gain + (k if ks > 1 else 0)
                            last = act.activation(w_hi[:, s, part], raw[:, s, part], ACT.Copy,
                                                  scale=g_layer[:, g:g + 1])
                    last.then_inc(hi_ready, 1)

            def high_inputs(i, q, t, halves=(0, 1)):
                for n in halves:
                    idx = 2 * t + n
                    act.wait_ge(x_turned, 20 * i + 4 * q + idx + 1)
                    act.activation(x_hi[:, 4 * n:4 * n + 4, t * P:(t + 1) * P],
                                   bank(X_BANK[q][idx]).rearrange("p (k n) -> p k n", k=4),
                                   ACT.Copy).then_inc(x_high, 1)

            def square_pre(i, n, t):
                act.wait_ge(h_ready, 16 * i + 4 * n + 2 * t + 2)
                act.activation(tmp[:, t, :], h[:, t, :], ACT.Square, scale=D ** -0.5,
                               accum_out=mean_pre[:, t:t + 1]).then_inc(squared_pre, 1)

            def square_post(i, n, src, t):
                if n < 3:
                    wait_product(act, f_done, 4 * i + n + 1, i, F_UNIT[n], t)
                else:
                    act.wait_ge(ple_e, 2 * i + t + 1)
                if t == 1:
                    act.wait_ge(squared_post, 8 * i + 2 * n + 1)
                act.activation(squares[:, :], src, ACT.Square, scale=D ** -0.5 / FACTOR[n],
                               accum_out=mean_post[:, t:t + 1]).then_inc(squared_post, 1)

            def boundary(i, n, q, pairs, next_unit, unit_after):
                square_post(i, n, pair(pairs[0]), 0)
                next_unit(0)
                high_inputs(i, q, 0)
                next_unit(1)
                square_post(i, n, pair(pairs[1]), 1)
                unit_after()
                if q == 4:
                    square_pre(i, n + 1, 0)
                    high_inputs(i, q, 1)
                else:
                    high_inputs(i, q, 1, (0,))
                    square_pre(i, n + 1, 0)
                    high_inputs(i, q, 1, (1,))
                square_pre(i, n + 1, 1)

            def high_ht(i, f, c):
                act.wait_ge(ht_turned, 2 * HTS * i + HTS * f + c + 1)
                act.activation(ht_hi[:, :, :], bank(HT_BANK).rearrange("p (k n) -> p k n", k=2),
                               ACT.Copy).then_inc(ht_high, 1)

            def high_last_ht(i, f, t):
                toks = slice(t * P, (t + 1) * P)
                act.wait_ge(ht_turned, 2 * HTS * i + HTS * f + NC + t)
                act.activation(x_hi[:, 0:2, toks], bank(HT_BANK).rearrange("p (k n) -> p k n", k=2)[:, :, toks],
                               ACT.Copy).then_inc(ht_high, 1)

            def silu(i, f, step, u, t, c=0):
                wait_product(act, gu_done, 2 * NC * i + NC * f + step + 1, i, u, t, c)
                act.activation(glu[:, t, 0, :], bank(GU_BANK[t])[:, 0:FC], ACT.Silu,
                               scale=r_pre[:, t:t + 1]).then_inc(silu_done, 1)

            def ffn(i, f, u0, g0, next_unit, loads):
                act.wait_ge(pre_scale, 8 * i + 4 * f + 1)
                silu(i, f, 0, u0 + 1, 0)
                high(i, u0 + 3, g0 + 4, halves=(0,))
                act.wait_ge(pre_scale, 8 * i + 4 * f + 2)
                silu(i, f, 0, u0 + 1, 1)
                high(i, u0 + 3, g0 + 4, halves=(1,))
                loads()
                with act.Fori(1, NC - 1) as c:
                    high(i, u0 + 1, c=c)
                    high_ht(i, f, c - 1)
                    high(i, u0 + 2, g0, c=c)
                    for t in range(TT):
                        silu(i, f, c, u0, t, c)
                    high(i, u0 + 3, g0 + 4, c=c)
                high(i, u0 + 3 * NC - 2)
                high_ht(i, f, NC - 2)
                high(i, u0 + 3 * NC - 1)
                for t in range(TT):
                    silu(i, f, NC - 1, u0 + 3 * NC - 3, t)
                high_last_ht(i, f, 0)
                next_unit()
                high_last_ht(i, f, 1)

            def stick_weights(i, m):
                hd = m - SB_C0
                if 0 <= hd < SB_HEADS:
                    act.wait_ge(s_later, SB_HEADS * i + hd + 1)
                    act.activation(w_att[:, hd % 2, :], bank(SB_BANK[hd % 2])[:, 0:384], ACT.Exp
                                   ).then_inc(s_weight, 1)

            def stick_softplus(i, m):
                hd = m - SB_Z0
                if 0 <= hd < SB_HEADS:
                    act.wait_ge(s_score, SB_HEADS * i + hd + 1)
                    act.activation(soft[:, hd % 2, :], bank(SB_BANK[hd % 2])[:, 0:384], ACT.Abs).then_inc(s_abs, 1)
                    act.wait_ge(s_abs, SB_HEADS * i + hd + 1)
                    act.activation(soft[:, hd % 2, :], soft[:, hd % 2, :], ACT.Exp, scale=-1.0).then_inc(s_exp, 1)
                    act.wait_ge(s_exp, SB_HEADS * i + hd + 1)
                    act.activation(soft[:, hd % 2, :], soft[:, hd % 2, :], ACT.Ln, bias=1.0).then_inc(s_log, 1)

            def diff_after(i, m):
                if m >= DF_Z0 and (m - DF_Z0) % 2 == 0 and (m - DF_Z0) // 2 < DF_HEADS:
                    hd = (m - DF_Z0) // 2
                    act.wait_ge(d_max, DF_HEADS * i + hd + 1)
                    for c in range(2):
                        for t, (lo, hi) in enumerate(((0, P), (P, 384))):
                            last = act.activation(prob[:, c, lo:hi], bank(DF_BANK[c])[:, lo:hi], ACT.Exp,
                                                  bias=neg_max[:, 2 * c + t:2 * c + t + 1],
                                                  accum_out=p_sum[:, 2 * c + t:2 * c + t + 1])
                    last.then_inc(d_exp, 1)
                if m >= DF_T0 and (m - DF_T0) % 2 == 0 and (m - DF_T0) // 2 < DF_HEADS:
                    hd = (m - DF_T0) // 2
                    act.wait_ge(d_turned, DF_HEADS * i + hd + 1)
                    act.activation(mixed_t[:, :], bank(DF_BANK[0])[:, 0:384], ACT.Copy).then_inc(d_kept, 1)

            def diff_mid(i, m):
                if m >= DF_P0 and (m - DF_P0) % 2 == 0 and (m - DF_P0) // 2 < DF_HEADS:
                    hd = (m - DF_P0) // 2
                    act.wait_ge(d_value, DF_HEADS * i + hd + 1)
                    if hd:
                        act.wait_ge(d_square, DF_HEADS * i + hd)
                    for t in range(TT):
                        last = act.activation(squares[:, t * P:(t + 1) * P], bank(DF_BANK[1])[:, t * P:(t + 1) * P],
                                              ACT.Square, scale=DF_V ** -0.5, accum_out=mean_sub[:, t:t + 1])
                    last.then_inc(d_square, 1)

            def keep(i, m):
                j = m // 2
                if m % 2 == 0 or m >= 20 or j in (SBV, DFV):
                    return
                if j == SBQ:
                    act.wait_ge(query_scale, i + 1)
                for t in range(TT):
                    wait_product(act, win_done, 10 * i + j + 1, i, U_WIN + m, t)
                    src = bank(WIN_BANK[j % 2][t])
                    if j < 6:
                        if t == 0 and QK_ORDER[j]:
                            act.wait_ge(qk_turned, 4 * i + QK_ORDER[j])
                        r = r_query if j in (SBQ, DFQ) else r_pre
                        act.activation(slab[:, t, :], src, ACT.Copy, scale=r[:, t:t + 1]).then_inc(kept_act, 1)
                    else:
                        g, n = (j - 6) // 2, (j - 6) % 2
                        act.activation(gates[:, g, t, n * W:(n + 1) * W], src, ACT.Copy,
                                       scale=r_pre[:, t:t + 1]).then_inc(kept_act, 1)

            def mixer(i):
                for m in range(23):
                    if m == 0:
                        pass
                    elif m < 18:
                        high(i, U_WIN + m + 2, 8 + 4 * (m % 2))
                    elif m in (20, 21):
                        high(i, U_WIN + m + 2, 32, ks=1)
                    else:
                        high(i, U_WIN + m + 2)
                    diff_mid(i, m)
                    if m == 3:
                        act.wait_ge(lam_step, 3 * i + 2)
                        act.activation(lam_e[:, :], lam_s[:, :], ACT.Exp).then_inc(lam_exp, 1)
                    if m == 20:
                        act.wait_ge(kept_act, 16 * i + 16)
                        for g in range(2):
                            for t in range(TT):
                                act.activation(gates[:, g, t, :], gates[:, g, t, :], ACT.Sigmoid
                                               ).then_inc(gate_sig, 1)
                    keep(i, m)
                    stick_weights(i, m)
                    stick_softplus(i, m)
                    diff_after(i, m)
                    if m in (2, 4):
                        k = (m - 2) // 2
                        act.wait_ge(qk_turned, 4 * i + k + 1)
                        act.activation((sbq_t, sbk_t)[k][:, :, :].rearrange("p k n -> p (k n)"), pair(QK_PAIR),
                                       ACT.Copy).then_inc(sb_turned, 1)
                    if m == 16:
                        act.wait_ge(os_turned, i + 1)
                        act.activation(os_hi[:, :, :].rearrange("p k n -> p (k n)"), pair(OS_PAIR),
                                       ACT.Copy).then_inc(os_high, 1)
                    if m == 20:
                        act.wait_ge(od_turned, i + 1)
                        act.activation(x_hi[:, 0:4, :].rearrange("p k n -> p (k n)"), pair(OD_PAIR),
                                       ACT.Copy).then_inc(od_high, 1)
                high(i, U_WIN + 25, halves=(0,))
                high_inputs(i, 2, 0)
                high(i, U_WIN + 25, halves=(1,))
                high_inputs(i, 2, 1)
                high(i, U_WIN + 26)
                high(i, U_WIN + 27)
                high(i, U_FFN2, 16)

            def load_post(i, name, n, s):
                act.wait_ge(h_ready, 16 * i + 4 * n + 4)
                act.dma_start(post_g[:, s, :],
                              a[name][bass.ds(i, 1), :].rearrange("o n -> (o n)").partition_broadcast(P)
                              ).then_inc(post_in[s], 16)

            act.wait_ge(layer_g, 1)
            high_inputs(0, 0, 0, (0,))
            load_x(2)
            load_x(3)
            high(0, 0, 0)
            high_inputs(0, 0, 0, (1,))
            high(0, 1, 4)
            square_pre(0, 0, 0)
            high(0, 2, 0)
            act.wait_ge(angles, 1)
            act.activation(rope_s[:, :, 32:64], ang[:, :, :], ACT.Sin)
            act.activation(rope_c[:, :, 0:32], cos_in[:, :, :], ACT.Sin).then_inc(sines, 1)
            high_inputs(0, 0, 1)
            square_pre(0, 0, 1)
            with act.Fori(0, DEPTH) as i:
                def loads():
                    load_post(i, "ffn1_post_g", 0, 0)
                    load_post(i, "mix_post_g", 0, 1)
                    act.dma_start(lam_layer[:, :, :].rearrange("p f d -> p (f d)"),
                                  a["diff_lambda"][bass.ds(i, 1), :, :].rearrange("o f d -> (o f d)"
                                                                                  ).partition_broadcast(P)
                                  ).then_inc(lam_loaded, 16)
                    act.dma_start(p_nat[:, :, :], a["p"][bass.ds(i, 1), 0, :, :].rearrange(
                        "o (t p) n -> p (o t) n", p=P)).then_inc(p_in, 16)

                ffn(i, 0, U_FFN1, 0, lambda: high(i, U_WIN, 8), loads)
                boundary(i, 0, 1, DOWN_PAIR,
                         lambda n: high(i, U_WIN + 1, 12, halves=(n,)), lambda: high(i, U_WIN + 2, 8))

                load_post(i, "ffn2_post_g", 1, 0)
                act.preload_act_table_set("natural_log_exp_and_others")
                act.wait_ge(pre_scale, 8 * i + 4)
                mixer(i)
                boundary(i, 1, 3, OUT_PAIR,
                         lambda n: high(i, U_FFN2 + 1, 20, halves=(n,)), lambda: high(i, U_FFN2 + 2, 16))

                act.preload_act_table_set("silu_and_others")
                ffn(i, 1, U_FFN2, 16, lambda: high(i, U_PROJ), lambda: load_post(i, "ple_post_g", 2, 1))
                act.wait_ge(p_turned, i + 1)
                act.activation(p_hi[:, :, :], bank(P_BANK).rearrange("p (k n) -> p k n", k=2),
                               ACT.Copy).then_inc(p_high, 1)
                boundary(i, 2, 4, DOWN_PAIR,
                         lambda n: high(i, U_GATE, 24, ks=2, halves=(n,)), lambda: high(i, U_GATE + 1, 26, ks=2))
                high(i, U_GATE + 2, 28, ks=2)
                high(i, U_GATE + 3, 30, ks=2)

                def gate(t):
                    act.wait_ge(pre_scale, 8 * i + 7 + t)
                    wait_product(act, f_done, 4 * i + 4, i, F_UNIT[3], t)
                    act.activation(gates[:, 0, t, :], pair(GATE_PAIR[t]), ACT.Sigmoid,
                                   scale=r_pre[:, t:t + 1]).then_inc(ple_sig, 1)

                with act.If(i < DEPTH - 1):
                    act.wait_ge(layer_g, i + 2)
                    high(i + 1, 0, 0)
                act.preload_act_table_set("sigmoid_and_others")
                gate(0)
                square_post(i, 3, gates[:, 1, 0, :], 0)
                with act.If(i < DEPTH - 1):
                    high(i + 1, 1, 4)
                    high_inputs(i + 1, 0, 0)
                gate(1)
                with act.If(i < DEPTH - 1):
                    square_pre(i + 1, 0, 0)
                square_post(i, 3, gates[:, 1, 1, :], 1)
                act.preload_act_table_set("silu_and_others")
                with act.If(i < DEPTH - 1):
                    high(i + 1, 2, 0)
                    high_inputs(i + 1, 0, 1)
                    square_pre(i + 1, 0, 1)

        @block.vector
        def _(dve):
            dve.memset(freq[:, 0:1], 1.0).then_inc(split_done, SLOTS)
            dve.memset(freq[:, 1:2], float(np.float32(THETA ** (-1 / 32)))).then_inc(h_ready, 4)
            for j in range(2, 32):
                last = dve.memset(freq[:, j:j + 1], float(np.float32(THETA ** (-j / 32))))

            linked = [0]

            def link(ins):
                linked[0] += 1
                ins.then_inc(setup_step, 1)
                dve.wait_ge(setup_step, linked[0])

            link(last)
            dve.wait_ge(cols_turned, 1)
            dve.tensor_copy(g_cols[:, :, 0:DEPTH * KD], bank(0)[:, 0:64].rearrange("p (n k) -> p n k", n=4))
            for n in range(DEPTH):
                dve.memset(neg_inits[:, n:n + 1], -LAM_INIT[n])
                last = dve.tensor_scalar(g_sub[:, n:n + 1], bank(0)[:, 64 + n:65 + n], 1.0 - LAM_INIT[n],
                                         None, ALU.mult)
            last.then_inc(cols_kept, 1)
            dve.wait_ge(cols_kept, 1)

            def start_layer(i):
                dve.tensor_copy(neg_init[:, :], neg_inits[:, bass.ds(i, 1)])
                dve.tensor_copy(g_layer[:, 32:33], g_sub[:, bass.ds(i, 1)])
                dve.tensor_copy(g_layer[:, 0:32].rearrange("p (n k) -> p n k", n=4),
                                g_cols[:, :, bass.ds(i * KD, KD)]).then_inc(layer_g, 1)

            start_layer(0)

            def low(i, u, gain=None, ks=4, c=0, halves=(0, 1)):
                s = slot(u)
                whi = w_hi[:, s, :].bitcast(F32)
                for half in halves:
                    dve.wait_ge(hi_ready, 2 * UNITS * i + 6 * c + 2 * u + half + 1)
                    pieces = 2 if ks == 4 and gain is not None else 1
                    n = UNIT // 2 // pieces
                    for k in range(pieces * half, pieces * half + pieces):
                        part = slice(k * n, (k + 1) * n)
                        if gain is None:
                            last = dve.tensor_tensor(w_lo[:, s, part], raw[:, s, part], whi[:, part], ALU.subtract)
                        else:
                            g = gain + (k if ks > 1 else 0)
                            last = dve.scalar_tensor_tensor(out=w_lo[:, s, part], in0=raw[:, s, part],
                                                            scalar=g_layer[:, g:g + 1], in1=whi[:, part],
                                                            op0=ALU.mult, op1=ALU.subtract)
                    if half:
                        last.then_inc(split_done, 1)

            def low_inputs(i, q, t, halves=(0, 1)):
                for n in halves:
                    idx = 2 * t + n
                    dve.wait_ge(x_high, 20 * i + 4 * q + idx + 1)
                    part = (slice(None), slice(4 * n, 4 * n + 4), slice(t * P, (t + 1) * P))
                    dve.tensor_tensor(x_lo[part], bank(X_BANK[q][idx]).rearrange("p (k n) -> p k n", k=4),
                                      x_hi[part].bitcast(F32), ALU.subtract).then_inc(x_split, 1)

            def low_ht(i, f, c):
                dve.wait_ge(ht_high, 2 * HTS * i + HTS * f + c + 1)
                dve.tensor_tensor(ht_lo[:, :, :], bank(HT_BANK).rearrange("p (k n) -> p k n", k=2),
                                  ht_hi[:, :, :].bitcast(F32), ALU.subtract).then_inc(ht_split, 1)

            def low_last_ht(i, f, t):
                toks = slice(t * P, (t + 1) * P)
                dve.wait_ge(ht_high, 2 * HTS * i + HTS * f + NC + t)
                dve.tensor_tensor(x_lo[:, 0:2, toks], bank(HT_BANK).rearrange("p (k n) -> p k n", k=2)[:, :, toks],
                                  x_hi[:, 0:2, toks].bitcast(F32), ALU.subtract).then_inc(ht_split, 1)

            def product(i, f, c, t):
                dve.wait_ge(silu_done, 4 * NC * i + 2 * NC * f + 2 * c + t + 1)
                dve.scalar_tensor_tensor(out=glu[:, t, 1, :], in0=bank(GU_BANK[t])[:, FC:2 * FC],
                                         scalar=r_pre[:, t:t + 1], in1=glu[:, t, 0, :],
                                         op0=ALU.mult, op1=ALU.mult).then_inc(prod_done, 1)

            def ffn(i, f, u0, g0, next_unit):
                product(i, f, 0, 0)
                low(i, u0 + 3, g0 + 4, halves=(0,))
                product(i, f, 0, 1)
                low(i, u0 + 3, g0 + 4, halves=(1,))
                with dve.Fori(1, NC - 1) as c:
                    low(i, u0 + 1, c=c)
                    low_ht(i, f, c - 1)
                    low(i, u0 + 2, g0, c=c)
                    for t in range(TT):
                        product(i, f, c, t)
                    low(i, u0 + 3, g0 + 4, c=c)
                low(i, u0 + 3 * NC - 2)
                low_ht(i, f, NC - 2)
                low(i, u0 + 3 * NC - 1)
                for t in range(TT):
                    product(i, f, NC - 1, t)
                low_last_ht(i, f, 0)
                next_unit()
                low_last_ht(i, f, 1)

            HALVES = [slice(0, W), slice(W, D)]

            def gained(i, n, src, t, k):
                dve.tensor_tensor(tmp[:, t, HALVES[k]], src[:, HALVES[k]], post_g[:, n % 2, HALVES[k]],
                                  ALU.mult).then_inc(scaled, 1)

            def wait_gained(i, n, t):
                dve.wait_ge(post_in[n % 2], 32 * i + 16 * (n // 2) + 16)
                if n < 3:
                    dve.wait_ge(squared_post, 8 * i + 2 * n + t + 1)
                else:
                    dve.wait_ge(ple_e, 2 * i + t + 1)

            def update_h(i, n, t, k):
                if k == 0:
                    dve.wait_ge(post_scale, 8 * i + 2 * n + t + 1)
                dve.wait_ge(scaled, 16 * i + 4 * n + 2 * t + k + 1)
                dve.scalar_tensor_tensor(out=h[:, t, HALVES[k]], in0=tmp[:, t, HALVES[k]],
                                         scalar=r_post[:, t:t + 1], in1=h[:, t, HALVES[k]],
                                         op0=ALU.mult, op1=ALU.add).then_inc(h_ready, 1)

            def boundary(i, n, q, pairs, next_unit, unit_after):
                wait_gained(i, n, 0)
                for k in range(2):
                    gained(i, n, pair(pairs[0]), 0, k)
                    update_h(i, n, 0, k)
                next_unit(0)
                low_inputs(i, q, 0)
                next_unit(1)
                wait_gained(i, n, 1)
                for k in range(2):
                    gained(i, n, pair(pairs[1]), 1, k)
                    update_h(i, n, 1, k)
                if q == 4:
                    unit_after()
                    low_inputs(i, q, 1)
                else:
                    low_inputs(i, q, 1, (0,))
                    unit_after()
                    low_inputs(i, q, 1, (1,))

            def merge(i, t):
                wait_product(dve, y_df_done, i + 1, i, U_BDF + 1, t)
                for n in range(2):
                    s = slice(n * W, (n + 1) * W)
                    dve.tensor_tensor(gates[:, 1, t, s], bank(Y_DF_PAIR[t] + n), gates[:, 1, t, s],
                                      ALU.mult).then_inc(gated_df, 1)
                for n in range(2):
                    s = slice(n * W, (n + 1) * W)
                    dve.wait_ge(gated_sb, 2 * i + t + 1)
                    dve.wait_ge(gated_df, 4 * i + 2 * t + n + 1)
                    dve.tensor_tensor(gates[:, 0, t, s], gates[:, 0, t, s], gates[:, 1, t, s],
                                      ALU.add).then_inc(merged, 1)

            def mixer(i):
                for m in range(23):
                    hd = m - SB_P0
                    if 0 <= hd < SB_HEADS:
                        dve.wait_ge(s_value, SB_HEADS * i + hd + 1)
                        dve.tensor_copy(o_sb[:, :, hd * SB_D:(hd + 1) * SB_D],
                                        bank(SB_BANK[hd % 2])[:, SB_OUT:W].rearrange("p (t n) -> p t n", t=TT)
                                        ).then_inc(s_kept, 1)
                    if m >= DF_P0 and (m - DF_P0) % 2 == 0 and (m - DF_P0) // 2 < DF_HEADS:
                        hd = (m - DF_P0) // 2
                        dve.wait_ge(d_scale, DF_HEADS * i + hd + 1)
                        for t in range(TT):
                            last = dve.tensor_scalar(o_df[:, t, hd * DF_V:(hd + 1) * DF_V],
                                                     bank(DF_BANK[1])[:, t * P:(t + 1) * P], r_sub[:, t:t + 1],
                                                     None, ALU.mult)
                        last.then_inc(d_normed, 1)
                    if m == 0:
                        pass
                    elif m < 18:
                        low(i, U_WIN + m + 2, 8 + 4 * (m % 2))
                    elif m in (20, 21):
                        low(i, U_WIN + m + 2, 32, ks=1)
                    else:
                        low(i, U_WIN + m + 2)
                    if m == 1:
                        dve.wait_ge(lam_loaded, 16 * i + 16)
                        dve.tensor_tensor(lam_pr[:, :, :], lam_layer[:, 0::2, :], lam_layer[:, 1::2, :], ALU.mult
                                          ).then_inc(lam_step, 1)
                        dve.wait_ge(lam_step, 3 * i + 1)
                        dve.tensor_reduce(lam_s[:, :], lam_pr[:, :, :], AX_X, ALU.add).then_inc(lam_step, 1)
                    if m == 4:
                        dve.wait_ge(lam_exp, i + 1)
                        dve.tensor_tensor(neg_lam[:, :], lam_e[:, 1:2], lam_e[:, 0:1], ALU.subtract
                                          ).then_inc(lam_step, 1)
                        dve.wait_ge(lam_step, 3 * i + 3)
                        dve.tensor_tensor(neg_lam[:, :], neg_lam[:, :], neg_init[:, :], ALU.add
                                          ).then_inc(lam_known, 1)
                    if m in (5, 11):
                        j = m // 2
                        for t in range(TT):
                            wait_product(dve, win_done, 10 * i + j + 1, i, U_WIN + m, t)
                            dve.tensor_scalar((v_sb, v_df)[j == DFV][:, t, :], bank(WIN_BANK[j % 2][t]),
                                              r_pre[:, t:t + 1], None, ALU.mult).then_inc(kept_dve, 1)
                    diff = m >= DF_Z0 and (m - DF_Z0) % 2 == 0 and (m - DF_Z0) // 2 < DF_HEADS
                    if diff:
                        hd = (m - DF_Z0) // 2
                        dve.wait_ge(d_score, DF_HEADS * i + hd + 1)
                        for c in range(2):
                            for t, (lo, hi) in enumerate(((0, P), (P, 384))):
                                last = dve.tensor_reduce(neg_max[:, 2 * c + t:2 * c + t + 1],
                                                         bank(DF_BANK[c])[:, lo:hi], AX_X, ALU.max, negate=True)
                        last.then_inc(d_max, 1)
                    if m in (9, 11):
                        k = (m - 9) // 2
                        dve.wait_ge(qk_turned, 4 * i + 2 + k + 1)
                        dve.tensor_copy((dfq_t, dfk_t)[k][:, :, :].rearrange("p k n -> p (k n)"),
                                        pair(QK_PAIR)).then_inc(df_turned, 1)
                    hd = m - SB_Z0
                    if 0 <= hd < SB_HEADS:
                        dve.wait_ge(s_log, SB_HEADS * i + hd + 1)
                        b = hd % 2
                        n = 3 * (SB_HEADS * i + hd)
                        dve.scalar_tensor_tensor(out=soft[:, b, :], in0=bank(SB_BANK[b])[:, 0:384], scalar=0.0,
                                                 in1=soft[:, b, :], op0=ALU.max, op1=ALU.add).then_inc(s_soft, 1)
                        dve.wait_ge(s_soft, n + 1)
                        dve.tensor_copy(sp_hi[:, b, :], soft[:, b, :]).then_inc(s_soft, 1)
                        dve.wait_ge(s_soft, n + 2)
                        dve.tensor_tensor(sp_lo[:, b, :], soft[:, b, :], sp_hi[:, b, :].bitcast(F32),
                                          ALU.subtract).then_inc(s_soft, 1)
                    if diff:
                        hd = (m - DF_Z0) // 2
                        n = DF_HEADS * i + hd + 1
                        dve.wait_ge(d_exp, n)
                        dve.reciprocal(p_rec[:, :], p_sum[:, :]).then_inc(d_rec, 1)
                        dve.wait_ge(d_rec, n)
                        dve.wait_ge(lam_known, i + 1)
                        dve.tensor_scalar(neg_lr[:, :], p_rec[:, 2:4], neg_lam[:, 0:1], None, ALU.mult
                                          ).then_inc(d_lam, 1)
                        dve.wait_ge(d_lam, n)
                        for t, (lo, hi) in enumerate(((0, P), (P, 384))):
                            last = dve.tensor_scalar(prob[:, 1, lo:hi], prob[:, 1, lo:hi], neg_lr[:, t:t + 1],
                                                     None, ALU.mult)
                        last.then_inc(d_part, 1)
                        dve.wait_ge(d_part, n)
                        for t, (lo, hi) in enumerate(((0, P), (P, 384))):
                            last = dve.scalar_tensor_tensor(out=mixed[:, lo:hi], in0=prob[:, 0, lo:hi],
                                                            scalar=p_rec[:, t:t + 1], in1=prob[:, 1, lo:hi],
                                                            op0=ALU.mult, op1=ALU.add)
                        last.then_inc(d_mixed, 1)
                    if m == 16:
                        dve.wait_ge(os_high, i + 1)
                        dve.tensor_tensor(os_lo[:, :, :].rearrange("p k n -> p (k n)"), pair(OS_PAIR),
                                          os_hi[:, :, :].rearrange("p k n -> p (k n)").bitcast(F32),
                                          ALU.subtract).then_inc(os_split, 1)
                    if m == 20:
                        dve.wait_ge(od_high, i + 1)
                        dve.tensor_tensor(x_lo[:, 0:4, :].rearrange("p k n -> p (k n)"), pair(OD_PAIR),
                                          x_hi[:, 0:4, :].rearrange("p k n -> p (k n)").bitcast(F32),
                                          ALU.subtract).then_inc(od_split, 1)
                    if m == 21:
                        for t in range(TT):
                            dve.wait_ge(gate_sig, 4 * i + 4)
                            wait_product(dve, y_sb_done, i + 1, i, U_BSB + 1, t)
                            dve.tensor_tensor(gates[:, 0, t, :], pair(Y_SB_PAIR[t]), gates[:, 0, t, :],
                                              ALU.mult).then_inc(gated_sb, 1)
                merge(i, 0)
                low(i, U_WIN + 25, halves=(0,))
                low_inputs(i, 2, 0)
                low(i, U_WIN + 25, halves=(1,))
                merge(i, 1)
                low_inputs(i, 2, 1)
                low(i, U_WIN + 26)
                low(i, U_WIN + 27)
                low(i, U_FFN2, 16)

            low_inputs(0, 0, 0, (0,))
            low(0, 0, 0)
            low_inputs(0, 0, 0, (1,))
            low(0, 1, 4)
            dve.wait_ge(pos_in, 16 * TT)
            link(dve.tensor_copy(pos_f[:, :], pos_i[:, :]))
            for t in range(TT):
                last = dve.tensor_scalar(ang[:, t, :], freq[:, :], pos_f[:, t:t + 1], None, ALU.mult)
            link(last)
            link(dve.tensor_scalar(turns[:, :, :], ang[:, :, :], 1 / (2 * math.pi), ROUND, ALU.mult, ALU.add))
            link(dve.tensor_scalar(turns[:, :, :], turns[:, :, :], -ROUND, None, ALU.add))
            for part in TWO_PI:
                link(dve.scalar_tensor_tensor(out=ang[:, :, :], in0=turns[:, :, :], scalar=-part, in1=ang[:, :, :],
                                              op0=ALU.mult, op1=ALU.add))
            link(dve.tensor_scalar(ang[:, :, :], ang[:, :, :], PI_IN, -PI_IN, ALU.min, ALU.max))
            link(dve.scalar_tensor_tensor(out=cos_in[:, :, :], in0=ang[:, :, :], scalar=-1.0, in1=ang[:, :, :],
                                          op0=ALU.mult, op1=ALU.min))
            dve.tensor_scalar(cos_in[:, :, :], cos_in[:, :, :], math.pi / 2, None, ALU.add).then_inc(angles, 1)
            dve.wait_ge(sines, 1)
            dve.tensor_scalar(rope_s[:, :, 0:32], rope_s[:, :, 32:64], -1.0, None, ALU.mult)
            dve.tensor_copy(rope_c[:, :, 32:64], rope_c[:, :, 0:32]).then_inc(rope_ready, 1)
            low_inputs(0, 0, 1, (0,))
            low(0, 2, 0)
            low_inputs(0, 0, 1, (1,))
            with dve.Fori(0, DEPTH) as i:
                ffn(i, 0, U_FFN1, 0, lambda: low(i, U_WIN, 8))
                boundary(i, 0, 1, DOWN_PAIR, lambda n: low(i, U_WIN + 1, 12, halves=(n,)),
                         lambda: low(i, U_WIN + 2, 8))
                mixer(i)
                boundary(i, 1, 3, OUT_PAIR, lambda n: low(i, U_FFN2 + 1, 20, halves=(n,)),
                         lambda: low(i, U_FFN2 + 2, 16))
                ffn(i, 1, U_FFN2, 16, lambda: low(i, U_PROJ))
                dve.wait_ge(p_high, i + 1)
                dve.tensor_tensor(p_lo[:, :, :], bank(P_BANK).rearrange("p (k n) -> p k n", k=2),
                                  p_hi[:, :, :].bitcast(F32), ALU.subtract).then_inc(p_split, 1)
                boundary(i, 2, 4, DOWN_PAIR, lambda n: low(i, U_GATE, 24, ks=2, halves=(n,)),
                         lambda: low(i, U_GATE + 1, 26, ks=2))
                low(i, U_GATE + 2, 28, ks=2)
                low(i, U_GATE + 3, 30, ks=2)

                def embed(t):
                    dve.wait_ge(ple_sig, 2 * i + t + 1)
                    wait_product(dve, e_done, i + 1, i, U_PROJ, t)
                    dve.tensor_tensor(gates[:, 1, t, :], pair(E_PAIR[t]), gates[:, 0, t, :], ALU.mult
                                      ).then_inc(ple_e, 1)

                def embedded(t):
                    wait_gained(i, 3, t)
                    for k in range(2):
                        gained(i, 3, gates[:, 1, t, :], t, k)
                    for k in range(2):
                        update_h(i, 3, t, k)

                with dve.If(i < DEPTH - 1):
                    dve.wait_ge(split_done, UNITS * (i + 1) + SLOTS)
                    start_layer(i + 1)
                    dve.wait_ge(layer_g, i + 2)
                    low(i + 1, 0, 0)
                embed(0)
                embedded(0)
                with dve.If(i < DEPTH - 1):
                    low(i + 1, 1, 4, halves=(0,))
                    low_inputs(i + 1, 0, 0)
                embed(1)
                with dve.If(i < DEPTH - 1):
                    low(i + 1, 1, 4, halves=(1,))
                embedded(1)
                with dve.If(i < DEPTH - 1):
                    low_inputs(i + 1, 0, 1, (0,))
                    low(i + 1, 2, 0)
                    low_inputs(i + 1, 0, 1, (1,))

        @block.tensor
        def _(pe):
            pe.wait_ge(const_id, 1)
            pe.wait_ge(g_in, 16 * 3)
            pe.wait_ge(last_g_in, 16 * 2)
            pe.transpose(bank(0)[:, 0:66], g_rows[0:66, :], ident[0:66, 0:66]).then_inc(cols_turned, 1)
            pe.transpose(bank(1)[:, 0:66], g_rows[0:66, :], ident[0:66, 0:66]).then_inc(units_used, SLOTS)

            def exact(dst, x_h, x_l, w_h, w_l, first, last):
                pe.matmul(dst, x_h, w_h, start=first, stop=False)
                pe.matmul(dst, x_h, w_l, start=False, stop=False)
                return pe.matmul(dst, x_l, w_h, start=False, stop=last)

            def wide(s, dst, xh, xl, k0, t, first, last, before=None):
                for k in range(4):
                    if before and k in before:
                        before[k]()
                    cols, toks = slice(k * W, (k + 1) * W), slice(t * P, (t + 1) * P)
                    mm = exact(dst, xh[:, k0 + k, toks], xl[:, k0 + k, toks], w_hi[:, s, cols], w_lo[:, s, cols],
                               first and k == 0, last and k == 3)
                return mm

            def deep(s, b, xh, xl, k0, t, first, last, before=None):
                toks = slice(t * P, (t + 1) * P)
                for n in range(2):
                    for k in range(2):
                        if before and 2 * n + k in before:
                            before[2 * n + k]()
                        cols = slice(k * D + n * W, k * D + (n + 1) * W)
                        mm = exact(bank(b + n), xh[:, k0 + k, toks], xl[:, k0 + k, toks],
                                   w_hi[:, s, cols], w_lo[:, s, cols], first and k == 0, last and k == 1)
                return mm

            def begin(i, u, c=0):
                pe.wait_ge(split_done, UNITS * i + 3 * c + u + 1 + SLOTS)

            def turn(i, q, idx):
                t, n = idx // 2, idx % 2
                if q == 2:
                    pe.wait_ge(merged, 4 * i + idx + 1)
                    src = gates[:, 0, t, :]
                else:
                    pe.wait_ge(h_ready, 16 * i + 4 * (q - (q > 2)) + idx + 1)
                    src = h[:, t, :]
                if q == 0:
                    pe.wait_ge(h_loaded[idx], 16)
                for k in range(4):
                    mm = pe.transpose(bank(X_BANK[q][idx])[:, k * P:(k + 1) * P],
                                      src[:, (4 * n + k) * P:(4 * n + k + 1) * P], ident[:, :])
                mm.then_inc(x_turned, 1)

            def turned_at(i, q, idxs, at):
                return {k: (lambda idx=idx: turn(i, q, idx)) for idx, k in zip(idxs, at)}

            def inputs(i, q, t, n):
                pe.wait_ge(x_split, 20 * i + 4 * q + 2 * t + n + 1)

            def by_tiles(i, u, product, done=None, before=None):
                for t in range(TT):
                    for s in range(2):
                        if t == 0:
                            begin(i, u + s)
                        mm = product(s, t, (before or {}).get((s, t)))
                        if t == 1:
                            mm.then_inc(units_used, 1)
                        elif s == 1 and done is not None:
                            mm.then_inc(done, 1)

            def turn_ht(i, f, c):
                pe.wait_ge(prod_done, 4 * NC * i + 2 * NC * f + 2 * c + 2)
                for k in range(2):
                    for t in range(TT):
                        mm = pe.transpose(bank(HT_BANK)[:, k * SEQ + t * P:k * SEQ + (t + 1) * P],
                                          glu[:, t, 1, k * P:(k + 1) * P], ident[:, :])
                mm.then_inc(ht_turned, 1)

            def turn_last_ht(i, f, t):
                pe.wait_ge(prod_done, 4 * NC * i + 2 * NC * f + 2 * (NC - 1) + t + 1)
                if t == 0:
                    pe.wait_ge(ht_split, 2 * HTS * i + HTS * f + NC - 1)
                for k in range(2):
                    mm = pe.transpose(bank(HT_BANK)[:, k * SEQ + t * P:k * SEQ + (t + 1) * P],
                                      glu[:, t, 1, k * P:(k + 1) * P], ident[:, :])
                mm.then_inc(ht_turned, 1)

            def ffn(i, f, q, u0, before_last):
                def gate_up(u, half, step, c=0):
                    begin(i, u, c)
                    for t in range(TT):
                        if half == 0:
                            pe.wait_ge(prod_done, 4 * NC * i + 2 * NC * f + 2 * step + t - 1)
                        mm = wide(slot(u), bank(GU_BANK[t]), x_hi, x_lo, 4 * half, t, half == 0, half == 1)
                        if half == 1 and t == 0:
                            mm.then_inc(gu_done, 1)
                    mm.then_inc(units_used, 1)

                def down(u, step, first=False, c=0):
                    begin(i, u, c)
                    pe.wait_ge(ht_split, 2 * HTS * i + HTS * f + step + 1)
                    for t in range(TT):
                        mm = deep(slot(u), DOWN_PAIR[t], ht_hi, ht_lo, 0, t, first, False)
                    mm.then_inc(units_used, 1)

                def step(c, at, first=False):
                    gate_up(u0 - 1, 0, c, at)
                    turn_ht(i, f, c - 1)
                    gate_up(u0, 1, c, at)
                    down(u0 + 1, c - 1, first=first, c=at)

                def first_gate_up(s, t, before):
                    inputs(i, q, t, s)
                    return wide(slot(u0 + s), bank(GU_BANK[t]), x_hi, x_lo, 4 * s, t, s == 0, s == 1, before)

                def last_down(s, t, before):
                    if s == 0:
                        pe.wait_ge(ht_split, 2 * HTS * i + HTS * f + NC - 1)
                    else:
                        pe.wait_ge(ht_split, 2 * HTS * i + HTS * f + NC + t)
                    xh, xl = (x_hi, x_lo) if s else (ht_hi, ht_lo)
                    return deep(slot(u0 + 3 * NC - 2 + s), DOWN_PAIR[t], xh, xl, 0, t, False, s == 1, before)

                by_tiles(i, u0, first_gate_up, gu_done, {(1, 0): turned_at(i, q, (2,), (3 if q == 0 else 2,)),
                                                         (0, 1): turned_at(i, q, (3,), (1,))})
                step(1, 1, first=True)
                with pe.Fori(2, NC - 1) as c:
                    step(c, c)
                gate_up(u0 + 3 * NC - 4, 0, NC - 1)
                turn_ht(i, f, NC - 2)
                gate_up(u0 + 3 * NC - 3, 1, NC - 1)
                before_last()
                by_tiles(i, u0 + 3 * NC - 2, last_down, f_done, {
                    (0, 0): {2: lambda: turn_last_ht(i, f, 0)}, (1, 0): {2: lambda: turn_last_ht(i, f, 1)},
                    (1, 1): turned_at(i, NEXT_INPUT[q], (0, 1), (1, 2))})

            def turn_four(dst, src):
                for k in range(4):
                    for t in range(TT):
                        mm = pe.transpose(dst[:, k * SEQ + t * P:k * SEQ + (t + 1) * P],
                                          src[:, t, k * P:(k + 1) * P], ident[:, :])
                return mm

            def stick_scores(i, hd):
                pe.wait_ge(sb_turned, 2 * i + 2)
                if hd >= 2:
                    pe.wait_ge(s_kept, SB_HEADS * i + hd - 1)
                dst, rows, k = bank(SB_BANK[hd % 2]), slice(64 * (hd % 2), 64 * (hd % 2) + 64), hd // 2
                pe.matmul(dst[:, 0:384], ident_b[:, :], mask_sb[:, :], start=True, stop=False, skip_group_check=True)
                pe.matmul(dst[:, 0:SEQ], sbk_t[rows, k, 0:P], sbq_t[rows, k, :], start=False, stop=False,
                          skip_group_check=True)
                pe.matmul(dst[:, SEQ:384], sbk_t[rows, k, P:SEQ], sbq_t[rows, k, P:SEQ], start=False, stop=True,
                          skip_group_check=True).then_inc(s_score, 1)

            def stick_later(i, hd):
                pe.wait_ge(s_soft, 3 * (SB_HEADS * i + hd + 1))
                dst = bank(SB_BANK[hd % 2])
                for part in range(2):
                    s = (sp_hi, sp_lo)[part][:, hd % 2, :]
                    pe.matmul(dst[:, 0:384], neg_tri[:, :], s, start=False, stop=False, skip_group_check=True)
                    mm = pe.matmul(dst[:, P:SEQ], neg_one[:, :], s[:, SEQ:384], start=False, stop=part == 1,
                                   skip_group_check=True)
                mm.then_inc(s_later, 1)

            def stick_values(i, hd):
                pe.wait_ge(s_weight, SB_HEADS * i + hd + 1)
                pe.wait_ge(kept_dve, 4 * i + 2)
                dst, w, c = bank(SB_BANK[hd % 2]), w_att[:, hd % 2, :], slice(hd * SB_D, (hd + 1) * SB_D)
                pe.matmul(dst[:, SB_OUT:SB_OUT + 64], w[:, 0:P], v_sb[:, 0, c], start=True, stop=True,
                          skip_group_check=True)
                pe.matmul(dst[:, SB_OUT + 64:W], w[:, P:SEQ], v_sb[:, 0, c], start=True, stop=False,
                          skip_group_check=True)
                pe.matmul(dst[:, SB_OUT + 64:W], w[:, SEQ:384], v_sb[:, 1, c], start=False, stop=True,
                          skip_group_check=True).then_inc(s_value, 1)

            def diff_scores(i, hd):
                pe.wait_ge(df_turned, 2 * i + 2)
                if hd:
                    pe.wait_ge(d_kept, DF_HEADS * i + hd)
                    pe.wait_ge(d_normed, DF_HEADS * i + hd)
                for c in range(2):
                    dst, rows = bank(DF_BANK[c]), slice(64 * c, 64 * c + 64)
                    pe.matmul(dst[:, 0:384], ident_b[:, :], mask_df[:, :], start=True, stop=False,
                              skip_group_check=True)
                    pe.matmul(dst[:, 0:P], dfq_t[rows, hd, 0:P], dfk_t[rows, hd, 0:P], start=False, stop=False,
                              skip_group_check=True)
                    mm = pe.matmul(dst[:, P:384], dfq_t[rows, hd, P:SEQ], dfk_t[rows, hd, :], start=False, stop=True,
                                   skip_group_check=True)
                mm.then_inc(d_score, 1)

            def diff_turn(i, hd):
                pe.wait_ge(d_mixed, DF_HEADS * i + hd + 1)
                for k in range(3):
                    mm = pe.transpose(bank(DF_BANK[0])[:, k * P:(k + 1) * P], mixed[:, k * P:(k + 1) * P],
                                      ident[:, :])
                mm.then_inc(d_turned, 1)

            def diff_values(i, hd):
                pe.wait_ge(d_kept, DF_HEADS * i + hd + 1)
                pe.wait_ge(kept_dve, 4 * i + 4)
                dst, c = bank(DF_BANK[1]), slice(hd * DF_V, (hd + 1) * DF_V)
                pe.matmul(dst[:, 0:P], mixed_t[:, 0:P], v_df[:, 0, c], start=True, stop=True, skip_group_check=True)
                pe.matmul(dst[:, P:SEQ], mixed_t[:, P:SEQ], v_df[:, 0, c], start=True, stop=False,
                          skip_group_check=True)
                pe.matmul(dst[:, P:SEQ], mixed_t[:, SEQ:384], v_df[:, 1, c], start=False, stop=True,
                          skip_group_check=True).then_inc(d_value, 1)

            def middle(i, m):
                if 0 <= m - SB_P0 < SB_HEADS:
                    stick_values(i, m - SB_P0)
                if 0 <= m - DF_P0 < 2 * DF_HEADS and (m - DF_P0) % 2 == 0:
                    diff_values(i, (m - DF_P0) // 2)

            def behind(i, m):
                if m == 2:
                    pe.wait_ge(kept_act, 16 * i + 2)
                    turn_four(pair(QK_PAIR), slab).then_inc(qk_turned, 1)
                if m == 4:
                    pe.wait_ge(kept_act, 16 * i + 4)
                    pe.wait_ge(sb_turned, 2 * i + 1)
                    turn_four(pair(QK_PAIR), slab).then_inc(qk_turned, 1)
                if m == 9:
                    pe.wait_ge(roped, 4 * i + 2)
                    pe.wait_ge(sb_turned, 2 * i + 2)
                    turn_four(pair(QK_PAIR), slab).then_inc(qk_turned, 1)
                if m == 11:
                    pe.wait_ge(roped, 4 * i + 4)
                    pe.wait_ge(df_turned, 2 * i + 1)
                    turn_four(pair(QK_PAIR), slab).then_inc(qk_turned, 1)
                if 0 <= m - SB_C0 < SB_HEADS:
                    stick_later(i, m - SB_C0)
                if 0 <= m - SB_Z0 < SB_HEADS:
                    stick_scores(i, m - SB_Z0)
                if 0 <= m - DF_Z0 < 2 * DF_HEADS and (m - DF_Z0) % 2 == 0:
                    diff_scores(i, (m - DF_Z0) // 2)
                if 0 <= m - DF_T0 < 2 * DF_HEADS and (m - DF_T0) % 2 == 0:
                    diff_turn(i, (m - DF_T0) // 2)
                if m == 16:
                    pe.wait_ge(s_kept, SB_HEADS * (i + 1))
                    turn_four(pair(OS_PAIR), o_sb).then_inc(os_turned, 1)
                if m == 20:
                    pe.wait_ge(d_normed, DF_HEADS * (i + 1))
                    turn_four(pair(OD_PAIR), o_df).then_inc(od_turned, 1)

            def kept(i, j, t):
                if j in (SBV, DFV):
                    pe.wait_ge(kept_dve, 4 * i + 2 * (SBV, DFV).index(j) + t + 1)
                else:
                    pe.wait_ge(kept_act, 16 * i + 2 * BY_ACT.index(j) + t + 1)

            def mixer(i):
                def first_win(s, t, before):
                    inputs(i, 1, t, s)
                    return wide(slot(U_WIN + s), bank(WIN_BANK[0][t]), x_hi, x_lo, 4 * s, t, s == 0, s == 1, before)

                def last_df(s, t, before):
                    return deep(slot(U_BDF + s), Y_DF_PAIR[t], x_hi, x_lo, 2 * s, t, s == 0, s == 1, before)

                def w_out(u, s, t, before):
                    inputs(i, 2, t, u // 2)
                    return deep(slot(U_WOUT + u + s), OUT_PAIR[t], x_hi, x_lo, 2 * (u + s), t,
                                u + s == 0, u + s == 3, before)

                by_tiles(i, U_WIN, first_win, win_done, {(1, 0): turned_at(i, 1, (2,), (2,)),
                                                         (0, 1): turned_at(i, 1, (3,), (1,))})
                for m in range(2, 20):
                    j, half = m // 2, m % 2
                    begin(i, U_WIN + m)
                    for t in range(TT):
                        if half == 0 and j >= 2:
                            kept(i, j - 2, t)
                        mm = wide(slot(U_WIN + m), bank(WIN_BANK[j % 2][t]), x_hi, x_lo, 4 * half, t,
                                  half == 0, half == 1)
                        if half == 1 and t == 0:
                            mm.then_inc(win_done, 1)
                        if t == 0:
                            middle(i, m)
                    mm.then_inc(units_used, 1)
                    behind(i, m)
                for m in (20, 21):
                    half = m % 2
                    begin(i, U_WIN + m)
                    if half == 0:
                        pe.wait_ge(os_split, i + 1)
                    for t in range(TT):
                        if m == 20:
                            kept(i, 8 + t, 1)
                        mm = deep(slot(U_WIN + m), Y_SB_PAIR[t], os_hi, os_lo, 2 * half, t, half == 0, half == 1)
                        if half == 1 and t == 0:
                            mm.then_inc(y_sb_done, 1)
                        if t == 0:
                            middle(i, m)
                    mm.then_inc(units_used, 1)
                    behind(i, m)
                pe.wait_ge(od_split, i + 1)
                by_tiles(i, U_BDF, last_df, y_df_done, {(1, 1): turned_at(i, 2, (0, 1), (0, 1))})
                by_tiles(i, U_WOUT, lambda s, t, before: w_out(0, s, t, before), None,
                         {(1, 0): turned_at(i, 2, (2, 3), (2, 3))})
                by_tiles(i, U_WOUT + 2, lambda s, t, before: w_out(2, s, t, before), f_done,
                         {(1, 1): turned_at(i, 3, (0, 1), (1, 2))})

            NEXT_INPUT = {0: 1, 3: 4}

            def turn_p(i):
                pe.wait_ge(p_in, 16 * i + 16)
                for k in range(2):
                    for t in range(TT):
                        mm = pe.transpose(bank(P_BANK)[:, k * SEQ + t * P:k * SEQ + (t + 1) * P],
                                          p_nat[:, t, k * P:(k + 1) * P], ident[:, :])
                mm.then_inc(p_turned, 1)

            pe.wait_ge(cols_kept, 1)
            for idx in range(2):
                turn(0, 0, idx)
            for n in range(WARM_UP):
                pe.transpose(bank(7)[:, 0:P], ident[:, :], ident[:, :])
            with pe.Fori(0, DEPTH) as i:
                ffn(i, 0, 0, U_FFN1, lambda: None)
                pe.wait_ge(const_all, 1)
                mixer(i)
                ffn(i, 1, 3, U_FFN2, lambda: turn_p(i))
                begin(i, U_PROJ)
                pe.wait_ge(p_split, i + 1)
                for t in range(TT):
                    mm = deep(slot(U_PROJ), E_PAIR[t], p_hi, p_lo, 0, t, True, True)
                    if t == 0:
                        mm.then_inc(e_done, 1)
                mm.then_inc(units_used, 1)
                for idx in range(2, 4):
                    turn(i, 4, idx)

                def gate(u, s, t, before):
                    inputs(i, 4, t, 1)
                    return deep(slot(U_GATE + u + s), GATE_PAIR[t], x_hi, x_lo, 2 * (u + s), t,
                                u + s == 0, u + s == 3, before)

                by_tiles(i, U_GATE, lambda s, t, before: gate(0, s, t, before))
                by_tiles(i, U_GATE + 2, lambda s, t, before: gate(2, s, t, before), f_done)
                with pe.If(i < DEPTH - 1):
                    for idx in range(2):
                        turn(i + 1, 0, idx)


_NAMES = ["x", "p", "positions",
          "ffn1_pre_g", "ffn1_w_gu", "ffn1_w_down", "ffn1_post_g",
          "mix_pre_g", "w_in", "diff_lambda", "diff_subln_g", "w_branch_sb", "w_branch_diff", "w_out", "mix_post_g",
          "ffn2_pre_g", "ffn2_w_gu", "ffn2_w_down", "ffn2_post_g",
          "ple_pre_g", "w_ple_gate", "w_ple_proj", "ple_post_g"]


def kernel(**inputs):
    import concourse.bacc as bacc
    from concourse.bass_utils import run_bass_kernel_spmd

    nc = bacc.Bacc("TRN2", target_bir_lowering=False, num_devices=1)
    arrays, args = {}, {}
    for name in _NAMES:
        x = np.ascontiguousarray(inputs[name])
        arrays[f"in_{name}"] = x
        args[name] = nc.dram_tensor(f"in_{name}", x.shape, mybir.dt.from_np(x.dtype), kind="ExternalInput").ap()
    out = nc.dram_tensor("out_h", (1, SEQ, D), F32, kind="ExternalOutput").ap()
    trunk_kernel(nc, args, out)
    r = run_bass_kernel_spmd(nc, [arrays], core_ids=[0])
    return r.results[0]["out_h"]
```
